# Optimizing a Trainium2 kernel written in Bass

```python
import math
import jax, jax.numpy as jnp
from jax import lax
import numpy as np

D_MODEL = 1024
BATCH = 1
SEQ = 512
DEPTH = 2

CHUNK = 64
N_META = 16
D_FF = 2816
N_BRANCH = 3
BRANCH_W = 512
RW_HEADS = 8
RW_HEAD = 64
RW_LORA_W = 64
RW_LORA_A = 64
RW_LORA_G = 128
RW_COLS = 3 * BRANCH_W + RW_LORA_W + RW_LORA_A + RW_LORA_G
RW_GN_EPS = 64e-5
ML_HEADS = 4
ML_HEAD = 128
ML_CONV = 4
ML_CHUNK = 64
ML_COLS = 4 * BRANCH_W + 2 * ML_HEADS
DSA_HEADS = 8
DSA_HEAD = 64
DSA_LATENT = 128
IDX_HEADS = 8
IDX_HEAD = 64
TOPK_MAX = 256
QBLOCK = 128
DSA_COLS = BRANCH_W + DSA_LATENT + IDX_HEADS * IDX_HEAD + IDX_HEAD + IDX_HEADS
GATE_COLS = N_BRANCH * D_MODEL
N_IN = RW_COLS + ML_COLS + DSA_COLS + GATE_COLS
NORM_EPS = 1e-6

kernel_name = "hybrid_rwkv7_mlstm_dsa_macaron_encoder"

def _split(x, sizes):
    return jnp.split(x, np.cumsum(sizes)[:-1].tolist(), axis=-1)

def _chunk_ids(t_len):
    pos = jnp.arange(t_len)
    return jnp.where(pos < N_META, 0, 1 + (pos - N_META) // CHUNK)

def _rms_norm(x, g):
    xf = x.astype(jnp.float32)
    y = xf * lax.rsqrt(jnp.mean(xf * xf, axis=-1, keepdims=True) + NORM_EPS)
    return (y * g.astype(jnp.float32)).astype(x.dtype)

def _swiglu(x, w_in, w_out):
    gate, up = jnp.split(x @ w_in, 2, axis=-1)
    return (jax.nn.silu(gate) * up) @ w_out

def _causal_dwconv(x, w, b):
    k_w, c = w.shape
    y = lax.conv_general_dilated(x, w[:, None, :].astype(x.dtype), window_strides=(1,),
                                 padding=[(k_w - 1, 0)], dimension_numbers=("NWC", "WIO", "NWC"),
                                 feature_group_count=c)
    return y + b

def _rwkv7_scan(r, w, k, v, kh, a):
    b, _, h, n = r.shape

    def step(s, xs):
        r_t, w_t, k_t, v_t, kh_t, a_t = xs
        sk = jnp.einsum("bhvk,bhk->bhv", s, kh_t)
        s = (s * w_t[:, :, None, :] - sk[..., None] * (a_t * kh_t)[:, :, None, :]
             + v_t[..., None] * k_t[:, :, None, :])
        return s, jnp.einsum("bhvk,bhk->bhv", s, r_t)

    xs = tuple(jnp.moveaxis(t, 1, 0) for t in (r, w, k, v, kh, a))
    _, y = lax.scan(step, jnp.zeros((b, h, n, n), jnp.float32), xs)
    return jnp.moveaxis(y, 0, 1)

def _rwkv7_mixer(p, mu, w0, w_up, a0, a_up, g_up, k_k, k_a, r_k, gn_gain, gn_bias):
    bsz, t_len, _ = p.shape
    f32 = jnp.float32
    prev = jnp.pad(p, ((0, 0), (1, 0), (0, 0)))[:, :-1]
    p = p + (prev - p) * mu
    r, k, v, w_lo, a_lo, g_lo = _split(p, (BRANCH_W, BRANCH_W, BRANCH_W, RW_LORA_W, RW_LORA_A, RW_LORA_G))
    d = (w0 + jnp.tanh(w_lo) @ w_up).astype(f32)
    decay = jnp.exp(-math.exp(-0.5) * jax.nn.sigmoid(d))
    a = jax.nn.sigmoid(a0 + a_lo @ a_up)
    gate = jax.nn.sigmoid(g_lo) @ g_up

    def heads(t):
        return t.astype(f32).reshape(bsz, t_len, RW_HEADS, RW_HEAD)

    kappa = heads(k * k_k)
    kh = kappa / jnp.maximum(jnp.sqrt(jnp.sum(kappa * kappa, axis=-1, keepdims=True)), 1e-12)
    k = k * (1.0 + (a - 1.0) * k_a)
    r_h, k_h, v_h, a_h = heads(r), heads(k), heads(v), heads(a)
    w_h = decay.reshape(bsz, t_len, RW_HEADS, RW_HEAD)
    y = _rwkv7_scan(r_h, w_h, k_h, v_h, kh, a_h)
    mean = jnp.mean(y, axis=-1, keepdims=True)
    var = jnp.mean((y - mean) ** 2, axis=-1, keepdims=True)
    y = (y - mean) * lax.rsqrt(var + RW_GN_EPS)
    y = y * gn_gain.astype(f32).reshape(RW_HEADS, RW_HEAD) + gn_bias.astype(f32).reshape(RW_HEADS, RW_HEAD)
    y = y + jnp.sum(r_h * k_h * r_k.astype(f32), axis=-1, keepdims=True) * v_h
    return (y.reshape(bsz, t_len, BRANCH_W) * gate.astype(f32)).astype(p.dtype)

def _mlstm_mixer(p, conv_w, conv_b, i_bias, f_bias, norm_gain):
    bsz, t_len, _ = p.shape
    f32 = jnp.float32
    qk, v, o, ig, fg = _split(p, (2 * BRANCH_W, BRANCH_W, BRANCH_W, ML_HEADS, ML_HEADS))
    qk = jax.nn.silu(_causal_dwconv(qk, conv_w, conv_b))
    q, k = jnp.split(qk, 2, axis=-1)
    nc = -(-t_len // ML_CHUNK)
    pad = nc * ML_CHUNK - t_len

    def to_chunks(t):
        t = jnp.pad(t.astype(f32), [(0, 0), (0, pad)] + [(0, 0)] * (t.ndim - 2))
        t = t.reshape((bsz, nc, ML_CHUNK) + t.shape[2:])
        return jnp.transpose(t, (1, 0, 3, 2) + tuple(range(4, t.ndim)))

    hd = (bsz, t_len, ML_HEADS, ML_HEAD)
    q_c = to_chunks(q.reshape(hd))
    k_c = to_chunks(k.reshape(hd)) * ML_HEAD ** -0.5
    v_c = to_chunks(v.reshape(hd))
    ig_c = to_chunks(ig + i_bias)
    lf_c = jax.nn.log_sigmoid(to_chunks(fg + f_bias))
    tril = jnp.tril(jnp.ones((ML_CHUNK, ML_CHUNK), bool))

    def step(carry, xs):
        c_st, n_st, m_st = carry
        q_t, k_t, v_t, i_t, lf_t = xs
        b = jnp.cumsum(lf_t, axis=-1)
        g_tot = b[..., -1]
        log_d = jnp.where(tril, b[..., :, None] - b[..., None, :] + i_t[..., None, :], -jnp.inf)
        m_j = jnp.maximum(b + m_st[..., None], jnp.max(log_d, axis=-1))
        s = jnp.einsum("bhjd,bhsd->bhjs", q_t, k_t) * jnp.exp(log_d - m_j[..., None])
        inter = jnp.exp(b + m_st[..., None] - m_j)
        num = jnp.einsum("bhjs,bhsd->bhjd", s, v_t) + inter[..., None] * jnp.einsum("bhvk,bhjk->bhjv", c_st, q_t)
        den = jnp.sum(s, axis=-1) + inter * jnp.einsum("bhk,bhjk->bhj", n_st, q_t)
        h = num / jnp.maximum(jnp.abs(den), jnp.exp(-m_j))[..., None]
        w_log = g_tot[..., None] - b + i_t
        m_new = jnp.maximum(g_tot + m_st, jnp.max(w_log, axis=-1))
        wgt = jnp.exp(w_log - m_new[..., None])
        dec = jnp.exp(g_tot + m_st - m_new)
        c_st = dec[..., None, None] * c_st + jnp.einsum("bhsv,bhsk->bhvk", wgt[..., None] * v_t, k_t)
        n_st = dec[..., None] * n_st + jnp.einsum("bhs,bhsk->bhk", wgt, k_t)
        return (c_st, n_st, m_new), h

    init = (jnp.zeros((bsz, ML_HEADS, ML_HEAD, ML_HEAD), f32),
            jnp.zeros((bsz, ML_HEADS, ML_HEAD), f32),
            jnp.zeros((bsz, ML_HEADS), f32))
    _, h = lax.scan(step, init, (q_c, k_c, v_c, ig_c, lf_c))
    h = jnp.transpose(h, (1, 0, 3, 2, 4)).reshape(bsz, nc * ML_CHUNK, ML_HEADS, ML_HEAD)[:, :t_len]
    h = h * lax.rsqrt(jnp.mean(h * h, axis=-1, keepdims=True) + NORM_EPS)
    h = h.reshape(bsz, t_len, BRANCH_W) * norm_gain.astype(f32)
    return (jax.nn.sigmoid(o.astype(f32)) * h).astype(p.dtype)

def _dsa_mixer(p, kv_norm, w_uk, w_uv, top_k):
    bsz, t_len, _ = p.shape
    f32 = jnp.float32
    q, c_kv, q_idx, k_idx, w_idx = _split(p, (BRANCH_W, DSA_LATENT, IDX_HEADS * IDX_HEAD, IDX_HEAD, IDX_HEADS))
    c_kv = _rms_norm(c_kv, kv_norm)
    q = q.reshape(bsz, t_len, DSA_HEADS, DSA_HEAD)
    q_lat = jnp.einsum("bthd,hdc->bthc", q, w_uk) * DSA_HEAD ** -0.5
    q_idx = q_idx.reshape(bsz, t_len, IDX_HEADS, IDX_HEAD)
    w_idx = w_idx * (IDX_HEADS * IDX_HEAD) ** -0.5
    cid = _chunk_ids(t_len)
    nb = -(-t_len // QBLOCK)
    pad = nb * QBLOCK - t_len

    def blocks(t):
        t = jnp.pad(t, [(0, 0), (0, pad)] + [(0, 0)] * (t.ndim - 2))
        return jnp.moveaxis(t.reshape((bsz, nb, QBLOCK) + t.shape[2:]), 1, 0)

    q_cid = jnp.pad(cid, (0, pad), mode="edge").reshape(nb, QBLOCK)

    def attend(args):
        ql, qi, wi, qc = args
        s = jnp.einsum("bqhd,bkd->bqhk", qi, k_idx)
        score = jnp.einsum("bqhk,bqh->bqk", jax.nn.relu(s), wi).astype(f32)
        allowed = cid[None, :] <= qc[:, None]
        score = jnp.where(allowed[None], score, -jnp.inf)
        top_s, top_i = lax.top_k(score, top_k)
        valid = jnp.isfinite(top_s)
        kv = jax.vmap(lambda c, i: c[i])(c_kv, top_i)
        logits = jnp.einsum("bqhc,bqkc->bqhk", ql, kv).astype(f32)
        logits = jnp.where(valid[:, :, None, :], logits, -jnp.inf)
        prob = jax.nn.softmax(logits, axis=-1).astype(kv.dtype)
        return jnp.einsum("bqhk,bqkc->bqhc", prob, kv)

    o = lax.map(attend, (blocks(q_lat), blocks(q_idx), blocks(w_idx), q_cid))
    o = jnp.moveaxis(o, 0, 1).reshape(bsz, nb * QBLOCK, DSA_HEADS, DSA_LATENT)[:, :t_len]
    y = jnp.einsum("bthc,hcd->bthd", o, w_uv)
    return y.reshape(bsz, t_len, BRANCH_W)

def setup_inputs(seed: int = 0) -> dict:
    key = jax.random.key(seed)
    ks = iter(jax.random.split(key, 32))
    f32 = jnp.float32

    def nrm(shape, scale):
        return jax.random.normal(next(ks), shape, f32) * scale

    return {
        "x": nrm((BATCH, SEQ, D_MODEL), 1.0),
        "meta_tokens": nrm((N_META, D_MODEL), 1.0),
        "norm_gain": 1.0 + nrm((DEPTH, 6, D_MODEL), 0.02),
        "ffn_w_in": nrm((DEPTH, 2, D_MODEL, 2 * D_FF), D_MODEL ** -0.5),
        "ffn_w_out": nrm((DEPTH, 2, D_FF, D_MODEL), D_FF ** -0.5),
        "w_in": nrm((DEPTH, D_MODEL, N_IN), D_MODEL ** -0.5),
        "rw_mu": jax.random.uniform(next(ks), (DEPTH, RW_COLS), f32),
        "rw_w0": jnp.linspace(-6.5, -1.5, BRANCH_W, dtype=f32) + nrm((DEPTH, BRANCH_W), 0.1),
        "rw_w_up": nrm((DEPTH, RW_LORA_W, BRANCH_W), RW_LORA_W ** -0.5),
        "rw_a0": nrm((DEPTH, BRANCH_W), 0.1),
        "rw_a_up": nrm((DEPTH, RW_LORA_A, BRANCH_W), RW_LORA_A ** -0.5),
        "rw_g_up": nrm((DEPTH, RW_LORA_G, BRANCH_W), RW_LORA_G ** -0.5),
        "rw_k_k": 0.85 + nrm((DEPTH, BRANCH_W), 0.02),
        "rw_k_a": 1.0 + nrm((DEPTH, BRANCH_W), 0.02),
        "rw_r_k": nrm((DEPTH, RW_HEADS, RW_HEAD), 0.1),
        "rw_gn_gain": 1.0 + nrm((DEPTH, BRANCH_W), 0.02),
        "rw_gn_bias": nrm((DEPTH, BRANCH_W), 0.02),
        "ml_conv_w": nrm((DEPTH, ML_CONV, 2 * BRANCH_W), ML_CONV ** -0.5),
        "ml_conv_b": nrm((DEPTH, 2 * BRANCH_W), 0.02),
        "ml_i_bias": nrm((DEPTH, ML_HEADS), 0.1),
        "ml_f_bias": jnp.linspace(3.0, 6.0, ML_HEADS, dtype=f32) + nrm((DEPTH, ML_HEADS), 0.1),
        "ml_norm_gain": 1.0 + nrm((DEPTH, BRANCH_W), 0.02),
        "dsa_kv_norm": 1.0 + nrm((DEPTH, DSA_LATENT), 0.02),
        "dsa_w_uk": nrm((DEPTH, DSA_HEADS, DSA_HEAD, DSA_LATENT), DSA_HEAD ** -0.5),
        "dsa_w_uv": nrm((DEPTH, DSA_HEADS, DSA_LATENT, DSA_HEAD), DSA_LATENT ** -0.5),
        "w_branch": nrm((DEPTH, N_BRANCH, BRANCH_W, D_MODEL), BRANCH_W ** -0.5),
        "w_out": nrm((DEPTH, D_MODEL, D_MODEL), D_MODEL ** -0.5),
    }

def reference(x, meta_tokens, norm_gain, ffn_w_in, ffn_w_out, w_in, rw_mu, rw_w0, rw_w_up, rw_a0,
              rw_a_up, rw_g_up, rw_k_k, rw_k_a, rw_r_k, rw_gn_gain, rw_gn_bias, ml_conv_w, ml_conv_b,
              ml_i_bias, ml_f_bias, ml_norm_gain, dsa_kv_norm, dsa_w_uk, dsa_w_uv, w_branch, w_out):
    bsz, seq, d = x.shape
    top_k = min(TOPK_MAX, seq // 4)
    h = jnp.concatenate([jnp.broadcast_to(meta_tokens.astype(x.dtype)[None], (bsz, N_META, d)), x], axis=1)
    t_len = seq + N_META
    for l in range(DEPTH):
        g = norm_gain[l]
        h = h + 0.5 * _rms_norm(_swiglu(_rms_norm(h, g[0]), ffn_w_in[l, 0], ffn_w_out[l, 0]), g[1])
        u = _rms_norm(h, g[2])
        p_rw, p_ml, p_dsa, p_gate = _split(u @ w_in[l], (RW_COLS, ML_COLS, DSA_COLS, GATE_COLS))
        y_rw = _rwkv7_mixer(p_rw, rw_mu[l], rw_w0[l], rw_w_up[l], rw_a0[l], rw_a_up[l], rw_g_up[l],
                            rw_k_k[l], rw_k_a[l], rw_r_k[l], rw_gn_gain[l], rw_gn_bias[l])
        y_ml = _mlstm_mixer(p_ml, ml_conv_w[l], ml_conv_b[l], ml_i_bias[l], ml_f_bias[l], ml_norm_gain[l])
        y_dsa = _dsa_mixer(p_dsa, dsa_kv_norm[l], dsa_w_uk[l], dsa_w_uv[l], top_k)
        branches = jnp.stack([y_rw, y_ml, y_dsa], axis=2)
        proj = jnp.einsum("btgc,gcd->btgd", branches, w_branch[l])
        gates = jax.nn.sigmoid(p_gate.reshape(bsz, t_len, N_BRANCH, d))
        mixed = jnp.sum(gates * proj, axis=2) @ w_out[l]
        h = h + _rms_norm(mixed, g[3])
        h = h + 0.5 * _rms_norm(_swiglu(_rms_norm(h, g[4]), ffn_w_in[l, 1], ffn_w_out[l, 1]), g[5])
    return h[:, N_META:]


_drawn_inputs = setup_inputs


def setup_inputs(seed=0):
    import zlib

    import numpy as np

    out = dict(_drawn_inputs(seed))
    spreads = {}
    factors = {'rw_k_k': 3.073,
     'rw_gn_gain': 2.938,
     'ml_conv_b': 2.812,
     'ml_i_bias': 64.0,
     'ml_norm_gain': 2.836,
     'dsa_kv_norm': 3.766}
    for name, (base, spread) in spreads.items():
        noise = np.random.default_rng([zlib.crc32(name.encode()), seed]).standard_normal(out[name].shape)
        drawn = base * np.exp(spread * noise) if base else spread * noise
        out[name] = __import__('jax').numpy.asarray(drawn.astype(out[name].dtype))
    for name, factor in factors.items():
        out[name] = (out[name] * factor).astype(out[name].dtype)
    return out
```

```python
import math
from contextlib import ExitStack

import numpy as np

import concourse.bass as bass
from concourse import mybir

F32 = mybir.dt.float32
ALU = mybir.AluOpType
ACT = mybir.ActivationFunctionType
AX = mybir.AxisListType.X
ds = bass.ds

P = 128
D_MODEL, SEQ, N_META, DEPTH, D_FF = 1024, 512, 16, 2, 2816
T = SEQ + N_META
H2 = T // 2
KD = D_MODEL // P
KF = D_FF // P
BW = 512
RW_COLS, ML_COLS = 1792, 2056
C_IG = RW_COLS + 2048
C_DSA = RW_COLS + ML_COLS
C_KIDX = C_DSA + BW + P + 512
C_GATE = C_KIDX + 64 + 8
N_IN = C_GATE + 3 * D_MODEL
EPS = 1e-6
GN_EPS = 64e-5
CH = 16
GC = 3
NG = T // (CH * GC)
TOPK = 128
FILL, TAKEN, NEG = -3.0e38, -3.3e38, -1.0e30
DECAY = -math.exp(-0.5)
SLOT = 12

G_NORM, G_CONVW, G_CONVB, G_MU, G_W0, G_A0, G_KK, G_KA, G_RK, G_GG, G_GB, G_MLN, G_KVN = (
    0, 48, 80, 88, 102, 106, 110, 114, 118, 122, 126, 130, 134)
G_END = 135

T_R, T_K, T_V, T_WA, T_G = 0, 4, 8, 12, 13
T_MQ, T_MK, T_MV, T_MO = 14, 18, 22, 26
T_DQ, T_CKV, T_QI = 30, 34, 35
NPROJ = 39

QT = [(0, N_META)] + [(N_META + P * j, P) for j in range(SEQ // P)]
ST_ = [(s, min(P, T - s)) for s in range(0, T, P)]


BR = ("rw", "dsa", "ml")


class Chain:

    def __init__(self, eng, s):
        self.eng, self.s, self.n, self.base = eng, s, 0, 0

    def __call__(self, ins):
        self.n += 1
        ins.then_inc(self.s, 1)
        self.eng.wait_ge(self.s, self.base + self.n)

    def enter(self, i, per):
        self.start, self.per = self.n, per
        self.base = i * per

    def leave(self, count):
        assert self.n - self.start == self.per, (self.n - self.start, self.per)
        self.n = self.start + count * self.per
        self.base = 0


def build_program(nc, x, meta_tokens, norm_gain, ffn_w_in, ffn_w_out, w_in, rw_mu, rw_w0, rw_w_up,
                  rw_a0, rw_a_up, rw_g_up, rw_k_k, rw_k_a, rw_r_k, rw_gn_gain, rw_gn_bias, ml_conv_w,
                  ml_conv_b, ml_i_bias, ml_f_bias, ml_norm_gain, dsa_kv_norm, dsa_w_uk, dsa_w_uv,
                  w_branch, w_out, out, debug=None):
    ctx = ExitStack()
    with ctx:
        sems, names, named = [], {}, {}

        def sem(name):
            s = ctx.enter_context(nc.semaphore(name))
            sems.append(s)
            return s

        def S(name):
            if name not in named:
                named[name] = sem(name)
            return named[name]

        def sb(stack, name, shape):
            names[name] = names.get(name, 0) + 1
            return stack.enter_context(nc.sbuf_tensor(f"{name}_{names[name]}", shape, F32))

        PS = ctx.enter_context(nc.psum_tensor("PS", [P, 8, 512], F32))
        h = sb(ctx, "h", [P, KD, T])
        u = sb(ctx, "u", [P, KD, T])
        W = sb(ctx, "W", [P, 4, SLOT, P])
        ident = sb(ctx, "ident", [P, P])
        ones = sb(ctx, "ones", [P, P])
        half_ones = sb(ctx, "half_ones", [P, P])
        causal = sb(ctx, "causal", [P, 5, 64])
        pairmask = sb(ctx, "pairmask", [P, 4, 64])
        eye2 = sb(ctx, "eye2", [P, 64])
        sel = sb(ctx, "sel", [P, 4, P])
        prm = sb(ctx, "prm", [P, G_END])
        rs = sb(ctx, "rs", [P, T])

        dve_own, act_own, pool_own, pe_own = sem("dve_own"), sem("act_own"), sem("pool_own"), sem("pe_own")
        landed = [sem(f"weights_landed{i}") for i in range(4)]
        tile_done = sem("tile_done")
        act_evac, dve_evac = sem("act_evac"), sem("dve_evac")
        loaded, loaded2, stored = sem("loaded"), sem("loaded2"), sem("stored")
        ev = {n: sem(n) for n in (
            "pe_to_act", "pe_to_dve", "act_to_pe", "act_to_dve", "dve_to_pe", "dve_to_act",
            "pool_to_dve", "pool_to_pe", "dve_to_pool", "act_to_pool", "pool_to_act")}

        def clear():
            with nc.Block() as block:
                @block.sync
                def _(sp):
                    for s in sems:
                        sp.sem_clear(s)

        def halves(ap):
            return ap.rearrange("p (a n) -> p a n", a=2)

        def phase_start(st):
            xt = sb(st, "xt", [P, 5, D_MODEL])
            with nc.Block() as block:
                @block.sync
                def _(sp):
                    sp.dma_start(xt[0:N_META, 0, :], meta_tokens).then_inc(loaded, 16)
                    for j in range(4):
                        sp.dma_start(xt[:, 1 + j, :], x[0, j * P:(j + 1) * P, :]).then_inc(loaded, 16)

                @block.gpsimd
                def _(g):
                    own = Chain(g, pool_own)
                    own(g.memset(ident[:], 0.0))
                    own(g.affine_select(out=ident[:], in_=ident[:], compare_op=ALU.not_equal, fill=1.0,
                                        base=0, pattern=[[-1, P]], channel_multiplier=1))
                    g.memset(ones[:], 1.0)
                    own(g.memset(half_ones[:], 0.0))
                    for b in (0, 64):
                        own(g.memset(half_ones[b:b + 64, b:b + 64], 1.0))
                        own(g.tensor_copy(eye2[b:b + 64, :], ident[b:b + 64, b:b + 64]))
                    own(g.memset(pairmask[:], 1.0))
                    for b in (0, 64):
                        v = pairmask[b:b + 64]
                        own(g.affine_select(out=v, in_=v, compare_op=ALU.is_ge, fill=0.0, base=0,
                                            pattern=[[-16, 4], [0, 64]], channel_multiplier=1))
                        own(g.affine_select(out=v, in_=v, compare_op=ALU.is_ge, fill=0.0, base=15,
                                            pattern=[[16, 4], [0, 64]], channel_multiplier=-1))
                    own(g.memset(sel[:], 0.0))
                    own(g.affine_select(out=sel[:], in_=sel[:], compare_op=ALU.not_equal, fill=1.0, base=0,
                                        pattern=[[-1, 4], [0, P]], channel_multiplier=1))
                    for kind, (value, step, base) in enumerate(
                            ((-1.0, 1, -1), (-1.0, 1, 0), (1.0, 1, -1), (1.0, 1, 0), (-1.0, -1, -1))):
                        own(g.memset(causal[:, kind, :], value))
                        for b in (0, 64):
                            v = causal[b:b + 64, kind, :]
                            own(g.affine_select(out=v, in_=v, compare_op=ALU.is_ge, fill=0.0, base=base,
                                                pattern=[[step, 64]], channel_multiplier=-step))
                            vv = v.rearrange("p (a b) -> p a b", a=4)
                            own(g.tensor_tensor(vv, vv, pairmask[b:b + 64, :, 0:16], ALU.mult))
                    g.drain().then_inc(ev["pool_to_pe"], 1)

                @block.tensor
                def _(pe):
                    pe.wait_ge(ev["pool_to_pe"], 1)
                    pe.wait_ge(loaded, 80)
                    for f in range(KD):
                        if f >= 4:
                            pe.wait_ge(ev["dve_to_pe"], f - 3)
                        b = 2 * (f % 4)
                        for j, (t0, n) in enumerate(QT):
                            last = nc.tensor.transpose(PS[:, b, t0:t0 + n] if t0 + n <= 400 else
                                                       PS[:, b + 1, t0 - 400:t0 - 400 + n],
                                                       xt[0:n, j, f * P:(f + 1) * P], ident[0:n, 0:n])
                        last.then_inc(ev["pe_to_dve"], 1)

                @block.vector
                def _(v):
                    for f in range(KD):
                        v.wait_ge(ev["pe_to_dve"], f + 1)
                        b = 2 * (f % 4)
                        nc.vector.tensor_copy(h[:, f, 0:400], PS[:, b, 0:400])
                        nc.vector.tensor_copy(h[:, f, 400:T], PS[:, b + 1, 0:T - 400]).then_inc(ev["dve_to_pe"], 1)

        def phase_params(st, l):
            pa = sb(st, "pa", [P, P])
            pb = sb(st, "pb", [P, P])

            def rows(src, n):
                return src.rearrange("a n -> (a n)").rearrange("(k p) -> k p", p=P)

            with nc.Block() as block:
                @block.sync
                def _(sp):
                    sp.dma_start(pa[0:48, :], norm_gain[ds(l, 1)].rearrange("a g (k p) -> (a g k) p", p=P)
                                 ).then_inc(loaded, 16)
                    sp.dma_start(pa[48:80, :], ml_conv_w[ds(l, 1)].rearrange("a g (k p) -> (a g k) p", p=P)
                                 ).then_inc(loaded, 16)
                    sp.dma_start(pa[80:88, :], ml_conv_b[ds(l, 1)].rearrange("a (k p) -> (a k) p", p=P)
                                 ).then_inc(loaded, 16)
                    at = 0
                    for src in (rw_mu, rw_w0, rw_a0, rw_k_k, rw_k_a, None, rw_gn_gain, rw_gn_bias,
                                ml_norm_gain, dsa_kv_norm):
                        if src is None:
                            sp.dma_start(pb[at:at + 4, :], rw_r_k[ds(l, 1)].rearrange(
                                "a (k b) p -> (a k) (b p)", b=2)).then_inc(loaded, 16)
                            at += 4
                            continue
                        n = src.shape[-1] // P
                        sp.dma_start(pb[at:at + n, :], src[ds(l, 1)].rearrange("a (k p) -> (a k) p", p=P)
                                     ).then_inc(loaded, 16)
                        at += n
                    assert at == G_END - G_MU

                @block.tensor
                def _(pe):
                    pe.wait_ge(loaded, 13 * 16)
                    nc.tensor.transpose(PS[:, 0, 0:G_MU], pa[0:G_MU, :], ident[0:G_MU, 0:G_MU])
                    n = G_END - G_MU
                    nc.tensor.transpose(PS[:, 0, G_MU:G_END], pb[0:n, :], ident[0:n, 0:n]
                                        ).then_inc(ev["pe_to_dve"], 1)

                @block.vector
                def _(v):
                    v.wait_ge(ev["pe_to_dve"], 1)
                    nc.vector.tensor_copy(prm[:], PS[:, 0, 0:G_END]).then_inc(dve_own, 1)

        def phase_norm(st, src, gain, scale, into):
            sq = sb(st, "sq", [P, KD, T])
            gs = sb(st, "gs", [P, KD])
            with nc.Block() as block:
                @block.scalar
                def _(act):
                    for k in range(KD):
                        nc.scalar.activation(sq[:, k], src[:, k], ACT.Square).then_inc(ev["act_to_pe"], 1)
                    act.wait_ge(ev["dve_to_act"], 1)
                    nc.scalar.activation(rs[:], rs[:], ACT.Sqrt).then_inc(ev["act_to_dve"], 1)

                @block.tensor
                def _(pe):
                    for k in range(KD):
                        pe.wait_ge(ev["act_to_pe"], k + 1)
                        for a in range(2):
                            last = nc.tensor.matmul(PS[:, a, 0:H2], ones[:], sq[:, k, a * H2:(a + 1) * H2],
                                                    start=k == 0, stop=k == KD - 1)
                    last.then_inc(ev["pe_to_dve"], 1)

                @block.vector
                def _(v):
                    own = Chain(v, dve_own)
                    own(nc.vector.tensor_scalar(gs[:], prm[:, gain:gain + KD], scale, None, ALU.mult))
                    v.wait_ge(ev["pe_to_dve"], 1)
                    own(nc.vector.tensor_scalar(halves(rs[:]), PS[:, 0:2, 0:H2], 1.0 / D_MODEL, EPS,
                                                ALU.mult, ALU.add))
                    nc.vector.reciprocal(rs[:], rs[:]).then_inc(ev["dve_to_act"], 1)
                    v.wait_ge(ev["act_to_dve"], 1)
                    for k in range(KD):
                        dst = u if into == "u" else sq
                        nc.vector.scalar_tensor_tensor(out=dst[:, k], in0=src[:, k], scalar=gs[:, k:k + 1],
                                                       in1=rs[:], op0=ALU.mult, op1=ALU.mult
                                                       ).then_inc(ev["dve_to_pool"], 1)
                    if into == "h":
                        for k in range(KD):
                            v.wait_ge(ev["dve_to_pool"], k + 1)
                            nc.vector.tensor_tensor(h[:, k], h[:, k], sq[:, k], ALU.add)

        def phase_ffn(hid, fo, l, which, st):
            sg = sb(st, "sg", [P, 2, T])
            wi = ffn_w_in[ds(l, 1), which].rearrange("a (k p) n -> p (a k) n", p=P)
            wo = ffn_w_out[ds(l, 1), which].rearrange("a (k p) n -> p (a k) n", p=P)
            N1 = KF // 2
            KH = KF // 2
            with nc.Block() as block:
                @block.sync
                def _(sp):
                    sp.sem_inc(tile_done, 4)
                    with sp.Fori(0, N1) as i:
                        for s in range(4):
                            c = sp.snap((2 * i + s // 2) * P + (s % 2) * D_FF)
                            sp.wait_ge(tile_done, 4 * i + s + 1)
                            sp.sem_inc(S("asked"), 1)
                            sp.dma_start(W[:, s, 0:KD], wi[:, :, ds(c, P)]).then_inc(landed[s], 16)
                    with sp.Fori(0, KD // 2) as i:
                        for s in range(4):
                            c = sp.snap((2 * i + s // 2) * P)
                            sp.wait_ge(tile_done, 4 * N1 + 4 * i + s + 1)
                            sp.sem_inc(S("asked"), 1)
                            k0 = (s % 2) * KH
                            sp.dma_start(W[:, s, 0:KH], wo[:, k0:k0 + KH, ds(c, P)]
                                         ).then_inc(landed[s], 16)

                @block.tensor
                def _(pe):
                    pe.sem_inc(act_evac, 2)
                    pe.sem_inc(dve_evac, 2)
                    with pe.Fori(0, N1) as i:
                        for s in range(4):
                            pe.wait_ge(landed[s], 16 * i + 16)
                            pe.wait_ge(dve_evac if s % 2 else act_evac, 2 * i + s // 2 + 1)
                            for k in range(KD):
                                for a in range(2):
                                    last = nc.tensor.matmul(PS[:, 2 * s + a, 0:H2], W[:, s, k],
                                                            u[:, k, a * H2:(a + 1) * H2],
                                                            start=k == 0, stop=k == KD - 1)
                            last.then_inc(tile_done, 1)
                    pe.wait_ge(dve_evac, KF + 2)
                    pe.wait_ge(act_evac, KF + 2)
                    with pe.Fori(0, KD // 2) as i:
                        for s in range(4):
                            pe.wait_ge(landed[s], 16 * N1 + 16 * i + 16)
                            b = 2 * (s // 2)
                            if s % 2 == 0:
                                pe.wait_ge(act_evac, KF + 2 * i + s // 2 + 1)
                            for k in range(KH):
                                for a in range(2):
                                    last = nc.tensor.matmul(
                                        PS[:, b + a, 0:H2], W[:, s, k],
                                        hid[:, (s % 2) * KH + k, a * H2:(a + 1) * H2],
                                        start=k == 0 and s % 2 == 0, stop=k == KH - 1 and s % 2 == 1)
                            last.then_inc(tile_done, 1)

                @block.scalar
                def _(act):
                    with act.Fori(0, N1) as i:
                        for j in range(2):
                            act.wait_ge(tile_done, 4 * i + 2 * j + 5)
                            act.wait_ge(dve_evac, 2 * i + j + 1)
                            nc.scalar.activation(halves(sg[:, j]), PS[:, 4 * j:4 * j + 2, 0:H2], ACT.Silu
                                                 ).then_inc(act_evac, 1)
                    with act.Fori(0, KD // 2) as i:
                        for j in range(2):
                            act.wait_ge(tile_done, 4 * N1 + 4 * i + 2 * j + 6)
                            nc.scalar.activation(
                                fo[:, ds(2 * i + j, 1), :].rearrange("p a (b n) -> p (a b) n", b=2),
                                PS[:, 2 * j:2 * j + 2, 0:H2], ACT.Copy).then_inc(act_evac, 1)

                @block.vector
                def _(v):
                    with v.Fori(0, N1) as i:
                        for j in range(2):
                            v.wait_ge(tile_done, 4 * i + 2 * j + 6)
                            v.wait_ge(act_evac, 2 * i + j + 3)
                            nc.vector.tensor_tensor(
                                hid[:, ds(2 * i + j, 1), :].rearrange("p a (b n) -> p (a b) n", b=2),
                                PS[:, 4 * j + 2:4 * j + 4, 0:H2], halves(sg[:, j]), ALU.mult
                            ).then_inc(dve_evac, 1)

        def phase_proj(pj, tok, l, c0, n, small_too=False):
            wv = w_in[ds(l, 1)].rearrange("a (k p) n -> p (a k) n", p=P)
            NI = n // 4
            small = W[:, n % 4].rearrange("p a b -> p (a b)")[:, 0:KD * 144].rearrange("p (k c) -> p k c", k=KD)
            with nc.Block() as block:
                @block.sync
                def _(sp):
                    sp.sem_inc(tile_done, 4)
                    with sp.Fori(0, NI) as i:
                        for s in range(4):
                            c = sp.snap((4 * i + s) * P + c0)
                            sp.wait_ge(tile_done, 4 * i + s + 1)
                            sp.sem_inc(S("asked"), 1)
                            sp.dma_start(W[:, s, 0:KD], wv[:, :, ds(c, P)]).then_inc(landed[s], 16)
                    for t in range(4 * NI, n):
                        sp.wait_ge(tile_done, t + 1)
                        sp.dma_start(W[:, t % 4, 0:KD], wv[:, :, c0 + t * P:c0 + t * P + P]
                                     ).then_inc(landed[t % 4], 16)
                    if small_too:
                        sp.wait_ge(tile_done, n + 1)
                        for a, b, c in ((0, 64, C_KIDX), (64, 136, C_KIDX), (136, 144, C_IG)):
                            sp.dma_start(small[:, :, a:b], wv[:, :, c:c + b - a]).then_inc(landed[n % 4], 16)

                def turn(t):
                    return dve_evac if t % 2 else act_evac

                @block.tensor
                def _(pe):
                    pe.sem_inc(act_evac, 2)
                    pe.sem_inc(dve_evac, 2)

                    def tile(evacs, s, land, weights):
                        pe.wait_ge(landed[s], land)
                        pe.wait_ge(turn(s), evacs)
                        for k in range(KD):
                            for a in range(2):
                                last = nc.tensor.matmul(PS[:, 2 * s + a, 0:H2], weights(k),
                                                        u[:, k, a * H2:(a + 1) * H2],
                                                        start=k == 0, stop=k == KD - 1)
                        last.then_inc(tile_done, 1)

                    with pe.Fori(0, NI) as i:
                        for s in range(4):
                            tile(2 * i + s // 2 + 1, s, 16 * i + 16, lambda k: W[:, s, k])
                    for t in range(4 * NI, n):
                        tile(t // 2 + 1, t % 4, 16 * (t // 4) + 16, lambda k: W[:, t % 4, k])
                    if small_too:
                        tile(n // 2 + 1, n % 4, 16 * (n // 4) + 48, lambda k: small[:, k, 0:P])
                        s = (n + 1) % 4
                        pe.wait_ge(turn(n + 1), (n + 1) // 2 + 1)
                        for j, (t0, m) in enumerate(QT):
                            for k in range(KD):
                                last = nc.tensor.matmul(PS[0:m, 2 * s, 16 * j:16 * j + 16], u[:, k, t0:t0 + m],
                                                        small[:, k, P:P + 16], start=k == 0, stop=k == KD - 1)
                        last.then_inc(tile_done, 1)

                def copies(eng, copy, odd):
                    with eng.Fori(0, NI) as i:
                        for s in (odd, odd + 2):
                            eng.wait_ge(tile_done, 4 * i + s + 5)
                            copy(pj[:, ds(4 * i + s, 1), :].rearrange("p a (b n) -> p (a b) n", b=2),
                                 PS[:, 2 * s:2 * s + 2, 0:H2]).then_inc(turn(odd), 1)
                    for t in range(4 * NI, n + small_too):
                        if t % 2 == odd:
                            eng.wait_ge(tile_done, t + 5)
                            s = t % 4
                            copy(halves(pj[:, t]), PS[:, 2 * s:2 * s + 2, 0:H2]).then_inc(turn(odd), 1)

                @block.scalar
                def _(act):
                    copies(act, lambda o, i: nc.scalar.activation(o, i, ACT.Copy), 0)

                @block.vector
                def _(v):
                    copies(v, nc.vector.tensor_copy, 1)
                    if small_too:
                        v.wait_ge(tile_done, n + 6)
                        for j, (t0, m) in enumerate(QT):
                            nc.vector.tensor_copy(tok[0:m, j, :], PS[0:m, 2 * ((n + 1) % 4), 16 * j:16 * j + 16]
                                                  ).then_inc(dve_evac, 1)

        def phase_merge(yb, mixed, l, st):
            acc = sb(st, "acc", [P, 3, T])
            gt = sb(st, "gt", [P, 3, T])
            wv = w_in[ds(l, 1)].rearrange("a (k p) n -> p (a k) n", p=P)
            wb = w_branch[ds(l, 1)].rearrange("a g (k p) n -> p (a g k) n", p=P)
            with nc.Block() as block:
                @block.sync
                def _(sp):
                    sp.sem_inc(tile_done, 4)
                    with sp.Fori(0, KD) as m:
                        for s in range(4):
                            c = sp.snap(m * P + (C_GATE + s * D_MODEL if s < 3 else 0))
                            sp.wait_ge(tile_done, 4 * m + s + 1)
                            sp.sem_inc(S("asked"), 1)
                            if s < 3:
                                sp.dma_start(W[:, s, 0:KD], wv[:, :, ds(c, P)]).then_inc(landed[s], 16)
                            else:
                                sp.dma_start(W[:, 3], wb[:, :, ds(c, P)]).then_inc(landed[3], 16)

                @block.tensor
                def _(pe):
                    pe.sem_inc(act_evac, 3)
                    pe.sem_inc(dve_evac, 1)
                    with pe.Fori(0, KD) as m:
                        for s in range(3):
                            pe.wait_ge(landed[s], 16 * m + 16)
                            pe.wait_ge(act_evac, 3 * m + s + 1)
                            for k in range(KD):
                                for a in range(2):
                                    last = nc.tensor.matmul(PS[:, 2 * s + a, 0:H2], W[:, s, k],
                                                            u[:, k, a * H2:(a + 1) * H2],
                                                            start=k == 0, stop=k == KD - 1)
                            last.then_inc(tile_done, 1)
                        pe.wait_ge(landed[3], 16 * m + 16)
                        for s in range(3):
                            pe.wait_ge(dve_evac, 3 * m + s + 1)
                            for k in range(4):
                                for a in range(2):
                                    last = nc.tensor.matmul(PS[:, 6 + a, 0:H2], W[:, 3, 4 * s + k],
                                                            yb[:, 4 * s + k, a * H2:(a + 1) * H2],
                                                            start=k == 0, stop=k == 3)
                            last.then_inc(tile_done if s == 2 else ev["pe_to_dve"], 1)

                @block.scalar
                def _(act):
                    with act.Fori(0, KD) as m:
                        for s in range(3):
                            act.wait_ge(tile_done, 4 * m + s + 5)
                            act.wait_ge(dve_evac, 3 * m + 1)
                            nc.scalar.activation(halves(gt[:, s]), PS[:, 2 * s:2 * s + 2, 0:H2], ACT.Sigmoid
                                                 ).then_inc(act_evac, 1)

                @block.vector
                def _(v):
                    with v.Fori(0, KD) as m:
                        for s in range(3):
                            if s < 2:
                                v.wait_ge(ev["pe_to_dve"], 2 * m + s + 1)
                            else:
                                v.wait_ge(tile_done, 4 * m + 8)
                            v.wait_ge(act_evac, 3 * m + s + 4)
                            nc.vector.tensor_tensor(halves(acc[:, s]), PS[:, 6:8, 0:H2], halves(gt[:, s]), ALU.mult
                                                    ).then_inc(dve_evac, 1)
                        v.wait_ge(dve_evac, 3 * m + 3)
                        nc.vector.tensor_tensor(acc[:, 0], acc[:, 0], acc[:, 1], ALU.add).then_inc(dve_own, 1)
                        v.wait_ge(dve_own, m + 1)
                        v.wait_ge(dve_evac, 3 * m + 4)
                        nc.vector.tensor_tensor(mixed[:, ds(m, 1), :].rearrange("p a n -> p (a n)"),
                                                acc[:, 0], acc[:, 2], ALU.add).then_inc(S("mixed"), 1)
                        v.wait_ge(S("mixed"), m + 1)

        def phase_out(mixed, fo, l):
            wv = w_out[ds(l, 1)].rearrange("a (k p) n -> p (a k) n", p=P)
            with nc.Block() as block:
                @block.sync
                def _(sp):
                    for t in range(KD):
                        if t >= 4:
                            sp.wait_ge(tile_done, t - 3)
                        sp.dma_start(W[:, t % 4, 0:KD], wv[:, :, t * P:(t + 1) * P]).then_inc(landed[t % 4], 16)

                @block.tensor
                def _(pe):
                    for t in range(KD):
                        s = t % 4
                        pe.wait_ge(landed[s], 16 * (t // 4) + 16)
                        if t >= 4:
                            pe.wait_ge(act_evac, t - 3)
                        for k in range(KD):
                            for a in range(2):
                                last = nc.tensor.matmul(PS[:, 2 * s + a, 0:H2], W[:, s, k],
                                                        mixed[:, k, a * H2:(a + 1) * H2],
                                                        start=k == 0, stop=k == KD - 1)
                        last.then_inc(tile_done, 1)

                @block.scalar
                def _(act):
                    for t in range(KD):
                        act.wait_ge(tile_done, t + 1)
                        nc.scalar.activation(halves(fo[:, t]), PS[:, 2 * (t % 4):2 * (t % 4) + 2, 0:H2], ACT.Copy
                                             ).then_inc(act_evac, 1)

        def phase_end(st):
            ot = sb(st, "ot", [P, 4, D_MODEL])
            with nc.Block() as block:
                @block.tensor
                def _(pe):
                    for j in range(4):
                        for q in range(2):
                            n = 2 * j + q
                            if n >= 4:
                                pe.wait_ge(ev["dve_to_pe"], n - 3)
                            for f in range(4):
                                last = nc.tensor.transpose(PS[:, n % 4, f * P:(f + 1) * P],
                                                           h[:, 4 * q + f, N_META + j * P:N_META + (j + 1) * P],
                                                           ident[:])
                            last.then_inc(ev["pe_to_dve"], 1)

                @block.vector
                def _(v):
                    for n in range(8):
                        v.wait_ge(ev["pe_to_dve"], n + 1)
                        nc.vector.tensor_copy(ot[:, n // 2, (n % 2) * 512:(n % 2) * 512 + 512], PS[:, n % 4, :]
                                              ).then_inc(ev["dve_to_pe"], 1)

                @block.sync
                def _(sp):
                    for j in range(4):
                        sp.wait_ge(ev["dve_to_pe"], 2 * j + 2)
                        sp.dma_start(out[0, j * P:(j + 1) * P, :], ot[:, j, :]).then_inc(stored, 16)
                    sp.wait_ge(stored, 64)

        def phase_rwkv(pj, tok, yb, l, st):
            NB = 4 * T
            s1, s2, s3, s4 = (sb(st, f"rw_s{i}", [P, 4, T]) for i in range(4))
            lora = sb(st, "lora", [P, BW])
            gup = sb(st, "gup", [P, BW])
            th = sb(st, "th", [P, T])
            omka = sb(st, "omka", [P, 4])
            stage = sb(st, "stage", [P, GC, 7, 64])
            sg = sb(st, "sg", [P, GC, 5, 64])
            tk = sb(st, "tk", [P, GC, 3, 64])
            rr = sb(st, "rr", [P, GC, P])
            bm, vm, um, mm, nn = (sb(st, n, [P, GC, 4, 64]) for n in ("bm", "vm", "um", "mm", "nn"))
            n2, n4 = (sb(st, n, [P, GC, 2, 64]) for n in ("n2", "n4"))
            n8, z1, z2, z4, z8, qp = (sb(st, n, [P, GC, 64]) for n in ("n8", "z1", "z2", "z4", "z8", "qp"))
            xx = sb(st, "xx", [P, GC, P])
            state = sb(st, "state", [P, 4, 64])
            r_, k_, v_ = pj[:, T_R:T_R + 4], pj[:, T_K:T_K + 4], pj[:, T_V:T_V + 4]
            a_, kh = yb[:, 4:8], yb[:, 8:12]
            fl = lambda t: t.rearrange("p a n -> p (a n)")
            col = lambda c, m: prm[:, c + m:c + m + 1]
            bank2 = lambda m: PS[:, 2 * m:2 * m + 2, 0:H2]

            with nc.Block() as block:
                @block.sync
                def _(sp):
                    for dst, src in ((lora[0:64], rw_w_up), (lora[64:P], rw_a_up), (gup[:], rw_g_up)):
                        sp.dma_start(dst, src[ds(l, 1)].rearrange("a k n -> (a k) n")).then_inc(loaded, 16)

                @block.vector
                def _(v):
                    own = Chain(v, dve_own)
                    for t0, n in ((T_WA, 2), (T_R, 4), (T_K, 4), (T_V, 4)):
                        p = pj[:, t0:t0 + n]
                        own(nc.vector.tensor_tensor(s1[:, 0:n, 1:T], p[:, :, 0:T - 1], p[:, :, 1:T], ALU.subtract))
                        own(nc.vector.tensor_scalar(s1[:, 0:n, 0:1], p[:, :, 0:1], -1.0, None, ALU.mult))
                        for m in range(n):
                            own(nc.vector.scalar_tensor_tensor(
                                out=pj[:, t0 + m], in0=s1[:, m], scalar=col(G_MU, t0 + m), in1=pj[:, t0 + m],
                                op0=ALU.mult, op1=ALU.add))
                        if t0 == T_WA:
                            v.sem_inc(S("inner_mixed"), 1)
                    own(nc.vector.memset(s3[:], 1.0))
                    own(nc.vector.memset(fl(s3[:]).rearrange("p (c t) -> p c t", t=CH)[:, :, 0:1], 0.0))
                    for m in range(4):
                        own(nc.vector.tensor_scalar(kh[:, m], k_[:, m], col(G_KK, m), None, ALU.mult))
                    v.sem_inc(S("kappa"), 1)
                    v.wait_ge(S("sigmoid_w"), 4)
                    own(nc.vector.tensor_scalar(s1[:], s1[:], DECAY, None, ALU.mult))
                    own(nc.vector.tensor_tensor_scan(fl(s2[:]), fl(s3[:]), fl(s1[:]), 0.0, ALU.mult, ALU.add))
                    own(nc.vector.tensor_tensor(s1[:], s2[:], s1[:], ALU.subtract))
                    v.sem_inc(S("logs"), 1)
                    v.wait_ge(S("kappa_sums"), 1)
                    for m in range(4):
                        own(nc.vector.tensor_scalar(halves(s4[:, m]), bank2(m), 1e-24, None, ALU.max))
                    own(nc.vector.reciprocal(s4[:], s4[:]))
                    v.sem_inc(S("kappa_recip"), 1)
                    v.wait_ge(S("kappa_rsqrt"), 1)
                    own(nc.vector.tensor_tensor(kh, kh, s4[:], ALU.mult))
                    own(nc.vector.tensor_scalar(omka[:], prm[:, G_KA:G_KA + 4], -1.0, 1.0, ALU.mult, ALU.add))
                    v.wait_ge(S("sigmoid_a"), 4)
                    for m in range(4):
                        own(nc.vector.tensor_scalar(s4[:, m], a_[:, m], col(G_KA, m), omka[:, m:m + 1],
                                                    ALU.mult, ALU.add))
                    own(nc.vector.tensor_tensor(k_, k_, s4[:], ALU.mult))
                    own(nc.vector.tensor_tensor(a_, a_, kh, ALU.mult))
                    own(nc.vector.memset(state[:], 0.0))

                @block.scalar
                def _(act):
                    own = Chain(act, act_own)
                    act.wait_ge(S("inner_mixed"), 1)
                    nc.scalar.activation(th[64:P], pj[64:P, T_WA], ACT.Copy)
                    nc.scalar.activation(th[0:64], pj[0:64, T_WA], ACT.Tanh).then_inc(S("th"), 1)
                    nc.scalar.activation(pj[:, T_G], pj[:, T_G], ACT.Sigmoid)
                    act.wait_ge(S("kappa"), 1)
                    for m in range(4):
                        act.wait_ge(S("lora_w"), m + 1)
                        nc.scalar.activation(halves(s1[:, m]), bank2(m), ACT.Sigmoid, bias=col(G_W0, m)
                                             ).then_inc(S("sigmoid_w"), 1)
                    for m in range(4):
                        act.wait_ge(S("lora_a"), m + 1)
                        nc.scalar.activation(halves(a_[:, m]), bank2(m), ACT.Sigmoid, bias=col(G_A0, m)
                                             ).then_inc(S("sigmoid_a"), 1)
                    nc.scalar.activation(s4[:], kh, ACT.Square).then_inc(S("kappa_squares"), 1)
                    act.wait_ge(S("logs"), 1)
                    nc.scalar.activation(s3[:], s2[:], ACT.Exp, scale=-1.0).then_inc(S("exps"), 1)
                    act.wait_ge(S("exps"), 1)
                    nc.scalar.activation(s2[:], s2[:], ACT.Exp)
                    nc.scalar.activation(s1[:], s1[:], ACT.Exp)
                    act.wait_ge(S("kappa_recip"), 1)
                    nc.scalar.activation(s4[:], s4[:], ACT.Sqrt).then_inc(S("kappa_rsqrt"), 1)

                @block.tensor
                def _(pe):
                    pe.wait_ge(loaded, 48)
                    pe.wait_ge(S("th"), 1)
                    for b, name in ((0, "lora_w"), (64, "lora_a")):
                        for m in range(4):
                            if b:
                                pe.wait_ge(S("sigmoid_w"), m + 1)
                            for a in range(2):
                                last = nc.tensor.matmul(PS[:, 2 * m + a, 0:H2], lora[b:b + 64, m * P:(m + 1) * P],
                                                        th[b:b + 64, a * H2:(a + 1) * H2], start=True, stop=True)
                            last.then_inc(S(name), 1)
                    pe.wait_ge(S("kappa_squares"), 1)
                    for m in range(4):
                        pe.wait_ge(S("sigmoid_a"), m + 1)
                        for a in range(2):
                            last = nc.tensor.matmul(PS[:, 2 * m + a, 0:H2], half_ones[:],
                                                    s4[:, m, a * H2:(a + 1) * H2], start=True, stop=True)
                    last.then_inc(S("kappa_sums"), 1)
            clear()

            kP, kQ, kB, kC, kBt, kCt, kV = range(7)
            PAR = ((0, slice(0, 64)), (1, slice(64, P)))
            tps = PS[:, 3:5].rearrange("p a b -> p (a b)")[:, 0:768].rearrange("p (c k n) -> p c k n", c=GC, k=4)
            nps = PS[:, 5, 0:GC * P].rearrange("p (c k n) -> p c k n", c=GC, k=2)
            zps = PS[:, 4, 0:GC * 64].rearrange("p (c n) -> p c n", c=GC)
            wps = PS[:, 3, 0:GC * 64].rearrange("p (c n) -> p c n", c=GC)
            sps = PS[:, 6, 0:256].rearrange("p (a n) -> p a n", a=4)
            yps = PS[:, 7, 0:GC * 64].rearrange("p (c n) -> p c n", c=GC)
            with nc.Block() as block:
                @block.vector
                def _(v):
                    own = Chain(v, dve_own)
                    with v.Fori(0, NG) as i:
                        own.enter(i, 17)
                        grp = lambda t: t[:, :, ds(i * GC * CH, GC * CH)].rearrange("p a (c t) -> p c a t", c=GC)
                        stg = lambda kind: stage[:, :, kind].rearrange("p c (a t) -> p c a t", a=4)

                        def each(kind, a, b):
                            for c in range(GC):
                                ins = nc.vector.tensor_tensor(stg(kind)[:, c], a[:, c], b[:, c], ALU.mult)
                            return ins
                        wc = lambda c: grp(s2[:])[:, c, :, CH - 1:CH]
                        each(kP, grp(kh), grp(s1[:]))
                        each(kQ, grp(r_), grp(s2[:]))
                        each(kB, grp(a_), grp(s3[:]))
                        own(each(kC, grp(k_), grp(s3[:])))
                        for c in range(GC):
                            for src, dst in ((kB, kBt), (kC, kCt)):
                                nc.vector.tensor_tensor(stg(dst)[:, c], stg(src)[:, c],
                                                        wc(c).broadcast_to([P, 4, CH]), ALU.mult)
                            nc.vector.tensor_copy(stg(kV)[:, c], grp(v_)[:, c])
                            last = nc.vector.tensor_tensor(mm[:, c], eye2[:].unsqueeze(1).broadcast_to([P, 4, 64]),
                                                           wc(c).broadcast_to([P, 4, 64]), ALU.mult)
                        own(last)
                        v.sem_inc(S("staged"), 1)
                        v.wait_ge(S("products"), i + 1)
                        own(nc.vector.tensor_tensor(
                            sg[:].rearrange("p c k n -> p c (k n)"), PS[:, 0:GC, 0:320],
                            causal[:].rearrange("p k n -> p (k n)").unsqueeze(1).broadcast_to([P, GC, 320]),
                            ALU.mult))
                        v.sem_inc(S("masked"), 1)
                        own(nc.vector.tensor_tensor(z1[:], sg[:, :, 0], eye2[:].unsqueeze(1).broadcast_to(
                            [P, GC, 64]), ALU.add))
                        v.wait_ge(S("squared"), 3 * i + 1)
                        own(nc.vector.tensor_copy(n2[:], nps))
                        v.sem_inc(S("powers"), 1)
                        v.wait_ge(S("squared"), 3 * i + 2)
                        own(nc.vector.tensor_copy(n4[:], nps))
                        own(nc.vector.tensor_tensor(z2[:], zps, z1[:], ALU.add))
                        v.sem_inc(S("powers"), 1)
                        v.wait_ge(S("squared"), 3 * i + 3)
                        own(nc.vector.tensor_copy(n8[:], nps[:, :, 0]))
                        own(nc.vector.tensor_tensor(z4[:], zps, z2[:], ALU.add))
                        v.sem_inc(S("powers"), 1)
                        v.wait_ge(S("last_factor"), i + 1)
                        own(nc.vector.tensor_tensor(z8[:], zps, z4[:], ALU.add))
                        v.sem_inc(S("inverse"), 1)
                        v.wait_ge(S("transfer"), i + 1)
                        own(nc.vector.tensor_tensor(qp[:], zps, stage[:, :, kQ], ALU.add))
                        for c in range(GC):
                            own(nc.vector.tensor_tensor(
                                mm[:, c], mm[:, c], PS[:, c, 0:256].rearrange("p (a n) -> p a n", a=4), ALU.add))
                        v.sem_inc(S("transfer_out"), 1)
                        for c in range(GC):
                            v.wait_ge(S("stepped"), GC * i + c + 1)
                            if c == 0:
                                v.wait_ge(S("inputs_out"), i + 1)
                            own(nc.vector.tensor_tensor(state[:], sps, nn[:, c], ALU.add))
                            v.sem_inc(S("state"), 1)
                    own.leave(NG)

                @block.scalar
                def _(act):
                    own = Chain(act, act_own)
                    with act.Fori(0, NG) as i:
                        own.enter(i, 3)
                        act.wait_ge(S("turned"), i + 1)
                        nc.scalar.activation(rr[:, :, 0:64], tps[:, :, 0], ACT.Copy)
                        nc.scalar.activation(tk[:, :, 0], tps[:, :, 1], ACT.Copy)
                        nc.scalar.activation(tk[:, :, 1], tps[:, :, 2], ACT.Copy, scale=-1.0)
                        own(nc.scalar.activation(tk[:, :, 2], tps[:, :, 3], ACT.Copy))
                        act.sem_inc(S("rows"), 1)
                        act.wait_ge(S("read_in"), i + 1)
                        nc.scalar.activation(rr[:, :, 64:P], wps, ACT.Copy).then_inc(S("sides"), 1)
                        act.wait_ge(S("solved"), i + 1)
                        own(nc.scalar.activation(xx[:], PS[:, 5, 0:GC * P].rearrange("p (c n) -> p c n", c=GC),
                                                 ACT.Copy))
                        act.sem_inc(S("solution"), 1)
                        act.wait_ge(S("inputs"), i + 1)
                        act.wait_ge(S("transfer_out"), i + 1)
                        own(nc.scalar.activation(nn[:].rearrange("p c a n -> p c (a n)"), PS[:, 0:GC, 256:512],
                                                 ACT.Copy))
                        act.sem_inc(S("inputs_out"), 1)
                        act.wait_ge(S("stepped"), GC * i + GC)
                        for c in range(GC):
                            last = nc.scalar.activation(
                                yb[:, 0:4, ds(i * GC * CH + c * CH, CH)],
                                yps[:, c].rearrange("p (a t) -> p a t", a=4), ACT.Copy)
                        last.then_inc(S("y_out"), 1)
                    own.leave(NG)

                @block.gpsimd
                def _(g):
                    msk = pairmask[:]
                    with g.Fori(0, NG) as i:
                        g.wait_ge(S("rows"), i + 1)
                        for c in range(GC):
                            g.tensor_tensor(bm[:, c], tk[:, c, 1].unsqueeze(1).broadcast_to([P, 4, 64]), msk, ALU.mult)
                            last = g.tensor_tensor(vm[:, c], tk[:, c, 0].unsqueeze(1).broadcast_to([P, 4, 64]), msk,
                                                   ALU.mult)
                        last.then_inc(S("rows_masked"), 1)
                        g.wait_ge(S("solution"), i + 1)
                        for c in range(GC):
                            last = g.tensor_tensor(um[:, c], xx[:, c, 64:P].unsqueeze(1).broadcast_to([P, 4, 64]),
                                                   msk, ALU.mult)
                        last.then_inc(S("solution_masked"), 1)

                @block.tensor
                def _(pe):
                    mmul = nc.tensor.matmul

                    def both(fn):
                        for b, sl in PAR:
                            last = fn(sl)
                        return last
                    pe.sem_inc(S("y_out"), 1)
                    pe.sem_inc(S("state"), 1)
                    with pe.Fori(0, NG) as i:
                        pe.wait_ge(S("staged"), i + 1)
                        pe.sem_inc(S("pe_passed"), 1)
                        for c in range(GC):
                            for lhs, rhs, c0, n in ((kB, slice(kP, kQ + 1), 0, 128), (kC, slice(kP, kQ + 1), 128, 128),
                                                    (kP, slice(kB, kB + 1), 256, 64)):
                                last = both(lambda sl: mmul(
                                    PS[sl, c, c0:c0 + n], stage[sl, c, lhs],
                                    stage[sl, c, rhs].rearrange("p k n -> p (k n)"), start=True, stop=True))
                        last.then_inc(S("products"), 1)
                        for c in range(GC):
                            for k, kind in enumerate((kP, kV, kBt, kCt)):
                                last = both(lambda sl: mmul(tps[sl, c, k], stage[sl, c, kind], eye2[sl],
                                                            start=True, stop=True))
                        last.then_inc(S("turned"), 1)
                        pe.wait_ge(S("masked"), i + 1)
                        pe.sem_inc(S("pe_passed"), 1)
                        for c in range(GC):
                            both(lambda sl: mmul(nps[sl, c, 0], sg[sl, c, 0], sg[sl, c, 4], start=True, stop=True))
                            last = both(lambda sl: mmul(nps[sl, c, 1], sg[sl, c, 4], sg[sl, c, 0],
                                                        start=True, stop=True))
                        last.then_inc(S("squared"), 1)
                        pe.wait_ge(S("rows"), i + 1)
                        pe.sem_inc(S("pe_passed"), 1)
                        for c in range(GC):
                            last = both(lambda sl: mmul(wps[sl, c], sg[sl, c, 2], tk[sl, c, 0], start=True, stop=True))
                        last.then_inc(S("read_in"), 1)
                        pe.wait_ge(S("powers"), 3 * i + 1)
                        pe.sem_inc(S("pe_passed"), 1)
                        for c in range(GC):
                            both(lambda sl: mmul(nps[sl, c, 0], n2[sl, c, 1], n2[sl, c, 0], start=True, stop=True))
                            both(lambda sl: mmul(nps[sl, c, 1], n2[sl, c, 0], n2[sl, c, 1], start=True, stop=True))
                            last = both(lambda sl: mmul(zps[sl, c], n2[sl, c, 0], z1[sl, c], start=True, stop=True))
                        last.then_inc(S("squared"), 1)
                        pe.wait_ge(S("powers"), 3 * i + 2)
                        pe.sem_inc(S("pe_passed"), 1)
                        for c in range(GC):
                            both(lambda sl: mmul(nps[sl, c, 0], n4[sl, c, 1], n4[sl, c, 0], start=True, stop=True))
                            last = both(lambda sl: mmul(zps[sl, c], n4[sl, c, 0], z2[sl, c], start=True, stop=True))
                        last.then_inc(S("squared"), 1)
                        pe.wait_ge(S("powers"), 3 * i + 3)
                        pe.sem_inc(S("pe_passed"), 1)
                        for c in range(GC):
                            last = both(lambda sl: mmul(zps[sl, c], n8[sl, c], z4[sl, c], start=True, stop=True))
                        last.then_inc(S("last_factor"), 1)
                        pe.wait_ge(S("inverse"), i + 1)
                        pe.wait_ge(S("sides"), i + 1)
                        pe.sem_inc(S("pe_passed"), 1)
                        for c in range(GC):
                            last = both(lambda sl: mmul(PS[sl, 5, c * P:(c + 1) * P], z8[sl, c], rr[sl, c],
                                                        start=True, stop=True))
                        last.then_inc(S("solved"), 1)
                        pe.wait_ge(S("solution"), i + 1)
                        pe.wait_ge(S("rows_masked"), i + 1)
                        pe.sem_inc(S("pe_passed"), 1)
                        for c in range(GC):
                            both(lambda sl: mmul(zps[sl, c], xx[sl, c, 0:64], sg[sl, c, 1], start=True, stop=True))
                            last = both(lambda sl: mmul(PS[sl, c, 0:256], xx[sl, c, 0:64],
                                                        bm[sl, c].rearrange("p a n -> p (a n)"), start=True, stop=True))
                        last.then_inc(S("transfer"), 1)
                        pe.wait_ge(S("solution_masked"), i + 1)
                        pe.wait_ge(S("transfer_out"), i + 1)
                        pe.sem_inc(S("pe_passed"), 1)
                        for c in range(GC):
                            both(lambda sl: mmul(PS[sl, c, 256:512], tk[sl, c, 2],
                                                 vm[sl, c].rearrange("p a n -> p (a n)"), start=True, stop=False))
                            last = both(lambda sl: mmul(PS[sl, c, 256:512], tk[sl, c, 1],
                                                        um[sl, c].rearrange("p a n -> p (a n)"),
                                                        start=False, stop=True))
                        last.then_inc(S("inputs"), 1)
                        pe.wait_ge(S("y_out"), i + 1)
                        pe.sem_inc(S("pe_passed"), 1)
                        for c in range(GC):
                            for b, sl in PAR:
                                mmul(yps[sl, c], tk[sl, c, 0], sg[sl, c, 3], start=True, stop=False,
                                     skip_group_check=True)
                                mmul(yps[sl, c], xx[sl, c, 64:P], sg[sl, c, 1], start=False, stop=False,
                                     skip_group_check=True)
                            pe.wait_ge(S("state"), GC * i + c + 1)
                            pe.sem_inc(S("pe_passed"), 1)
                            for a in range(4):
                                both(lambda sl: mmul(yps[sl, c, a * CH:(a + 1) * CH], state[sl, a],
                                                     qp[sl, c, a * CH:(a + 1) * CH], start=False, stop=a == 3,
                                                     skip_group_check=True))
                            for a in range(4):
                                last = both(lambda sl: mmul(sps[sl, a], mm[sl, c, a], state[sl, a],
                                                            start=True, stop=True))
                            last.then_inc(S("stepped"), 1)
            clear()

            with nc.Block() as block:
                y = yb[:, 0:4]

                @block.vector
                def _(v):
                    own = Chain(v, dve_own)
                    v.wait_ge(S("sum_y"), 1)
                    for m in range(4):
                        own(nc.vector.tensor_scalar(halves(s1[:, m]), bank2(m), -1.0 / 64, None, ALU.mult))
                    v.sem_inc(S("sum_y_out"), 1)
                    own(nc.vector.tensor_tensor(y, y, s1[:], ALU.add))
                    v.sem_inc(S("centred"), 1)
                    for m in range(4):
                        own(nc.vector.scalar_tensor_tensor(out=s2[:, m], in0=r_[:, m], scalar=col(G_RK, m),
                                                           in1=k_[:, m], op0=ALU.mult, op1=ALU.mult))
                    v.sem_inc(S("bonus_terms"), 1)
                    v.wait_ge(S("sum_sq"), 1)
                    for m in range(4):
                        own(nc.vector.tensor_scalar(halves(s4[:, m]), bank2(m), 1.0 / 64, GN_EPS, ALU.mult, ALU.add))
                    v.sem_inc(S("sum_sq_out"), 1)
                    own(nc.vector.reciprocal(s4[:], s4[:]))
                    v.sem_inc(S("var_recip"), 1)
                    v.wait_ge(S("var_rsqrt"), 1)
                    own(nc.vector.tensor_tensor(y, y, s4[:], ALU.mult))
                    for m in range(4):
                        own(nc.vector.tensor_scalar(y[:, m], y[:, m], col(G_GG, m), col(G_GB, m), ALU.mult, ALU.add))
                    v.wait_ge(S("sum_bonus"), 1)
                    for m in range(4):
                        own(nc.vector.tensor_tensor(halves(s1[:, m]), bank2(m), halves(v_[:, m]), ALU.mult))
                    v.sem_inc(S("sum_bonus_out"), 1)
                    own(nc.vector.tensor_tensor(y, y, s1[:], ALU.add))
                    v.wait_ge(S("gates"), 1)
                    for m in range(4):
                        own(nc.vector.tensor_tensor(halves(y[:, m]), bank2(m), halves(y[:, m]), ALU.mult))

                @block.scalar
                def _(act):
                    act.wait_ge(S("centred"), 1)
                    nc.scalar.activation(s3[:], y, ACT.Square).then_inc(S("y_squares"), 1)
                    act.wait_ge(S("var_recip"), 1)
                    nc.scalar.activation(s4[:], s4[:], ACT.Sqrt).then_inc(S("var_rsqrt"), 1)

                @block.tensor
                def _(pe):
                    def sums(src, weights, name):
                        for m in range(4):
                            for a in range(2):
                                last = nc.tensor.matmul(PS[:, 2 * m + a, 0:H2], weights(m),
                                                        src(m)[:, a * H2:(a + 1) * H2], start=True, stop=True)
                        last.then_inc(S(name), 1)
                    sums(lambda m: y[:, m], lambda m: half_ones[:], "sum_y")
                    pe.wait_ge(S("y_squares"), 1)
                    sums(lambda m: s3[:, m], lambda m: half_ones[:], "sum_sq")
                    pe.wait_ge(S("bonus_terms"), 1)
                    pe.wait_ge(S("sum_sq_out"), 1)
                    sums(lambda m: s2[:, m], lambda m: half_ones[:], "sum_bonus")
                    pe.wait_ge(S("sum_bonus_out"), 1)
                    sums(lambda m: pj[:, T_G], lambda m: gup[:, m * P:(m + 1) * P], "gates")

        def phase_dsa(pj, tok, yb, l, st):
            H = 8
            Q0, CKV, QI, KI = 0, 4, 5, 9
            qlat = sb(st, "qlat", [P, H, T])
            wuk = sb(st, "wuk", [P, 4, P])
            wuv = sb(st, "wuv", [P, H, 64])
            sq = sb(st, "dsa_sq", [P, T])
            ckv_tok = sb(st, "ckv_tok", [P, 5, P])
            wi = sb(st, "wi", [P, 5, H])
            relu = sb(st, "relu", [P, 2, T])
            score = sb(st, "score", [P, T])
            best = sb(st, "best", [P, 8])
            bias = sb(st, "bias", [P, T])
            lg = sb(st, "lg", [P, 2, T])
            pt = sb(st, "pt", [P, 2, 5, P])
            ot = sb(st, "ot_dsa", [P, H, P])
            stat = sb(st, "stat", [P, 2, 4])
            flat = lambda b: PS[:, b:b + 2].rearrange("p a n -> p (a n)")
            ckv = pj[:, CKV]
            NQ = len(QT)

            def spans(nk):
                return ((0, min(nk, 512)),) + (((512, nk),) if nk > 512 else ())

            with nc.Block() as block:
                @block.sync
                def _(sp):
                    for b in range(2):
                        sp.dma_start(wuk[64 * b:64 * b + 64],
                                     dsa_w_uk[ds(l, 1)].rearrange("o (a b) d c -> b d (o a) c", b=2)[b]
                                     ).then_inc(loaded, 16)
                    sp.dma_start(wuv[:], dsa_w_uv[ds(l, 1)].rearrange("o h c d -> c (o h) d")).then_inc(loaded, 16)

                @block.tensor
                def _(pe):
                    pe.wait_ge(S("ckv_squares"), 1)
                    for a in range(2):
                        last = nc.tensor.matmul(PS[:, a, 0:H2], ones[:], sq[:, a * H2:(a + 1) * H2],
                                                start=True, stop=True)
                    last.then_inc(S("ckv_sum"), 1)
                    pe.wait_ge(loaded, 48)
                    for hd in range(H):
                        b, m = 64 * (hd % 2), hd % 3 + 1
                        if hd >= 3:
                            pe.wait_ge(S("qlat"), hd - 2)
                        for a in range(2):
                            last = nc.tensor.matmul(PS[:, 2 * m + a, 0:H2], wuk[b:b + 64, hd // 2],
                                                    pj[b:b + 64, Q0 + hd // 2, a * H2:(a + 1) * H2],
                                                    start=True, stop=True)
                        last.then_inc(S("qlat_made"), 1)
                    pe.wait_ge(S("ckv"), 1)
                    for j, (t0, n) in enumerate(QT):
                        last = nc.tensor.transpose(PS[0:n, j // 4, (j % 4) * P:(j % 4 + 1) * P],
                                                   pj[:, CKV, t0:t0 + n], ident[:])
                    last.then_inc(S("ckv_turned"), 1)

                @block.scalar
                def _(act):
                    nc.scalar.activation(sq[:], ckv, ACT.Square).then_inc(S("ckv_squares"), 1)
                    act.wait_ge(S("ckv_recip"), 1)
                    nc.scalar.activation(rs[:], rs[:], ACT.Sqrt).then_inc(S("ckv_rsqrt"), 1)
                    for hd in range(H):
                        act.wait_ge(S("qlat_made"), hd + 1)
                        m = hd % 3 + 1
                        nc.scalar.activation(halves(qlat[:, hd]), PS[:, 2 * m:2 * m + 2, 0:H2], ACT.Copy,
                                             scale=0.125).then_inc(S("qlat"), 1)

                @block.vector
                def _(v):
                    own = Chain(v, dve_own)
                    v.wait_ge(S("ckv_sum"), 1)
                    own(nc.vector.tensor_scalar(halves(rs[:]), PS[:, 0:2, 0:H2], 1.0 / P, EPS, ALU.mult, ALU.add))
                    nc.vector.reciprocal(rs[:], rs[:]).then_inc(S("ckv_recip"), 1)
                    v.wait_ge(S("ckv_rsqrt"), 1)
                    nc.vector.scalar_tensor_tensor(out=ckv, in0=ckv, scalar=prm[:, G_KVN:G_KVN + 1], in1=rs[:],
                                                   op0=ALU.mult, op1=ALU.mult).then_inc(S("ckv"), 1)
                    for j, (t0, n) in enumerate(QT):
                        nc.vector.tensor_scalar(wi[0:n, j], tok[0:n, j, 0:H], 512.0 ** -0.5, None, ALU.mult)
                    v.wait_ge(S("ckv_turned"), 1)
                    for j, (t0, n) in enumerate(QT):
                        nc.vector.tensor_copy(ckv_tok[0:n, j], PS[0:n, j // 4, (j % 4) * P:(j % 4 + 1) * P])
            clear()

            with nc.Block() as block:
                @block.tensor
                def _(pe):
                    for j, (t0, n) in enumerate(QT):
                        nk = t0 + n
                        for hd in range(H if j else 0):
                            s, b, q = (j - 1) * H + hd, 64 * (hd % 2), hd % 2
                            if s >= 2:
                                pe.wait_ge(S("relu"), s - 1)
                            if hd < 2 and j > 1:
                                pe.wait_ge(S("logits_out"), (j - 1) * H + H)
                            elif hd < 2:
                                pe.wait_ge(S("logits_out"), H)
                            for k0, k1 in spans(nk):
                                last = nc.tensor.matmul(flat(2 * q)[0:n, k0:k1], pj[b:b + 64, QI + hd // 2, t0:t0 + n],
                                                        pj[b:b + 64, KI, k0:k1], start=True, stop=True)
                            last.then_inc(S("index"), 1)

                        def logits(hd):
                            e, q = j * H + hd, hd % 2
                            if j and hd < 2:
                                pe.wait_ge(S("relu"), j * H)
                            if e >= 2:
                                pe.wait_ge(S("logits_out"), e - 1)
                            for k0, k1 in spans(nk):
                                last = nc.tensor.matmul(flat(2 * q)[0:n, k0:k1], qlat[:, hd, t0:t0 + n],
                                                        pj[:, CKV, k0:k1], start=True, stop=True)
                            last.then_inc(S("logits"), 1)

                        def values(hd):
                            e, q = j * H + hd, hd % 2
                            pe.wait_ge(S("probs"), e + 1)
                            if e >= 1:
                                pe.wait_ge(S("probs_turned_out"), e)
                            for m in range(j + 1):
                                k0, kn = QT[m]
                                dst = PS[0:kn, 5, 0:n] if m == 0 else PS[0:kn, 4, (m - 1) * P:(m - 1) * P + n]
                                last = nc.tensor.transpose(dst, lg[0:n, q, k0:k0 + kn], ident[0:n, 0:n])
                            last.then_inc(S("probs_turned"), 1)
                            pe.wait_ge(S("probs_turned_out"), e + 1)
                            if e >= 1:
                                pe.wait_ge(S("value"), e)
                            for m in range(j + 1):
                                k0, kn = QT[m]
                                last = nc.tensor.matmul(PS[:, 6, 0:n], ckv_tok[0:kn, m], pt[0:kn, q, m, 0:n],
                                                        start=m == 0, stop=m == j)
                            last.then_inc(S("value_made"), 1)

                        logits(0)
                        for hd in range(H):
                            if hd + 1 < H:
                                logits(hd + 1)
                            values(hd)
                        pe.wait_ge(S("value"), (j + 1) * H)
                        if j:
                            pe.wait_ge(S("y"), j)
                        for hd in range(H):
                            b = 64 * (hd % 2)
                            last = nc.tensor.matmul(PS[b:b + 64, 7, (hd // 2) * P:(hd // 2) * P + n], wuv[:, hd],
                                                    ot[:, hd, 0:n], start=True, stop=True)
                        last.then_inc(S("y_made"), 1)

                @block.scalar
                def _(act):
                    for j, (t0, n) in enumerate(QT):
                        nk = t0 + n
                        for hd in range(H if j else 0):
                            s, q = (j - 1) * H + hd, hd % 2
                            act.wait_ge(S("index"), s + 1)
                            if s >= 2:
                                act.wait_ge(S("scored"), s - 1)
                            nc.scalar.activation(relu[0:n, q, 0:nk], flat(2 * q)[0:n, 0:nk], ACT.Relu
                                                 ).then_inc(S("relu"), 1)
                        for hd in range(H):
                            e, q = j * H + hd, hd % 2
                            act.wait_ge(S("max"), e + 1)
                            nc.scalar.activation(lg[0:n, q, 0:nk], lg[0:n, q, 0:nk], ACT.Exp,
                                                 bias=stat[0:n, q, 1:2], accum_out=stat[0:n, q, 2:3]
                                                 ).then_inc(S("exp"), 1)
                            act.wait_ge(S("probs_turned"), e + 1)
                            if e >= 2:
                                act.wait_ge(S("value_made"), e - 1)
                            if j:
                                nc.scalar.activation(pt[:, q, 1:j + 1, 0:n], PS[:, 4, 0:j * P].rearrange(
                                    "p (m n) -> p m n", n=P)[:, :, 0:n], ACT.Copy)
                            nc.scalar.activation(pt[0:N_META, q, 0, 0:n], PS[0:N_META, 5, 0:n], ACT.Copy
                                                 ).then_inc(S("probs_turned_out"), 1)
                            act.wait_ge(S("value_made"), e + 1)
                            if j and hd == 0:
                                act.wait_ge(S("y_made"), j)
                            nc.scalar.activation(ot[:, hd, 0:n], PS[:, 6, 0:n], ACT.Copy).then_inc(S("value"), 1)

                @block.vector
                def _(v):
                    own = Chain(v, dve_own)
                    for j, (t0, n) in enumerate(QT):
                        nk = t0 + n
                        for hd in range(H if j else 0):
                            s, q = (j - 1) * H + hd, hd % 2
                            v.wait_ge(S("relu"), s + 1)
                            if hd == 0:
                                own(nc.vector.tensor_scalar(score[0:n, 0:nk], relu[0:n, q, 0:nk], wi[0:n, j, hd:hd + 1],
                                                            None, ALU.mult))
                            else:
                                own(nc.vector.scalar_tensor_tensor(
                                    out=score[0:n, 0:nk], in0=relu[0:n, q, 0:nk], scalar=wi[0:n, j, hd:hd + 1],
                                    in1=score[0:n, 0:nk], op0=ALU.mult, op1=ALU.add))
                            v.sem_inc(S("scored"), 1)
                        if j:
                            own(nc.vector.memset(score[0:64, nk - 64:nk], FILL))
                            for _ in range(TOPK // 8):
                                own(nc.vector.max(best[0:n], score[0:n, 0:nk]))
                                own(nc.vector.match_replace(score[0:n, 0:nk], best[0:n], score[0:n, 0:nk], TAKEN))
                            own(nc.vector.tensor_scalar(bias[0:n, 0:nk], score[0:n, 0:nk], TAKEN, NEG,
                                                        ALU.not_equal, ALU.mult))
                            own(nc.vector.memset(bias[0:64, nk - 64:nk], NEG))
                        else:
                            own(nc.vector.memset(bias[:, 0:nk], 0.0))
                        for hd in range(H):
                            e, q = j * H + hd, hd % 2
                            v.wait_ge(S("logits"), e + 1)
                            if e >= 2:
                                v.wait_ge(S("probs_turned"), e - 1)
                            own(nc.vector.tensor_tensor_reduce(
                                out=lg[0:n, q, 0:nk], in0=flat(2 * q)[0:n, 0:nk], in1=bias[0:n, 0:nk], scale=1.0,
                                scalar=TAKEN, op0=ALU.add, op1=ALU.max, accum_out=stat[0:n, q, 0:1]))
                            v.sem_inc(S("logits_out"), 1)
                            own(nc.vector.tensor_scalar(stat[0:n, q, 1:2], stat[0:n, q, 0:1], -1.0, None, ALU.mult))
                            v.sem_inc(S("max"), 1)
                            v.wait_ge(S("exp"), e + 1)
                            own(nc.vector.reciprocal(stat[0:n, q, 3:4], stat[0:n, q, 2:3]))
                            own(nc.vector.tensor_scalar(lg[0:n, q, 0:nk], lg[0:n, q, 0:nk], stat[0:n, q, 3:4], None,
                                                        ALU.mult))
                            v.sem_inc(S("probs"), 1)
                        v.wait_ge(S("y_made"), j + 1)
                        nc.vector.tensor_copy(yb[:, 8:12, t0:t0 + n], PS[:, 7].rearrange(
                            "p (a n) -> p a n", n=P)[:, :, 0:n]).then_inc(S("y"), 1)

        def phase_mlstm(pj, tok, yb, l, st):
            H = 4
            MQ, MK, MV, MO = 0, 4, 8, 12
            NS = len(ST_)
            cv = sb(st, "cv", [P, 8, T])
            vt = sb(st, "vt", [P, NS, BW])
            gi, gf, bsum, msum, tmp4, one4, zer4 = (sb(st, n, [4, T]) for n in (
                "gi", "gf", "bsum", "msum", "tmp4", "one4", "zer4"))
            ibf = sb(st, "ibf", [4, 2])
            at = sb(st, "at", [P, NS, 4])
            nmb = sb(st, "nmb", [P, 2, T])
            dd = sb(st, "dd", [P, 2, T])
            ss = sb(st, "ss", [P, 2, T])
            den = sb(st, "den", [P, T])
            hq = sb(st, "hq", [P, 4, T])
            flat = lambda b: PS[:, b:b + 2].rearrange("p a n -> p (a n)")
            hy = yb[:, 4:8]

            def spans(j0):
                return ((j0, 512), (512, T)) if j0 < 512 else ((512, T),)

            with nc.Block() as block:
                @block.sync
                def _(sp):
                    for c, src in enumerate((ml_i_bias, ml_f_bias)):
                        sp.dma_start(ibf[:, c:c + 1], src[ds(l, 1)].rearrange("a h -> h a")).then_inc(loaded, 16)

                @block.tensor
                def _(pe):
                    for g in range(2):
                        for j, (t0, n) in enumerate(QT):
                            b, c = (1, 0) if j == 4 else (0, t0)
                            last = nc.tensor.transpose(PS[0:4, 2 * g + b, c:c + n], tok[0:n, j, 8 + 4 * g:12 + 4 * g],
                                                       ident[0:n, 0:n])
                    last.then_inc(S("gates_turned"), 1)
                    for j, (t0, n) in enumerate(ST_):
                        if j >= 2:
                            pe.wait_ge(S("v_out"), j - 1)
                        for m in range(4):
                            last = nc.tensor.transpose(PS[0:n, 4 + j % 2, m * P:(m + 1) * P],
                                                       pj[:, MV + m, t0:t0 + n], ident[:])
                        last.then_inc(S("v_turned"), 1)
                    pe.wait_ge(S("a"), 1)
                    for j, (t0, n) in enumerate(ST_):
                        last = nc.tensor.transpose(PS[0:n, 6, 4 * j:4 * j + 4], tmp4[:, t0:t0 + n], ident[0:4, 0:4])
                    last.then_inc(S("a_turned"), 1)

                @block.vector
                def _(v):
                    own = Chain(v, dve_own)
                    v.wait_ge(loaded, 32)
                    v.wait_ge(S("gates_turned"), 1)
                    for g, dst in ((0, gi), (1, gf)):
                        for c0, c1, b in ((0, 400, 0), (400, T, 1)):
                            last = nc.vector.tensor_scalar(dst[:, c0:c1], PS[0:4, 2 * g + b, 0:c1 - c0],
                                                           ibf[:, g:g + 1], None, ALU.add)
                    own(last)
                    v.sem_inc(S("gates_in"), 1)
                    nc.vector.memset(one4[:], 1.0)
                    nc.vector.memset(zer4[:], 0.0)
                    own(nc.vector.tensor_scalar(cv[:, 0], pj[:, 0], prm[:, G_CONVW + 24:G_CONVW + 25],
                                                prm[:, G_CONVB:G_CONVB + 1], ALU.mult, ALU.add))
                    for m in range(8):
                        if m:
                            own(nc.vector.tensor_scalar(cv[:, m], pj[:, m], prm[:, G_CONVW + 24 + m:G_CONVW + 25 + m],
                                                        prm[:, G_CONVB + m:G_CONVB + m + 1], ALU.mult, ALU.add))
                        for back in (1, 2, 3):
                            c = G_CONVW + 8 * (3 - back) + m
                            own(nc.vector.scalar_tensor_tensor(
                                out=cv[:, m, back:T], in0=pj[:, m, 0:T - back], scalar=prm[:, c:c + 1],
                                in1=cv[:, m, back:T], op0=ALU.mult, op1=ALU.add))
                        v.sem_inc(S("convolved"), 1)
                    v.wait_ge(S("softplus"), 1)
                    own(nc.vector.tensor_scalar(gf[:], gf[:], 0.0, None, ALU.min))
                    own(nc.vector.tensor_tensor(gf[:], gf[:], msum[:], ALU.subtract))
                    own(nc.vector.tensor_tensor_scan(bsum[:], one4[:], gf[:], 0.0, ALU.mult, ALU.add))
                    own(nc.vector.tensor_tensor(tmp4[:], gi[:], bsum[:], ALU.subtract))
                    v.sem_inc(S("a"), 1)
                    own(nc.vector.tensor_tensor_scan(msum[:], tmp4[:], tmp4[:], 0.0, ALU.max, ALU.max))
                    own(nc.vector.tensor_tensor(bsum[:], bsum[:], msum[:], ALU.add))
                    own(nc.vector.tensor_scalar(bsum[:], bsum[:], -1.0, 85.0, ALU.mult, ALU.min))
                    own(nc.vector.tensor_scalar(msum[:], msum[:], -1.0, None, ALU.mult))
                    v.sem_inc(S("m"), 1)
                    v.wait_ge(S("a_turned"), 1)
                    for j, (t0, n) in enumerate(ST_):
                        last = nc.vector.tensor_copy(at[0:n, j], PS[0:n, 6, 4 * j:4 * j + 4])
                    own(last)

                @block.scalar
                def _(act):
                    own = Chain(act, act_own)
                    act.wait_ge(S("gates_in"), 1)
                    own(nc.scalar.activation(msum[:], gf[:], ACT.Abs))
                    own(nc.scalar.activation(msum[:], msum[:], ACT.Exp, scale=-1.0))
                    own(nc.scalar.activation(msum[:], msum[:], ACT.Ln, bias=1.0))
                    act.sem_inc(S("softplus"), 1)
                    for j, (t0, n) in enumerate(ST_):
                        act.wait_ge(S("v_turned"), j + 1)
                        nc.scalar.activation(vt[0:n, j], PS[0:n, 4 + j % 2, :], ACT.Copy).then_inc(S("v_out"), 1)
                    for m in range(8):
                        act.wait_ge(S("convolved"), m + 1)
                        nc.scalar.activation(cv[:, m], cv[:, m], ACT.Silu)
                    nc.scalar.activation(pj[:, MO:MO + 4], pj[:, MO:MO + 4], ACT.Sigmoid)
                    act.wait_ge(S("m"), 1)
                    nc.scalar.activation(bsum[:], bsum[:], ACT.Exp).then_inc(act_own, 1)
            clear()

            with nc.Block() as block:
                @block.tensor
                def _(pe):
                    def spread(hd):
                        if hd:
                            pe.wait_ge(S("weighed"), NS * hd)
                        for a in range(2):
                            last = nc.tensor.matmul(PS[:, a, 0:H2], sel[0:4, hd], msum[:, a * H2:(a + 1) * H2],
                                                    start=True, stop=True)
                        last.then_inc(S("spread"), 1)

                    for hd in range(H):
                        spread(hd)
                        pe.wait_ge(S("spread_out"), hd + 1)

                        def scores(i):
                            e = hd * NS + i
                            s0, n = ST_[i]
                            if i >= 2:
                                pe.wait_ge(S("weighed"), e - 1)
                            for j0, j1 in spans(s0):
                                last = nc.tensor.matmul(flat(2 * (i % 2))[0:n, j0:j1], cv[:, MK + hd, s0:s0 + n],
                                                        cv[:, MQ + hd, j0:j1], start=True, stop=True)
                            last.then_inc(S("scores"), 1)

                        scores(0)
                        for i in range(NS):
                            if i + 1 < NS:
                                scores(i + 1)
                            e = hd * NS + i
                            s0, n = ST_[i]
                            pe.wait_ge(S("weighed"), e + 1)
                            if i == 0 and hd:
                                pe.wait_ge(S("head_out"), hd)
                            for bank, lhs in ((4, vt[0:n, i, hd * P:(hd + 1) * P]), (6, ones[0:n])):
                                for j0, j1 in spans(s0):
                                    last = nc.tensor.matmul(
                                        flat(bank)[:, j0:j1], lhs, ss[0:n, i % 2, j0:j1], start=i == 0,
                                        stop=i == (NS - 1 if j0 == 512 else NS - 2), skip_group_check=True)
                            last.then_inc(S("summed"), 1)
                        pe.wait_ge(S("weighed"), NS * (hd + 1))
                        for a in range(2):
                            last = nc.tensor.matmul(PS[:, a, 0:H2], sel[0:4, hd], bsum[:, a * H2:(a + 1) * H2],
                                                    start=True, stop=True)
                        last.then_inc(S("floor"), 1)
                        pe.wait_ge(S("head_out"), hd + 1)
                    pe.wait_ge(S("h_squares"), 1)
                    for m in range(4):
                        for a in range(2):
                            last = nc.tensor.matmul(PS[:, 2 * m + a, 0:H2], ones[:], hq[:, m, a * H2:(a + 1) * H2],
                                                    start=True, stop=True)
                    last.then_inc(S("h_sums"), 1)

                @block.vector
                def _(v):
                    own = Chain(v, dve_own)
                    for hd in range(H):
                        v.wait_ge(S("spread_out"), hd + 1)

                        def decay(i):
                            s0, n = ST_[i]
                            if hd * NS + i >= 2:
                                v.wait_ge(S("weighed"), hd * NS + i - 1)
                            nc.vector.tensor_scalar(dd[0:n, i % 2, s0:T], nmb[0:n, hd % 2, s0:T],
                                                    at[0:n, i, hd:hd + 1], 0.0, ALU.add, ALU.min
                                                    ).then_inc(S("decay_log"), 1)
                        decay(0)
                        for i in range(NS):
                            if i + 1 < NS:
                                decay(i + 1)
                            e = hd * NS + i
                            s0, n = ST_[i]
                            v.wait_ge(S("decay"), e + 1)
                            v.wait_ge(S("scores"), e + 1)
                            if e >= 2:
                                v.wait_ge(S("summed"), e - 1)
                            nc.vector.scalar_tensor_tensor(
                                out=ss[0:n, i % 2, s0:T], in0=flat(2 * (i % 2))[0:n, s0:T], scalar=P ** -0.5,
                                in1=dd[0:n, i % 2, s0:T], op0=ALU.mult, op1=ALU.mult).then_inc(S("weighed"), 1)
                        v.wait_ge(S("floor"), hd + 1)
                        v.wait_ge(S("den"), hd + 1)
                        own(nc.vector.tensor_tensor(halves(den[:]), PS[:, 0:2, 0:H2], halves(den[:]), ALU.max))
                        own(nc.vector.reciprocal(den[:], den[:]))
                        own(nc.vector.tensor_tensor(hy[:, hd], flat(4)[:, 0:T], den[:], ALU.mult))
                        v.sem_inc(S("head_out"), 1)
                    v.wait_ge(S("h_sums"), 1)
                    for m in range(4):
                        last = nc.vector.tensor_scalar(halves(hq[:, m]), PS[:, 2 * m:2 * m + 2, 0:H2], 1.0 / P, EPS,
                                                       ALU.mult, ALU.add)
                    own(last)
                    own(nc.vector.reciprocal(hq[:], hq[:]))
                    v.sem_inc(S("h_recip"), 1)
                    v.wait_ge(S("h_rsqrt"), 1)
                    own(nc.vector.tensor_tensor(hy, hy, hq[:], ALU.mult))
                    for m in range(4):
                        nc.vector.scalar_tensor_tensor(
                            out=hy[:, m], in0=hy[:, m], scalar=prm[:, G_MLN + m:G_MLN + m + 1], in1=pj[:, MO + m],
                            op0=ALU.mult, op1=ALU.mult)

                @block.scalar
                def _(act):
                    for hd in range(H):
                        act.wait_ge(S("spread"), hd + 1)
                        nc.scalar.activation(halves(nmb[:, hd % 2]), PS[:, 0:2, 0:H2], ACT.Copy
                                             ).then_inc(S("spread_out"), 1)
                        for i in range(NS):
                            e = hd * NS + i
                            s0, n = ST_[i]
                            act.wait_ge(S("decay_log"), e + 1)
                            nc.scalar.activation(dd[0:n, i % 2, s0:T], dd[0:n, i % 2, s0:T], ACT.Exp
                                                 ).then_inc(S("decay_exp"), 1)
                        act.wait_ge(S("summed"), NS * (hd + 1))
                        if hd:
                            act.wait_ge(S("head_out"), hd)
                        nc.scalar.activation(den[:], flat(6)[:, 0:T], ACT.Abs).then_inc(S("den"), 1)
                    act.wait_ge(S("head_out"), H)
                    nc.scalar.activation(hq[:], hy, ACT.Square).then_inc(S("h_squares"), 1)
                    act.wait_ge(S("h_recip"), 1)
                    nc.scalar.activation(hq[:], hq[:], ACT.Sqrt).then_inc(S("h_rsqrt"), 1)

                @block.gpsimd
                def _(g):
                    for e in range(H * NS):
                        s0, n = ST_[e % NS]
                        g.wait_ge(S("decay_exp"), e + 1)
                        d = dd[0:n, (e % NS) % 2, s0:s0 + n]
                        g.affine_select(out=d, in_=d, compare_op=ALU.is_ge, fill=0.0, base=0, pattern=[[1, n]],
                                        channel_multiplier=-1).then_inc(S("decay"), 1)

        def run(phase, *args):
            with ExitStack() as st:
                phase(*args, st) if phase in with_stack_last else phase(st, *args)
            clear()

        with_stack_last = (phase_ffn, phase_merge)

        run(phase_start)
        with nc.Fori(0, DEPTH) as l:
            run(phase_params, l)

            def ffn(which):
                run(phase_norm, h, G_NORM + KD * 4 * which, 1.0, "u")
                with ExitStack() as st:
                    hid = sb(st, "hid", [P, KF, T])
                    fo = sb(st, "fo", [P, KD, T])
                    with ExitStack() as st2:
                        phase_ffn(hid, fo, l, which, st2)
                    clear()
                    run(phase_norm, fo, G_NORM + KD * (4 * which + 1), 0.5, "h")

            ffn(0)
            run(phase_norm, h, G_NORM + 2 * KD, 1.0, "u")
            with ExitStack() as outer:
                yb = sb(outer, "yb", [P, 12, T])
                if len(BR) < 3:
                    with nc.Block() as block:
                        @block.vector
                        def _(v):
                            nc.vector.memset(yb[:], 1.0)
                with ExitStack() as st:
                    pj = sb(st, "pj", [P, 16, T])
                    tok = sb(st, "tok", [P, 5, 16])
                    for name, branch, c0, n, small_too in (
                            ("rw", phase_rwkv, 0, 14, False), ("dsa", phase_dsa, C_DSA, 9, True),
                            ("ml", phase_mlstm, RW_COLS, 16, False)):
                        if name not in BR:
                            continue
                        phase_proj(pj, tok, l, c0, n, small_too)
                        clear()
                        with ExitStack() as st2:
                            branch(pj, tok, yb, l, st2)
                        clear()
                if debug is not None:
                    debug(nc, "yb", yb, l)
                mixed = sb(outer, "mixed", [P, KD, T])
                fo = sb(outer, "fo2", [P, KD, T])
                with ExitStack() as st:
                    phase_merge(yb, mixed, l, st)
                clear()
                phase_out(mixed, fo, l)
                clear()
                run(phase_norm, fo, G_NORM + 3 * KD, 1.0, "h")
            ffn(1)
        run(phase_end)


_INS = ["x", "meta_tokens", "norm_gain", "ffn_w_in", "ffn_w_out", "w_in", "rw_mu", "rw_w0", "rw_w_up", "rw_a0",
        "rw_a_up", "rw_g_up", "rw_k_k", "rw_k_a", "rw_r_k", "rw_gn_gain", "rw_gn_bias", "ml_conv_w", "ml_conv_b",
        "ml_i_bias", "ml_f_bias", "ml_norm_gain", "dsa_kv_norm", "dsa_w_uk", "dsa_w_uv", "w_branch", "w_out"]


def kernel(**inputs):
    import concourse.bacc as bacc
    from concourse.bass_utils import run_bass_kernel_spmd

    nc = bacc.Bacc("TRN2", target_bir_lowering=False, num_devices=1)
    arrays, args = {}, []
    for name in _INS:
        a = np.ascontiguousarray(inputs[name])
        arrays[f"in_{name}"] = a
        args.append(nc.dram_tensor(f"in_{name}", a.shape, mybir.dt.from_np(a.dtype), kind="ExternalInput").ap())
    args.append(nc.dram_tensor("out_0", (1, SEQ, D_MODEL), F32, kind="ExternalOutput").ap())
    build_program(nc, *args)
    r = run_bass_kernel_spmd(nc, [arrays], core_ids=[0])
    return r.results[0]["out_0"]
```

```python
import math
from contextlib import ExitStack

import numpy as np

import concourse.bass as bass
from concourse import mybir

F32 = mybir.dt.float32
F32R = mybir.dt.float32r
ALU = mybir.AluOpType
ACT = mybir.ActivationFunctionType
AX = mybir.AxisListType.X
ds = bass.ds

P = 128
D_MODEL, SEQ, N_META, DEPTH, D_FF = 1024, 512, 16, 2, 2816
T = SEQ + N_META
H2 = T // 2
KD = D_MODEL // P
KF = D_FF // P
BW = 512
RW_COLS, ML_COLS = 1792, 2056
C_IG = RW_COLS + 2048
C_DSA = RW_COLS + ML_COLS
C_KIDX = C_DSA + BW + P + 512
C_GATE = C_KIDX + 64 + 8
N_IN = C_GATE + 3 * D_MODEL
EPS = 1e-6
GN_EPS = 64e-5
CH = 16
GC = 3
NG = T // (CH * GC)
TOPK = 128
FILL, TAKEN, NEG = -3.0e38, -3.3e38, -1.0e30
DECAY = -math.exp(-0.5)

G_NORM, G_CONVW, G_CONVB, G_MU, G_W0, G_A0, G_KK, G_KA, G_RK, G_GG, G_GB, G_MLN, G_KVN = (
    0, 48, 80, 88, 102, 106, 110, 114, 118, 122, 126, 130, 134)
G_END = 135

T_R, T_K, T_V, T_WA, T_G = 0, 4, 8, 12, 13
T_MQ, T_MK, T_MV, T_MO = 14, 18, 22, 26
T_DQ, T_CKV, T_QI = 30, 34, 35
NPROJ = 39

QT = [(0, N_META)] + [(N_META + P * j, P) for j in range(SEQ // P)]
ST_ = [(s, min(P, T - s)) for s in range(0, T, P)]


BR = ("rw", "dsa", "ml")


class Chain:

    def __init__(self, eng, s):
        self.eng, self.s, self.n, self.base = eng, s, 0, 0

    def __call__(self, ins):
        self.n += 1
        ins.then_inc(self.s, 1)
        self.eng.wait_ge(self.s, self.base + self.n)

    def enter(self, i, per):
        self.start, self.per = self.n, per
        self.base = i * per

    def leave(self, count):
        assert self.n - self.start == self.per, (self.n - self.start, self.per)
        self.n = self.start + count * self.per
        self.base = 0


def build_program(nc, x, meta_tokens, norm_gain, ffn_w_in, ffn_w_out, w_in, rw_mu, rw_w0, rw_w_up,
                  rw_a0, rw_a_up, rw_g_up, rw_k_k, rw_k_a, rw_r_k, rw_gn_gain, rw_gn_bias, ml_conv_w,
                  ml_conv_b, ml_i_bias, ml_f_bias, ml_norm_gain, dsa_kv_norm, dsa_w_uk, dsa_w_uv,
                  w_branch, w_out, out, debug=None):
    ctx = ExitStack()
    with ctx:
        sems, names, named = [], {}, {}

        def sem(name):
            s = ctx.enter_context(nc.semaphore(name))
            sems.append(s)
            return s

        def S(name):
            if name not in named:
                named[name] = sem(name)
            return named[name]

        def sb(stack, name, shape, dt=F32):
            names[name] = names.get(name, 0) + 1
            return stack.enter_context(nc.sbuf_tensor(f"{name}_{names[name]}", shape, dt))

        PS = ctx.enter_context(nc.psum_tensor("PS", [P, 8, 512], F32))
        h = sb(ctx, "h", [P, KD, T])
        uh = sb(ctx, "u_high", [P, KD, T], F32R)
        ul = sb(ctx, "u_low", [P, KD, T], F32R)
        ident = sb(ctx, "ident", [P, P])
        ones = sb(ctx, "ones", [P, P])
        half_ones = sb(ctx, "half_ones", [P, P])
        causal = sb(ctx, "causal", [P, 5, 64])
        pairmask = sb(ctx, "pairmask", [P, 4, 64])
        eye2 = sb(ctx, "eye2", [P, 64])
        sel = sb(ctx, "sel", [P, 4, P])
        prm = sb(ctx, "prm", [P, G_END])
        rs = sb(ctx, "rs", [P, T])

        dve_own, act_own, pool_own, pe_own = sem("dve_own"), sem("act_own"), sem("pool_own"), sem("pe_own")
        landed = [sem(f"weights_landed{i}") for i in range(4)]
        tile_done = sem("tile_done")
        act_evac, dve_evac = sem("act_evac"), sem("dve_evac")
        loaded, loaded2, stored = sem("loaded"), sem("loaded2"), sem("stored")
        ev = {n: sem(n) for n in (
            "pe_to_act", "pe_to_dve", "act_to_pe", "act_to_dve", "dve_to_pe", "dve_to_act",
            "pool_to_dve", "pool_to_pe", "dve_to_pool", "act_to_pool", "pool_to_act")}

        def weight_buffers(st, units):
            return (sb(st, "W", [P, 2, units, P]), sb(st, "W_high", [P, 2, units, P], F32R),
                    sb(st, "W_low", [P, 2, units, P], F32R))

        def exact(dst, wh, wl, xh, xl, first, final):
            nc.tensor.matmul(dst, wh, xh, start=first, stop=False)
            nc.tensor.matmul(dst, wh, xl, start=False, stop=False)
            return nc.tensor.matmul(dst, wl, xh, start=False, stop=final)

        def high_part(act, n, land, W, WH, w, k):
            act.wait_ge(landed[w], land)
            act.wait_ge(tile_done, n + 1)
            act.sem_inc(S("act_passed"), 1)
            nc.scalar.activation(WH[:, w, 0:k], W[:, w, 0:k], ACT.Copy).then_inc(S("high"), 1)

        def low_part(g, n, W, WH, WL, w, k):
            g.wait_ge(S("high"), n + 1)
            g.sem_inc(S("pool_passed"), 1)
            g.tensor_tensor(WL[:, w, 0:k], W[:, w, 0:k], WH[:, w, 0:k].bitcast(F32), ALU.subtract
                            ).then_inc(S("split"), 1)

        def clear():
            with nc.Block() as block:
                @block.sync
                def _(sp):
                    for s in sems:
                        sp.sem_clear(s)

        def halves(ap):
            return ap.rearrange("p (a n) -> p a n", a=2)

        def phase_start(st):
            xt = sb(st, "xt", [P, 5, D_MODEL])
            with nc.Block() as block:
                @block.sync
                def _(sp):
                    sp.dma_start(xt[0:N_META, 0, :], meta_tokens).then_inc(loaded, 16)
                    for j in range(4):
                        sp.dma_start(xt[:, 1 + j, :], x[0, j * P:(j + 1) * P, :]).then_inc(loaded, 16)

                @block.gpsimd
                def _(g):
                    own = Chain(g, pool_own)
                    own(g.memset(ident[:], 0.0))
                    own(g.affine_select(out=ident[:], in_=ident[:], compare_op=ALU.not_equal, fill=1.0,
                                        base=0, pattern=[[-1, P]], channel_multiplier=1))
                    g.memset(ones[:], 1.0)
                    own(g.memset(half_ones[:], 0.0))
                    for b in (0, 64):
                        own(g.memset(half_ones[b:b + 64, b:b + 64], 1.0))
                        own(g.tensor_copy(eye2[b:b + 64, :], ident[b:b + 64, b:b + 64]))
                    own(g.memset(pairmask[:], 1.0))
                    for b in (0, 64):
                        v = pairmask[b:b + 64]
                        own(g.affine_select(out=v, in_=v, compare_op=ALU.is_ge, fill=0.0, base=0,
                                            pattern=[[-16, 4], [0, 64]], channel_multiplier=1))
                        own(g.affine_select(out=v, in_=v, compare_op=ALU.is_ge, fill=0.0, base=15,
                                            pattern=[[16, 4], [0, 64]], channel_multiplier=-1))
                    own(g.memset(sel[:], 0.0))
                    own(g.affine_select(out=sel[:], in_=sel[:], compare_op=ALU.not_equal, fill=1.0, base=0,
                                        pattern=[[-1, 4], [0, P]], channel_multiplier=1))
                    for kind, (value, step, base) in enumerate(
                            ((-1.0, 1, -1), (-1.0, 1, 0), (1.0, 1, -1), (1.0, 1, 0), (-1.0, -1, -1))):
                        own(g.memset(causal[:, kind, :], value))
                        for b in (0, 64):
                            v = causal[b:b + 64, kind, :]
                            own(g.affine_select(out=v, in_=v, compare_op=ALU.is_ge, fill=0.0, base=base,
                                                pattern=[[step, 64]], channel_multiplier=-step))
                            vv = v.rearrange("p (a b) -> p a b", a=4)
                            own(g.tensor_tensor(vv, vv, pairmask[b:b + 64, :, 0:16], ALU.mult))
                    g.drain().then_inc(ev["pool_to_pe"], 1)

                @block.tensor
                def _(pe):
                    pe.wait_ge(ev["pool_to_pe"], 1)
                    pe.wait_ge(loaded, 80)
                    for f in range(KD):
                        if f >= 4:
                            pe.wait_ge(ev["dve_to_pe"], f - 3)
                        b = 2 * (f % 4)
                        for j, (t0, n) in enumerate(QT):
                            last = nc.tensor.transpose(PS[:, b, t0:t0 + n] if t0 + n <= 400 else
                                                       PS[:, b + 1, t0 - 400:t0 - 400 + n],
                                                       xt[0:n, j, f * P:(f + 1) * P], ident[0:n, 0:n])
                        last.then_inc(ev["pe_to_dve"], 1)

                @block.vector
                def _(v):
                    for f in range(KD):
                        v.wait_ge(ev["pe_to_dve"], f + 1)
                        b = 2 * (f % 4)
                        nc.vector.tensor_copy(h[:, f, 0:400], PS[:, b, 0:400])
                        nc.vector.tensor_copy(h[:, f, 400:T], PS[:, b + 1, 0:T - 400]).then_inc(ev["dve_to_pe"], 1)

        def phase_params(st, l):
            pa = sb(st, "pa", [P, P])
            pb = sb(st, "pb", [P, P])

            def rows(src, n):
                return src.rearrange("a n -> (a n)").rearrange("(k p) -> k p", p=P)

            with nc.Block() as block:
                @block.sync
                def _(sp):
                    sp.dma_start(pa[0:48, :], norm_gain[ds(l, 1)].rearrange("a g (k p) -> (a g k) p", p=P)
                                 ).then_inc(loaded, 16)
                    sp.dma_start(pa[48:80, :], ml_conv_w[ds(l, 1)].rearrange("a g (k p) -> (a g k) p", p=P)
                                 ).then_inc(loaded, 16)
                    sp.dma_start(pa[80:88, :], ml_conv_b[ds(l, 1)].rearrange("a (k p) -> (a k) p", p=P)
                                 ).then_inc(loaded, 16)
                    at = 0
                    for src in (rw_mu, rw_w0, rw_a0, rw_k_k, rw_k_a, None, rw_gn_gain, rw_gn_bias,
                                ml_norm_gain, dsa_kv_norm):
                        if src is None:
                            sp.dma_start(pb[at:at + 4, :], rw_r_k[ds(l, 1)].rearrange(
                                "a (k b) p -> (a k) (b p)", b=2)).then_inc(loaded, 16)
                            at += 4
                            continue
                        n = src.shape[-1] // P
                        sp.dma_start(pb[at:at + n, :], src[ds(l, 1)].rearrange("a (k p) -> (a k) p", p=P)
                                     ).then_inc(loaded, 16)
                        at += n
                    assert at == G_END - G_MU

                @block.tensor
                def _(pe):
                    pe.wait_ge(loaded, 13 * 16)
                    nc.tensor.transpose(PS[:, 0, 0:G_MU], pa[0:G_MU, :], ident[0:G_MU, 0:G_MU])
                    n = G_END - G_MU
                    nc.tensor.transpose(PS[:, 0, G_MU:G_END], pb[0:n, :], ident[0:n, 0:n]
                                        ).then_inc(ev["pe_to_dve"], 1)

                @block.vector
                def _(v):
                    v.wait_ge(ev["pe_to_dve"], 1)
                    nc.vector.tensor_copy(prm[:], PS[:, 0, 0:G_END]).then_inc(dve_own, 1)

        def phase_norm(st, src, gain, scale, into):
            sq = sb(st, "sq", [P, KD, T])
            gs = sb(st, "gs", [P, KD])
            with nc.Block() as block:
                @block.scalar
                def _(act):
                    for k in range(0, KD, 2):
                        nc.scalar.activation(sq[:, k], src[:, k], ACT.Square).then_inc(S("squares"), 1)
                    act.wait_ge(S("recip"), 1)
                    nc.scalar.activation(rs[:], rs[:], ACT.Sqrt).then_inc(S("rsqrt"), 1)
                    if into == "u":
                        for k in range(KD):
                            act.wait_ge(S("scaled"), k + 1)
                            nc.scalar.activation(uh[:, k], sq[:, k], ACT.Copy).then_inc(S("high"), 1)

                @block.tensor
                def _(pe):
                    for k in range(KD):
                        pe.wait_ge(S("squares_odd" if k % 2 else "squares"), k // 2 + 1)
                        for a in range(2):
                            last = nc.tensor.matmul(PS[:, a, 0:H2], ones[:], sq[:, k, a * H2:(a + 1) * H2],
                                                    start=k == 0, stop=k == KD - 1)
                    last.then_inc(S("sum"), 1)

                @block.vector
                def _(v):
                    own = Chain(v, dve_own)
                    for k in range(1, KD, 2):
                        nc.vector.tensor_tensor(sq[:, k], src[:, k], src[:, k], ALU.mult
                                                ).then_inc(S("squares_odd"), 1)
                    own(nc.vector.tensor_scalar(gs[:], prm[:, gain:gain + KD], scale, None, ALU.mult))
                    v.wait_ge(S("sum"), 1)
                    own(nc.vector.tensor_scalar(halves(rs[:]), PS[:, 0:2, 0:H2], 1.0 / D_MODEL, EPS,
                                                ALU.mult, ALU.add))
                    nc.vector.reciprocal(rs[:], rs[:]).then_inc(S("recip"), 1)
                    v.wait_ge(S("rsqrt"), 1)
                    for k in range(KD):
                        nc.vector.scalar_tensor_tensor(out=sq[:, k], in0=src[:, k], scalar=gs[:, k:k + 1],
                                                       in1=rs[:], op0=ALU.mult, op1=ALU.mult
                                                       ).then_inc(S("scaled"), 1)
                        if into == "u" and k % 2:
                            v.wait_ge(S("high"), k)
                            nc.vector.tensor_tensor(ul[:, k - 1], sq[:, k - 1], uh[:, k - 1].bitcast(F32),
                                                    ALU.subtract)
                        elif into == "h" and k % 2:
                            v.wait_ge(S("scaled"), k)
                            nc.vector.tensor_tensor(h[:, k - 1], h[:, k - 1], sq[:, k - 1], ALU.add)

                @block.gpsimd
                def _(g):
                    for k in range(1, KD, 2):
                        if into == "u":
                            g.wait_ge(S("high"), k + 1)
                            g.tensor_tensor(ul[:, k], sq[:, k], uh[:, k].bitcast(F32), ALU.subtract)
                        else:
                            g.wait_ge(S("scaled"), k + 1)
                            g.tensor_tensor(h[:, k], h[:, k], sq[:, k], ALU.add)

        def phase_ffn_in(hh, hl, l, which):
            with ExitStack() as st:
                W, WH, WL = weight_buffers(st, KD)
                sg = sb(st, "sg", [P, 2, T])
                hid = sb(st, "hid", [P, 2, T])
                wi = ffn_w_in[ds(l, 1), which].rearrange("a (k p) n -> p (a k) n", p=P)
                NI = KF // 2
                with nc.Block() as block:
                    @block.sync
                    def _(sp):
                        sp.sem_inc(S("split"), 2)
                        with sp.Fori(0, NI) as i:
                            for s in range(4):
                                c = sp.snap((2 * i + s // 2) * P + (s % 2) * D_FF)
                                sp.wait_ge(S("split"), 4 * i + s + 1)
                                sp.sem_inc(S("asked"), 1)
                                sp.dma_start(W[:, s % 2], wi[:, :, ds(c, P)]).then_inc(landed[s % 2], 16)

                    @block.gpsimd
                    def _(g):
                        with g.Fori(0, NI) as i:
                            for s in range(4):
                                low_part(g, 4 * i + s, W, WH, WL, s % 2, KD)

                    @block.tensor
                    def _(pe):
                        pe.sem_inc(tile_done, 2)
                        pe.sem_inc(act_evac, 2)
                        pe.sem_inc(dve_evac, 2)
                        with pe.Fori(0, NI) as i:
                            for s in range(4):
                                pe.wait_ge(S("split"), 4 * i + s + 3)
                                pe.wait_ge(dve_evac if s % 2 else act_evac, 2 * i + s // 2 + 1)
                                for k in range(KD):
                                    for a in range(2):
                                        half = slice(a * H2, (a + 1) * H2)
                                        last = exact(PS[:, 2 * s + a, 0:H2], WH[:, s % 2, k], WL[:, s % 2, k],
                                                     uh[:, k, half], ul[:, k, half], k == 0, k == KD - 1)
                                last.then_inc(tile_done, 1)

                    @block.scalar
                    def _(act):
                        with act.Fori(0, NI) as i:
                            for s in range(4):
                                high_part(act, 4 * i + s, 32 * i + 16 * (s // 2) + 16, W, WH, s % 2, KD)
                                if s % 2:
                                    j = s // 2
                                    act.wait_ge(tile_done, 4 * i + 2 * j + 3)
                                    act.wait_ge(dve_evac, 2 * i + j + 1)
                                    nc.scalar.activation(halves(sg[:, j]), PS[:, 4 * j:4 * j + 2, 0:H2], ACT.Silu
                                                         ).then_inc(act_evac, 1)

                    @block.vector
                    def _(v):
                        v.sem_inc(S("hidden_low"), 2)
                        with v.Fori(0, NI) as i:
                            for j in range(2):
                                v.wait_ge(tile_done, 4 * i + 2 * j + 4)
                                v.wait_ge(act_evac, 2 * i + j + 3)
                                v.wait_ge(S("hidden_low"), 2 * i + j + 1)
                                nc.vector.tensor_tensor(halves(hid[:, j]), PS[:, 4 * j + 2:4 * j + 4, 0:H2],
                                                        halves(sg[:, j]), ALU.mult).then_inc(dve_evac, 1)
                                v.wait_ge(dve_evac, 2 * i + j + 3)
                                part = lambda t: t[:, ds(2 * i + j, 1), :].rearrange("p a n -> p (a n)")
                                nc.vector.tensor_copy(part(hh), hid[:, j]).then_inc(S("hidden_high"), 1)
                                v.wait_ge(S("hidden_high"), 2 * i + j + 1)
                                nc.vector.tensor_tensor(part(hl), hid[:, j], part(hh).bitcast(F32), ALU.subtract
                                                        ).then_inc(S("hidden_low"), 1)
            clear()

        def phase_ffn_out(hh, hl, fo, l, which):
            with ExitStack() as st:
                KH = KF // 2
                W, WH, WL = weight_buffers(st, KH)
                wo = ffn_w_out[ds(l, 1), which].rearrange("a (k p) n -> p (a k) n", p=P)
                NI = KD // 2
                with nc.Block() as block:
                    @block.sync
                    def _(sp):
                        sp.sem_inc(S("split"), 2)
                        with sp.Fori(0, NI) as i:
                            for s in range(4):
                                c = sp.snap((2 * i + s // 2) * P)
                                sp.wait_ge(S("split"), 4 * i + s + 1)
                                sp.sem_inc(S("asked"), 1)
                                k0 = (s % 2) * KH
                                sp.dma_start(W[:, s % 2], wo[:, k0:k0 + KH, ds(c, P)]).then_inc(landed[s % 2], 16)

                    @block.gpsimd
                    def _(g):
                        with g.Fori(0, NI) as i:
                            for s in range(4):
                                low_part(g, 4 * i + s, W, WH, WL, s % 2, KH)

                    @block.scalar
                    def _(act):
                        with act.Fori(0, NI) as i:
                            for s in range(4):
                                high_part(act, 4 * i + s, 32 * i + 16 * (s // 2) + 16, W, WH, s % 2, KH)

                    @block.tensor
                    def _(pe):
                        pe.sem_inc(tile_done, 2)
                        pe.sem_inc(dve_evac, 2)
                        with pe.Fori(0, NI) as i:
                            for s in range(4):
                                pe.wait_ge(S("split"), 4 * i + s + 3)
                                if s % 2 == 0:
                                    pe.wait_ge(dve_evac, 2 * i + s // 2 + 1)
                                for k in range(KH):
                                    for a in range(2):
                                        half = slice(a * H2, (a + 1) * H2)
                                        kk = (s % 2) * KH + k
                                        last = exact(PS[:, 2 * (s // 2) + a, 0:H2], WH[:, s % 2, k], WL[:, s % 2, k],
                                                     hh[:, kk, half], hl[:, kk, half], kk == 0, kk == KF - 1)
                                last.then_inc(tile_done, 1)

                    @block.vector
                    def _(v):
                        with v.Fori(0, NI) as i:
                            for j in range(2):
                                v.wait_ge(tile_done, 4 * i + 2 * j + 4)
                                nc.vector.tensor_copy(
                                    fo[:, ds(2 * i + j, 1), :].rearrange("p a (b n) -> p (a b) n", b=2),
                                    PS[:, 2 * j:2 * j + 2, 0:H2]).then_inc(dve_evac, 1)
            clear()

        def phase_proj(pj, tok, l, c0, n, small_too=False):
            with ExitStack() as st:
                W, WH, WL = weight_buffers(st, KD + 1)
                wv = w_in[ds(l, 1)].rearrange("a (k p) n -> p (a k) n", p=P)
                NI = n // 2
                flatw = lambda t, w: t[:, w].rearrange("p a b -> p (a b)").rearrange("p (k c) -> p k c", k=KD)
                w_small = n % 2
                with nc.Block() as block:
                    @block.sync
                    def _(sp):
                        sp.sem_inc(S("split"), 2)
                        with sp.Fori(0, NI) as i:
                            for s in range(2):
                                c = sp.snap((2 * i + s) * P + c0)
                                sp.wait_ge(S("split"), 2 * i + s + 1)
                                sp.sem_inc(S("asked"), 1)
                                sp.dma_start(W[:, s, 0:KD], wv[:, :, ds(c, P)]).then_inc(landed[s], 16)
                        if n % 2:
                            sp.wait_ge(S("split"), n)
                            sp.dma_start(W[:, 0, 0:KD], wv[:, :, c0 + (n - 1) * P:c0 + n * P]
                                         ).then_inc(landed[0], 16)
                        if small_too:
                            sp.wait_ge(S("split"), n + 1)
                            for a, b, c in ((0, 64, C_KIDX), (64, 136, C_KIDX), (136, 144, C_IG)):
                                sp.dma_start(flatw(W, w_small)[:, :, a:b], wv[:, :, c:c + b - a]
                                             ).then_inc(landed[w_small], 16)

                    @block.gpsimd
                    def _(g):
                        with g.Fori(0, NI) as i:
                            for s in range(2):
                                low_part(g, 2 * i + s, W, WH, WL, s, KD)
                        if n % 2:
                            low_part(g, n - 1, W, WH, WL, 0, KD)
                        if small_too:
                            low_part(g, n, W, WH, WL, w_small, KD + 1)

                    @block.scalar
                    def _(act):
                        with act.Fori(0, NI) as i:
                            for s in range(2):
                                high_part(act, 2 * i + s, 16 * i + 16, W, WH, s, KD)
                        if n % 2:
                            high_part(act, n - 1, 16 * NI + 16, W, WH, 0, KD)
                        if small_too:
                            high_part(act, n, 16 * (n // 2) + 48, W, WH, w_small, KD + 1)

                    @block.tensor
                    def _(pe):
                        pe.sem_inc(tile_done, 2)
                        pe.sem_inc(dve_evac, 2)

                        def tile(t, s, weights):
                            pe.wait_ge(S("split"), t + 3)
                            pe.wait_ge(dve_evac, t + 1)
                            for k in range(KD):
                                for a in range(2):
                                    half = slice(a * H2, (a + 1) * H2)
                                    last = exact(PS[:, 2 * s + a, 0:H2], weights(WH, k), weights(WL, k),
                                                 uh[:, k, half], ul[:, k, half], k == 0, k == KD - 1)
                            last.then_inc(tile_done, 1)

                        with pe.Fori(0, NI) as i:
                            for s in range(2):
                                tile(2 * i + s, s, lambda t, k: t[:, s, k])
                        if n % 2:
                            tile(n - 1, 0, lambda t, k: t[:, 0, k])
                        if small_too:
                            tile(n, w_small, lambda t, k: flatw(t, w_small)[:, k, 0:P])
                            for j, (t0, m) in enumerate(QT):
                                for k in range(KD):
                                    sm = lambda t: flatw(t, w_small)[:, k, P:P + 16]
                                    tk = lambda t: t[:, k, t0:t0 + P]
                                    last = exact(PS[:, 4, 16 * j:16 * j + 16], tk(uh), tk(ul), sm(WH), sm(WL),
                                                 k == 0, k == KD - 1)
                            last.then_inc(tile_done, 1)

                    @block.vector
                    def _(v):
                        with v.Fori(0, NI) as i:
                            for s in range(2):
                                v.wait_ge(tile_done, 2 * i + s + 3)
                                nc.vector.tensor_copy(
                                    pj[:, ds(2 * i + s, 1), :].rearrange("p a (b n) -> p (a b) n", b=2),
                                    PS[:, 2 * s:2 * s + 2, 0:H2]).then_inc(dve_evac, 1)
                        for t in range(2 * NI, n + small_too):
                            v.wait_ge(tile_done, t + 3)
                            s = t % 2
                            nc.vector.tensor_copy(halves(pj[:, t]), PS[:, 2 * s:2 * s + 2, 0:H2]
                                                  ).then_inc(dve_evac, 1)
                        if small_too:
                            v.wait_ge(tile_done, n + 4)
                            for j, (t0, m) in enumerate(QT):
                                nc.vector.tensor_copy(tok[0:m, j, :], PS[0:m, 4, 16 * j:16 * j + 16]
                                                      ).then_inc(dve_evac, 1)
            clear()

        def phase_merge(yb, mixed, l, st):
            acc = sb(st, "acc", [P, 3, T])
            gt = sb(st, "gt", [P, 3, T])
            W, WH, WL = weight_buffers(st, KD)
            WB = sb(st, "W_branch", [P, 3 * BW // P, P])
            wv = w_in[ds(l, 1)].rearrange("a (k p) n -> p (a k) n", p=P)
            wb = w_branch[ds(l, 1)].rearrange("a g (k p) n -> p (a g k) n", p=P)
            NI = KD // 2
            with nc.Block() as block:
                @block.sync
                def _(sp):
                    sp.sem_inc(S("split"), 2)
                    sp.sem_inc(S("projected"), 1)
                    with sp.Fori(0, NI) as i:
                        for s in range(6):
                            c = sp.snap(2 * P * i + (s // 3) * P + C_GATE + (s % 3) * D_MODEL)
                            sp.wait_ge(S("split"), 6 * i + s + 1)
                            sp.sem_inc(S("asked"), 1)
                            sp.dma_start(W[:, s % 2], wv[:, :, ds(c, P)]).then_inc(landed[s % 2], 16)
                            if s % 3 == 0:
                                c = sp.snap(2 * P * i + (s // 3) * P)
                                sp.wait_ge(S("projected"), 2 * i + s // 3 + 1)
                                sp.sem_inc(S("asked"), 1)
                                sp.dma_start(WB[:], wb[:, :, ds(c, P)]).then_inc(landed[2], 16)

                @block.gpsimd
                def _(g):
                    with g.Fori(0, NI) as i:
                        for s in range(6):
                            low_part(g, 6 * i + s, W, WH, WL, s % 2, KD)

                @block.scalar
                def _(act):
                    def gate(i, s):
                        act.wait_ge(tile_done, 6 * i + s + 3)
                        act.wait_ge(dve_evac, 6 * i + 3 * (s // 3) + 1)
                        nc.scalar.activation(halves(gt[:, s % 3]), PS[:, 2 * (s % 3):2 * (s % 3) + 2, 0:H2],
                                             ACT.Sigmoid).then_inc(act_evac, 1)

                    with act.Fori(0, NI) as i:
                        for s in range(6):
                            high_part(act, 6 * i + s, 48 * i + 16 * (s // 2) + 16, W, WH, s % 2, KD)
                            if s:
                                gate(i, s - 1)
                        gate(i, 5)

                @block.tensor
                def _(pe):
                    pe.sem_inc(tile_done, 2)
                    pe.sem_inc(act_evac, 3)
                    pe.sem_inc(dve_evac, 1)
                    with pe.Fori(0, NI) as i:
                        for m in range(2):
                            for s in range(3):
                                n, w = 3 * m + s, (3 * m + s) % 2
                                pe.wait_ge(S("split"), 6 * i + n + 3)
                                pe.wait_ge(act_evac, 6 * i + n + 1)
                                for k in range(KD):
                                    for a in range(2):
                                        half = slice(a * H2, (a + 1) * H2)
                                        last = exact(PS[:, 2 * s + a, 0:H2], WH[:, w, k], WL[:, w, k],
                                                     uh[:, k, half], ul[:, k, half], k == 0, k == KD - 1)
                                last.then_inc(tile_done, 1)
                            pe.wait_ge(landed[2], 32 * i + 16 * m + 16)
                            for s in range(3):
                                pe.wait_ge(dve_evac, 6 * i + 3 * m + s + 1)
                                for k in range(4):
                                    for a in range(2):
                                        last = nc.tensor.matmul(PS[:, 6 + a, 0:H2], WB[:, 4 * s + k],
                                                                yb[:, 4 * s + k, a * H2:(a + 1) * H2],
                                                                start=k == 0, stop=k == 3)
                                last.then_inc(S("projected") if s == 2 else S("product"), 1)

                @block.vector
                def _(v):
                    with v.Fori(0, NI) as i:
                        for m in range(2):
                            for s in range(3):
                                if s < 2:
                                    v.wait_ge(S("product"), 4 * i + 2 * m + s + 1)
                                else:
                                    v.wait_ge(S("projected"), 2 * i + m + 2)
                                v.wait_ge(act_evac, 6 * i + 3 * m + s + 4)
                                nc.vector.tensor_tensor(halves(acc[:, s]), PS[:, 6:8, 0:H2], halves(gt[:, s]),
                                                        ALU.mult).then_inc(dve_evac, 1)
                            v.wait_ge(dve_evac, 6 * i + 3 * m + 3)
                            nc.vector.tensor_tensor(acc[:, 0], acc[:, 0], acc[:, 1], ALU.add).then_inc(dve_own, 1)
                            v.wait_ge(dve_own, 2 * i + m + 1)
                            v.wait_ge(dve_evac, 6 * i + 3 * m + 4)
                            nc.vector.tensor_tensor(mixed[:, ds(2 * i + m, 1), :].rearrange("p a n -> p (a n)"),
                                                    acc[:, 0], acc[:, 2], ALU.add).then_inc(S("mixed"), 1)
                            v.wait_ge(S("mixed"), 2 * i + m + 1)

        def phase_out(mixed, fo, l, st):
            W = sb(st, "W", [P, 4, KD, P])
            wv = w_out[ds(l, 1)].rearrange("a (k p) n -> p (a k) n", p=P)
            with nc.Block() as block:
                @block.sync
                def _(sp):
                    for t in range(KD):
                        if t >= 4:
                            sp.wait_ge(tile_done, t - 3)
                        sp.dma_start(W[:, t % 4, 0:KD], wv[:, :, t * P:(t + 1) * P]).then_inc(landed[t % 4], 16)

                @block.tensor
                def _(pe):
                    for t in range(KD):
                        s = t % 4
                        pe.wait_ge(landed[s], 16 * (t // 4) + 16)
                        if t >= 4:
                            pe.wait_ge(act_evac, t - 3)
                        for k in range(KD):
                            for a in range(2):
                                last = nc.tensor.matmul(PS[:, 2 * s + a, 0:H2], W[:, s, k],
                                                        mixed[:, k, a * H2:(a + 1) * H2],
                                                        start=k == 0, stop=k == KD - 1)
                        last.then_inc(tile_done, 1)

                @block.scalar
                def _(act):
                    for t in range(KD):
                        act.wait_ge(tile_done, t + 1)
                        nc.scalar.activation(halves(fo[:, t]), PS[:, 2 * (t % 4):2 * (t % 4) + 2, 0:H2], ACT.Copy
                                             ).then_inc(act_evac, 1)

        def phase_end(st):
            ot = sb(st, "ot", [P, 4, D_MODEL])
            with nc.Block() as block:
                @block.tensor
                def _(pe):
                    for j in range(4):
                        for q in range(2):
                            n = 2 * j + q
                            if n >= 4:
                                pe.wait_ge(ev["dve_to_pe"], n - 3)
                            for f in range(4):
                                last = nc.tensor.transpose(PS[:, n % 4, f * P:(f + 1) * P],
                                                           h[:, 4 * q + f, N_META + j * P:N_META + (j + 1) * P],
                                                           ident[:])
                            last.then_inc(ev["pe_to_dve"], 1)

                @block.vector
                def _(v):
                    for n in range(8):
                        v.wait_ge(ev["pe_to_dve"], n + 1)
                        nc.vector.tensor_copy(ot[:, n // 2, (n % 2) * 512:(n % 2) * 512 + 512], PS[:, n % 4, :]
                                              ).then_inc(ev["dve_to_pe"], 1)

                @block.sync
                def _(sp):
                    for j in range(4):
                        sp.wait_ge(ev["dve_to_pe"], 2 * j + 2)
                        sp.dma_start(out[0, j * P:(j + 1) * P, :], ot[:, j, :]).then_inc(stored, 16)
                    sp.wait_ge(stored, 64)

        def phase_rwkv(pj, tok, yb, l, st):
            s1, s2, s3 = (sb(st, f"rw_s{i}", [P, 4, T]) for i in range(3))
            gup = sb(st, "gup", [P, BW])
            early = st.enter_context(ExitStack())
            s4 = sb(early, "rw_s3", [P, 4, T])
            lora = sb(early, "lora", [P, BW])
            th = sb(early, "th", [P, T])
            omka = sb(early, "omka", [P, 4])
            r_, k_, v_ = pj[:, T_R:T_R + 4], pj[:, T_K:T_K + 4], pj[:, T_V:T_V + 4]
            a_, kh = yb[:, 4:8], yb[:, 8:12]
            fl = lambda t: t.rearrange("p a n -> p (a n)")
            col = lambda c, m: prm[:, c + m:c + m + 1]
            bank2 = lambda m: PS[:, 2 * m:2 * m + 2, 0:H2]

            with nc.Block() as block:
                @block.sync
                def _(sp):
                    for dst, src in ((lora[0:64], rw_w_up), (lora[64:P], rw_a_up), (gup[:], rw_g_up)):
                        sp.dma_start(dst, src[ds(l, 1)].rearrange("a k n -> (a k) n")).then_inc(loaded, 16)

                @block.vector
                def _(v):
                    own = Chain(v, dve_own)
                    for t0, n in ((T_WA, 2), (T_R, 4), (T_K, 4), (T_V, 4)):
                        p = pj[:, t0:t0 + n]
                        own(nc.vector.tensor_tensor(s1[:, 0:n, 1:T], p[:, :, 0:T - 1], p[:, :, 1:T], ALU.subtract))
                        own(nc.vector.tensor_scalar(s1[:, 0:n, 0:1], p[:, :, 0:1], -1.0, None, ALU.mult))
                        for m in range(n):
                            own(nc.vector.scalar_tensor_tensor(
                                out=pj[:, t0 + m], in0=s1[:, m], scalar=col(G_MU, t0 + m), in1=pj[:, t0 + m],
                                op0=ALU.mult, op1=ALU.add))
                        if t0 == T_WA:
                            v.sem_inc(S("inner_mixed"), 1)
                    own(nc.vector.memset(s3[:], 1.0))
                    own(nc.vector.memset(fl(s3[:]).rearrange("p (c t) -> p c t", t=CH)[:, :, 0:1], 0.0))
                    for m in range(4):
                        own(nc.vector.tensor_scalar(kh[:, m], k_[:, m], col(G_KK, m), None, ALU.mult))
                    v.sem_inc(S("kappa"), 1)
                    v.wait_ge(S("sigmoid_w"), 4)
                    own(nc.vector.tensor_scalar(s1[:], s1[:], DECAY, None, ALU.mult))
                    own(nc.vector.tensor_tensor_scan(fl(s2[:]), fl(s3[:]), fl(s1[:]), 0.0, ALU.mult, ALU.add))
                    own(nc.vector.tensor_tensor(s1[:], s2[:], s1[:], ALU.subtract))
                    v.sem_inc(S("logs"), 1)
                    v.wait_ge(S("kappa_sums"), 1)
                    for m in range(4):
                        own(nc.vector.tensor_scalar(halves(s4[:, m]), bank2(m), 1e-24, None, ALU.max))
                    own(nc.vector.reciprocal(s4[:], s4[:]))
                    v.sem_inc(S("kappa_recip"), 1)
                    v.wait_ge(S("kappa_rsqrt"), 1)
                    own(nc.vector.tensor_tensor(kh, kh, s4[:], ALU.mult))
                    own(nc.vector.tensor_scalar(omka[:], prm[:, G_KA:G_KA + 4], -1.0, 1.0, ALU.mult, ALU.add))
                    v.wait_ge(S("sigmoid_a"), 4)
                    for m in range(4):
                        own(nc.vector.tensor_scalar(s4[:, m], a_[:, m], col(G_KA, m), omka[:, m:m + 1],
                                                    ALU.mult, ALU.add))
                    own(nc.vector.tensor_tensor(k_, k_, s4[:], ALU.mult))
                    own(nc.vector.tensor_tensor(a_, a_, kh, ALU.mult))

                @block.scalar
                def _(act):
                    own = Chain(act, act_own)
                    act.wait_ge(S("inner_mixed"), 1)
                    nc.scalar.activation(th[64:P], pj[64:P, T_WA], ACT.Copy)
                    nc.scalar.activation(th[0:64], pj[0:64, T_WA], ACT.Tanh).then_inc(S("th"), 1)
                    nc.scalar.activation(pj[:, T_G], pj[:, T_G], ACT.Sigmoid)
                    act.wait_ge(S("kappa"), 1)
                    for m in range(4):
                        act.wait_ge(S("lora_w"), m + 1)
                        nc.scalar.activation(halves(s1[:, m]), bank2(m), ACT.Sigmoid, bias=col(G_W0, m)
                                             ).then_inc(S("sigmoid_w"), 1)
                    for m in range(4):
                        act.wait_ge(S("lora_a"), m + 1)
                        nc.scalar.activation(halves(a_[:, m]), bank2(m), ACT.Sigmoid, bias=col(G_A0, m)
                                             ).then_inc(S("sigmoid_a"), 1)
                    nc.scalar.activation(s4[:], kh, ACT.Square).then_inc(S("kappa_squares"), 1)
                    act.wait_ge(S("logs"), 1)
                    nc.scalar.activation(s3[:], s2[:], ACT.Exp, scale=-1.0).then_inc(S("exps"), 1)
                    act.wait_ge(S("exps"), 1)
                    nc.scalar.activation(s2[:], s2[:], ACT.Exp)
                    nc.scalar.activation(s1[:], s1[:], ACT.Exp)
                    act.wait_ge(S("kappa_recip"), 1)
                    nc.scalar.activation(s4[:], s4[:], ACT.Sqrt).then_inc(S("kappa_rsqrt"), 1)

                @block.tensor
                def _(pe):
                    pe.wait_ge(loaded, 48)
                    pe.wait_ge(S("th"), 1)
                    for b, name in ((0, "lora_w"), (64, "lora_a")):
                        for m in range(4):
                            if b:
                                pe.wait_ge(S("sigmoid_w"), m + 1)
                            for a in range(2):
                                last = nc.tensor.matmul(PS[:, 2 * m + a, 0:H2], lora[b:b + 64, m * P:(m + 1) * P],
                                                        th[b:b + 64, a * H2:(a + 1) * H2], start=True, stop=True)
                            last.then_inc(S(name), 1)
                    pe.wait_ge(S("kappa_squares"), 1)
                    for m in range(4):
                        pe.wait_ge(S("sigmoid_a"), m + 1)
                        for a in range(2):
                            last = nc.tensor.matmul(PS[:, 2 * m + a, 0:H2], half_ones[:],
                                                    s4[:, m, a * H2:(a + 1) * H2], start=True, stop=True)
                    last.then_inc(S("kappa_sums"), 1)
            clear()

            early.close()

            rec = st.enter_context(ExitStack())
            stage = sb(rec, "stage", [P, 2, GC, 7, 64])
            stage_bd = sb(rec, "stage_bd", [P, GC, 3, P])
            sg = sb(rec, "sg", [P, 2, GC, 5, 64])
            tk = sb(rec, "tk", [P, GC, 2, 64])
            v_bd = sb(rec, "v_bd", [P, 2, GC, P])
            tk_bd = sb(rec, "tk_bd", [P, GC, 2, P])
            rr = sb(rec, "rr", [P, GC, P])
            bm, vm, um, mm, nn = (sb(rec, n, [P, GC, 4, 64]) for n in ("bm", "vm", "um", "mm", "nn"))
            n2, n4 = (sb(rec, n, [P, GC, 2, 64]) for n in ("n2", "n4"))
            n8, za, zb, qp = (sb(rec, n, [P, GC, 64]) for n in ("n8", "za", "zb", "qp"))
            xx = sb(rec, "xx", [P, GC, P])
            xx_bd = sb(rec, "xx_bd", [P, GC, 2, P])
            state = sb(rec, "state", [P, 4, 64])
            kC, kB, kP, kQ, kV, kBt, kCt = range(7)
            PAR = ((0, slice(0, 64)), (1, slice(64, P)))
            gw = GC * CH
            tps = PS[:, 3:5].rearrange("p a b -> p (a b)")[:, 0:768].rearrange("p (c k n) -> p c k n", c=GC, k=4)
            nps = PS[:, 5, 0:GC * P].rearrange("p (c k n) -> p c k n", c=GC, k=2)
            wps = PS[:, 0, 0:GC * 64].rearrange("p (c n) -> p c n", c=GC)
            zps = PS[:, 1, 256:256 + GC * 64].rearrange("p (c n) -> p c n", c=GC)
            sps = PS[:, 6, 0:256].rearrange("p (a n) -> p a n", a=4)
            yps = PS[:, 7, 0:GC * 64].rearrange("p (c n) -> p c n", c=GC)
            n_ps = (PS[:, 3, 0:256], PS[:, 3, 256:512], PS[:, 4, 0:256])
            flat = lambda t: t.rearrange("p a n -> p (a n)")

            with nc.Block() as block:
                @block.vector
                def _(v):
                    own = Chain(v, dve_own)
                    tt = nc.vector.tensor_tensor

                    def stage_now(g, s):
                        grp = lambda t: t[:, :, ds(g * gw, gw)].rearrange("p a (c t) -> p c a t", c=GC)
                        for kind, a, b in ((kC, k_, s3[:]), (kB, a_, s3[:]), (kP, kh, s1[:]), (kQ, r_, s2[:])):
                            for c in range(GC):
                                last = tt(stage[:, s, c, kind].rearrange("p (a t) -> p a t", a=4),
                                          grp(a)[:, c], grp(b)[:, c], ALU.mult)
                        own(last)
                        v.sem_inc(S("staged"), 1)

                    def stage_rest(g, s):
                        grp = lambda t: t[:, :, ds(g * gw, gw)].rearrange("p a (c t) -> p c a t", c=GC)
                        stg = lambda c, kind: stage[:, s, c, kind].rearrange("p (a t) -> p a t", a=4)
                        for c in range(GC):
                            w = grp(s2[:])[:, c, :, CH - 1:CH].broadcast_to([P, 4, CH])
                            nc.vector.tensor_copy(stg(c, kV), grp(v_)[:, c])
                            nc.vector.scalar_tensor_tensor(out=stg(c, kBt), in0=stg(c, kB), scalar=-1.0, in1=w,
                                                           op0=ALU.mult, op1=ALU.mult)
                            last = tt(stg(c, kCt), stg(c, kC), w, ALU.mult)
                        last.then_inc(S("staged_rest"), 1)

                    def add_inputs(p, c):
                        v.wait_ge(S("stepped"), GC * p + c + 1)
                        if c == 0:
                            v.wait_ge(S("inputs_out"), p + 1)
                        tt(state[:], sps, nn[:, c], ALU.add).then_inc(S("state"), 1)

                    def group(g, s, prev, nxt):
                        if nxt:
                            if prev:
                                v.wait_ge(S("turned"), g)
                            stage_now(g + 1, 1 - s)
                        if prev:
                            add_inputs(g - 1, 0)
                        v.wait_ge(S("products"), g + 1)
                        tt(sg[:, s].rearrange("p c k n -> p c (k n)"), PS[:, 0:GC, 0:320],
                           flat(causal[:]).unsqueeze(1).broadcast_to([P, GC, 320]), ALU.mult
                           ).then_inc(S("masked"), 1)
                        v.wait_ge(S("masked"), g + 1)
                        own(tt(za[:], sg[:, s, :, 0], eye2[:].unsqueeze(1).broadcast_to([P, GC, 64]), ALU.add))
                        if prev:
                            add_inputs(g - 1, 1)
                        v.wait_ge(S("squared"), 3 * g + 1)
                        own(nc.vector.tensor_copy(n2[:], nps))
                        v.sem_inc(S("powers"), 1)
                        v.wait_ge(S("squared"), 3 * g + 2)
                        nc.vector.tensor_copy(n4[:], nps)
                        own(tt(zb[:], zps, za[:], ALU.add))
                        v.sem_inc(S("powers"), 1)
                        if prev:
                            add_inputs(g - 1, 2)
                        for c in range(GC):
                            w = s2[:, :, ds(g * gw + (c + 1) * CH - 1, 1)]
                            tt(mm[:, c], eye2[:].unsqueeze(1).broadcast_to([P, 4, 64]),
                               w.broadcast_to([P, 4, 64]), ALU.mult)
                        v.wait_ge(S("squared"), 3 * g + 3)
                        nc.vector.tensor_copy(n8[:], nps[:, :, 0])
                        own(tt(za[:], zps, zb[:], ALU.add))
                        v.sem_inc(S("powers"), 1)
                        v.wait_ge(S("last_factor"), g + 1)
                        tt(zb[:], zps, za[:], ALU.add).then_inc(S("inverse"), 1)
                        if nxt:
                            stage_rest(g + 1, 1 - s)
                        v.wait_ge(S("solution"), g + 1)
                        tt(um[:], xx[:, :, 64:P].unsqueeze(2).broadcast_to([P, GC, 4, 64]),
                           pairmask[:].unsqueeze(1).broadcast_to([P, GC, 4, 64]), ALU.mult
                           ).then_inc(S("solution_masked"), 1)
                        v.wait_ge(S("transfer"), g + 1)
                        tt(qp[:], zps, stage[:, s, :, kQ], ALU.add)
                        own(tt(mm[:].rearrange("p c a n -> p c (a n)"), mm[:].rearrange("p c a n -> p c (a n)"),
                               PS[:, 0:GC, 0:256], ALU.add))
                        v.sem_inc(S("transfer_out"), 1)

                    nc.vector.memset(state[:], 0.0).then_inc(S("state"), 1)
                    stage_now(0, 0)
                    stage_rest(0, 0)
                    group(0, 0, False, True)
                    with v.Fori(0, (NG - 3) // 2) as i:
                        own.enter(i, 12)
                        group(2 * i + 1, 1, True, True)
                        group(2 * i + 2, 0, True, True)
                    own.leave((NG - 3) // 2)
                    group(NG - 2, 1, True, True)
                    group(NG - 1, 0, True, False)
                    for c in range(GC):
                        add_inputs(NG - 1, c)

                @block.scalar
                def _(act):
                    copy = lambda dst, src: nc.scalar.activation(dst, src, ACT.Copy)

                    def stage_diagonal(g, s):
                        act.wait_ge(S("staged"), g + 1)
                        for b, sl in PAR:
                            last = copy(stage_bd[sl, :, :, sl], stage[sl, s, :, kC:kP + 1])
                        last.then_inc(S("staged_diagonal"), 1)

                    def y_out(p):
                        act.wait_ge(S("stepped"), GC * p + GC)
                        for c in range(GC):
                            last = copy(yb[:, 0:4, ds(p * gw + c * CH, CH)],
                                        yps[:, c].rearrange("p (a t) -> p a t", a=4))
                        last.then_inc(S("y_out"), 1)

                    def group(g, s, prev, nxt):
                        act.wait_ge(S("turned"), g + 1)
                        copy(tk[:], tps[:, :, 1:3])
                        copy(rr[:, :, 0:64], tps[:, :, 0]).then_inc(S("rows"), 1)
                        for b, sl in PAR:
                            copy(v_bd[sl, s, :, sl], tps[sl, :, 1])
                            last = copy(tk_bd[sl, :, :, sl], tps[sl, :, 2:4])
                        last.then_inc(S("rows_diagonal"), 1)
                        act.wait_ge(S("read_in"), g + 1)
                        copy(rr[:, :, 64:P], wps).then_inc(S("sides"), 1)
                        if prev:
                            y_out(g - 1)
                        if nxt:
                            stage_diagonal(g + 1, 1 - s)
                        act.wait_ge(S("solved"), g + 1)
                        solved = PS[:, 5, 0:GC * P].rearrange("p (c n) -> p c n", c=GC)
                        copy(xx[:], solved).then_inc(S("solution"), 1)
                        for b, sl in PAR:
                            last = copy(xx_bd[sl, :, :, sl], solved[sl].rearrange("p c (k n) -> p c k n", k=2))
                        last.then_inc(S("solution_diagonal"), 1)
                        act.wait_ge(S("inputs"), g + 1)
                        copy(nn[:].rearrange("p c a n -> p (c a n)"),
                             PS[:, 3:5].rearrange("p a b -> p (a b)")[:, 0:768]).then_inc(S("inputs_out"), 1)

                    act.wait_ge(S("zeros"), 1)
                    stage_diagonal(0, 0)
                    group(0, 0, False, True)
                    with act.Fori(0, (NG - 3) // 2) as i:
                        group(2 * i + 1, 1, True, True)
                        group(2 * i + 2, 0, True, True)
                    group(NG - 2, 1, True, True)
                    group(NG - 1, 0, True, False)
                    y_out(NG - 1)

                @block.gpsimd
                def _(g):
                    for t in (stage_bd, v_bd, tk_bd, xx_bd):
                        last = g.memset(t[:], 0.0)
                    last.then_inc(S("zeros"), 1)
                    msk = pairmask[:].unsqueeze(1).broadcast_to([P, GC, 4, 64])
                    with g.Fori(0, NG) as i:
                        g.wait_ge(S("rows"), i + 1)
                        g.sem_inc(S("pool_passed"), 1)
                        g.tensor_tensor(bm[:], tk[:, :, 1].unsqueeze(2).broadcast_to([P, GC, 4, 64]), msk, ALU.mult)
                        g.tensor_tensor(vm[:], tk[:, :, 0].unsqueeze(2).broadcast_to([P, GC, 4, 64]), msk, ALU.mult
                                        ).then_inc(S("rows_masked"), 1)

                @block.tensor
                def _(pe):
                    mmul = nc.tensor.matmul

                    def whole(dst, lhs, rhs, start=True, stop=True):
                        return mmul(dst, lhs, rhs, start=start, stop=stop, skip_group_check=True)

                    def both(fn):
                        for b, sl in PAR:
                            last = fn(sl)
                        return last

                    def wait(name, value):
                        pe.wait_ge(S(name), value)
                        pe.sem_inc(S("pe_passed"), 1)

                    def step(p, s, c):
                        if c == 0:
                            wait("y_out", p + 1)
                            wait("transfer_out", p + 1)
                        whole(yps[:, c], v_bd[:, s, c], sg[:, s, c, 3], stop=False)
                        whole(yps[:, c], xx_bd[:, c, 1], sg[:, s, c, 1], start=False, stop=False)
                        wait("state", GC * p + c + 1)
                        for a in range(4):
                            both(lambda sl: mmul(sps[sl, a], mm[sl, c, a], state[sl, a],
                                                 start=True, stop=True))
                        for a in range(4):
                            last = both(lambda sl: mmul(yps[sl, c, a * CH:(a + 1) * CH], state[sl, a],
                                                        qp[sl, c, a * CH:(a + 1) * CH], start=False,
                                                        stop=a == 3, skip_group_check=True))
                        last.then_inc(S("stepped"), 1)

                    def group(g, s, prev, nxt):
                        if prev:
                            step(g - 1, 1 - s, 0)
                        wait("staged_diagonal", g + 1)
                        for c in range(GC):
                            for k, rhs, c0, n in ((1, slice(kP, kQ + 1), 0, 128), (0, slice(kP, kQ + 1), 128, 128),
                                                  (2, slice(kB, kB + 1), 256, 64)):
                                last = whole(PS[:, c, c0:c0 + n], stage_bd[:, c, k], flat(stage[:, s, c, rhs]))
                        last.then_inc(S("products"), 1)
                        if prev:
                            wait("inputs_out", g)
                        wait("staged_rest", g + 1)
                        for c in range(GC):
                            whole(tps[:, c, 0], stage_bd[:, c, 2], eye2[:])
                            for k, kind in ((1, kV), (2, kBt), (3, kCt)):
                                last = both(lambda sl: mmul(tps[sl, c, k], stage[sl, s, c, kind], eye2[sl],
                                                            start=True, stop=True))
                        last.then_inc(S("turned"), 1)
                        if prev:
                            step(g - 1, 1 - s, 1)
                        wait("masked", g + 1)
                        for c in range(GC):
                            both(lambda sl: mmul(nps[sl, c, 0], sg[sl, s, c, 0], sg[sl, s, c, 4],
                                                 start=True, stop=True))
                            last = both(lambda sl: mmul(nps[sl, c, 1], sg[sl, s, c, 4], sg[sl, s, c, 0],
                                                        start=True, stop=True))
                        last.then_inc(S("squared"), 1)
                        wait("rows", g + 1)
                        for c in range(GC):
                            last = both(lambda sl: mmul(wps[sl, c], sg[sl, s, c, 2], tk[sl, c, 0],
                                                        start=True, stop=True))
                        last.then_inc(S("read_in"), 1)
                        wait("powers", 3 * g + 1)
                        for c in range(GC):
                            both(lambda sl: mmul(nps[sl, c, 0], n2[sl, c, 1], n2[sl, c, 0], start=True, stop=True))
                            both(lambda sl: mmul(nps[sl, c, 1], n2[sl, c, 0], n2[sl, c, 1], start=True, stop=True))
                            last = both(lambda sl: mmul(zps[sl, c], n2[sl, c, 0], za[sl, c], start=True, stop=True))
                        last.then_inc(S("squared"), 1)
                        if prev:
                            step(g - 1, 1 - s, 2)
                        wait("powers", 3 * g + 2)
                        for c in range(GC):
                            both(lambda sl: mmul(nps[sl, c, 0], n4[sl, c, 1], n4[sl, c, 0], start=True, stop=True))
                            last = both(lambda sl: mmul(zps[sl, c], n4[sl, c, 0], zb[sl, c], start=True, stop=True))
                        last.then_inc(S("squared"), 1)
                        wait("powers", 3 * g + 3)
                        for c in range(GC):
                            last = both(lambda sl: mmul(zps[sl, c], n8[sl, c], za[sl, c], start=True, stop=True))
                        last.then_inc(S("last_factor"), 1)
                        wait("sides", g + 1)
                        wait("inverse", g + 1)
                        for c in range(GC):
                            last = both(lambda sl: mmul(PS[sl, 5, c * P:(c + 1) * P], zb[sl, c], rr[sl, c],
                                                        start=True, stop=True))
                        last.then_inc(S("solved"), 1)
                        wait("rows_diagonal", g + 1)
                        wait("rows_masked", g + 1)
                        for c in range(GC):
                            whole(n_ps[c], tk_bd[:, c, 1], flat(vm[:, c]), start=c != 1, stop=False)
                        wait("solution_diagonal", g + 1)
                        for c in range(GC):
                            whole(zps[:, c], xx_bd[:, c, 0], sg[:, s, c, 1])
                            last = whole(PS[:, c, 0:256], xx_bd[:, c, 0], flat(bm[:, c]))
                        last.then_inc(S("transfer"), 1)
                        wait("solution_masked", g + 1)
                        for c in range(GC):
                            last = whole(n_ps[c], tk_bd[:, c, 0], flat(um[:, c]),
                                         start=False)
                        last.then_inc(S("inputs"), 1)

                    pe.sem_inc(S("y_out"), 1)
                    group(0, 0, False, True)
                    with pe.Fori(0, (NG - 3) // 2) as i:
                        group(2 * i + 1, 1, True, True)
                        group(2 * i + 2, 0, True, True)
                    group(NG - 2, 1, True, True)
                    group(NG - 1, 0, True, False)
                    for c in range(GC):
                        step(NG - 1, 0, c)
            clear()
            rec.close()
            s4 = sb(st, "rw_s3", [P, 4, T])

            with nc.Block() as block:
                y = yb[:, 0:4]

                @block.vector
                def _(v):
                    own = Chain(v, dve_own)
                    v.wait_ge(S("sum_y"), 1)
                    for m in range(4):
                        own(nc.vector.tensor_scalar(halves(s1[:, m]), bank2(m), -1.0 / 64, None, ALU.mult))
                    v.sem_inc(S("sum_y_out"), 1)
                    own(nc.vector.tensor_tensor(y, y, s1[:], ALU.add))
                    v.sem_inc(S("centred"), 1)
                    for m in range(4):
                        own(nc.vector.scalar_tensor_tensor(out=s2[:, m], in0=r_[:, m], scalar=col(G_RK, m),
                                                           in1=k_[:, m], op0=ALU.mult, op1=ALU.mult))
                    v.sem_inc(S("bonus_terms"), 1)
                    v.wait_ge(S("sum_sq"), 1)
                    for m in range(4):
                        own(nc.vector.tensor_scalar(halves(s4[:, m]), bank2(m), 1.0 / 64, GN_EPS, ALU.mult, ALU.add))
                    v.sem_inc(S("sum_sq_out"), 1)
                    own(nc.vector.reciprocal(s4[:], s4[:]))
                    v.sem_inc(S("var_recip"), 1)
                    v.wait_ge(S("var_rsqrt"), 1)
                    own(nc.vector.tensor_tensor(y, y, s4[:], ALU.mult))
                    for m in range(4):
                        own(nc.vector.tensor_scalar(y[:, m], y[:, m], col(G_GG, m), col(G_GB, m), ALU.mult, ALU.add))
                    v.wait_ge(S("sum_bonus"), 1)
                    for m in range(4):
                        own(nc.vector.tensor_tensor(halves(s1[:, m]), bank2(m), halves(v_[:, m]), ALU.mult))
                    v.sem_inc(S("sum_bonus_out"), 1)
                    own(nc.vector.tensor_tensor(y, y, s1[:], ALU.add))
                    v.wait_ge(S("gates"), 1)
                    for m in range(4):
                        own(nc.vector.tensor_tensor(halves(y[:, m]), bank2(m), halves(y[:, m]), ALU.mult))

                @block.scalar
                def _(act):
                    act.wait_ge(S("centred"), 1)
                    nc.scalar.activation(s3[:], y, ACT.Square).then_inc(S("y_squares"), 1)
                    act.wait_ge(S("var_recip"), 1)
                    nc.scalar.activation(s4[:], s4[:], ACT.Sqrt).then_inc(S("var_rsqrt"), 1)

                @block.tensor
                def _(pe):
                    def sums(src, weights, name):
                        for m in range(4):
                            for a in range(2):
                                last = nc.tensor.matmul(PS[:, 2 * m + a, 0:H2], weights(m),
                                                        src(m)[:, a * H2:(a + 1) * H2], start=True, stop=True)
                        last.then_inc(S(name), 1)
                    sums(lambda m: y[:, m], lambda m: half_ones[:], "sum_y")
                    pe.wait_ge(S("y_squares"), 1)
                    sums(lambda m: s3[:, m], lambda m: half_ones[:], "sum_sq")
                    pe.wait_ge(S("bonus_terms"), 1)
                    pe.wait_ge(S("sum_sq_out"), 1)
                    sums(lambda m: s2[:, m], lambda m: half_ones[:], "sum_bonus")
                    pe.wait_ge(S("sum_bonus_out"), 1)
                    sums(lambda m: pj[:, T_G], lambda m: gup[:, m * P:(m + 1) * P], "gates")

        def phase_dsa(pj, tok, yb, l, st):
            H = 8
            Q0, CKV, QI, KI = 0, 4, 5, 9
            qlat = sb(st, "qlat", [P, H, T])
            wuk = sb(st, "wuk", [P, 4, P])
            wuv = sb(st, "wuv", [P, H, 64])
            sq = sb(st, "dsa_sq", [P, T])
            ckv_tok = sb(st, "ckv_tok", [P, 5, P])
            wi = sb(st, "wi", [P, 5, H])
            relu = sb(st, "relu", [P, 2, T])
            score = sb(st, "score", [P, T])
            best = sb(st, "best", [P, 8])
            bias = sb(st, "bias", [P, T])
            lg = sb(st, "lg", [P, 2, T])
            pt = sb(st, "pt", [P, 2, 5, P])
            ot = sb(st, "ot_dsa", [P, H, P])
            stat = sb(st, "stat", [P, 2, 4])
            flat = lambda b: PS[:, b:b + 2].rearrange("p a n -> p (a n)")
            ckv = pj[:, CKV]
            NQ = len(QT)

            def spans(nk):
                return ((0, min(nk, 512)),) + (((512, nk),) if nk > 512 else ())

            with nc.Block() as block:
                @block.sync
                def _(sp):
                    for b in range(2):
                        sp.dma_start(wuk[64 * b:64 * b + 64],
                                     dsa_w_uk[ds(l, 1)].rearrange("o (a b) d c -> b d (o a) c", b=2)[b]
                                     ).then_inc(loaded, 16)
                    sp.dma_start(wuv[:], dsa_w_uv[ds(l, 1)].rearrange("o h c d -> c (o h) d")).then_inc(loaded, 16)

                @block.tensor
                def _(pe):
                    pe.wait_ge(S("ckv_squares"), 1)
                    for a in range(2):
                        last = nc.tensor.matmul(PS[:, a, 0:H2], ones[:], sq[:, a * H2:(a + 1) * H2],
                                                start=True, stop=True)
                    last.then_inc(S("ckv_sum"), 1)
                    pe.wait_ge(loaded, 48)
                    for hd in range(H):
                        b, m = 64 * (hd % 2), hd % 3 + 1
                        if hd >= 3:
                            pe.wait_ge(S("qlat"), hd - 2)
                        for a in range(2):
                            last = nc.tensor.matmul(PS[:, 2 * m + a, 0:H2], wuk[b:b + 64, hd // 2],
                                                    pj[b:b + 64, Q0 + hd // 2, a * H2:(a + 1) * H2],
                                                    start=True, stop=True)
                        last.then_inc(S("qlat_made"), 1)
                    pe.wait_ge(S("ckv"), 1)
                    for j, (t0, n) in enumerate(QT):
                        last = nc.tensor.transpose(PS[0:n, j // 4, (j % 4) * P:(j % 4 + 1) * P],
                                                   pj[:, CKV, t0:t0 + n], ident[:])
                    last.then_inc(S("ckv_turned"), 1)

                @block.scalar
                def _(act):
                    nc.scalar.activation(sq[:], ckv, ACT.Square).then_inc(S("ckv_squares"), 1)
                    act.wait_ge(S("ckv_recip"), 1)
                    nc.scalar.activation(rs[:], rs[:], ACT.Sqrt).then_inc(S("ckv_rsqrt"), 1)
                    for hd in range(H):
                        act.wait_ge(S("qlat_made"), hd + 1)
                        m = hd % 3 + 1
                        nc.scalar.activation(halves(qlat[:, hd]), PS[:, 2 * m:2 * m + 2, 0:H2], ACT.Copy,
                                             scale=0.125).then_inc(S("qlat"), 1)

                @block.vector
                def _(v):
                    own = Chain(v, dve_own)
                    v.wait_ge(S("ckv_sum"), 1)
                    own(nc.vector.tensor_scalar(halves(rs[:]), PS[:, 0:2, 0:H2], 1.0 / P, EPS, ALU.mult, ALU.add))
                    nc.vector.reciprocal(rs[:], rs[:]).then_inc(S("ckv_recip"), 1)
                    v.wait_ge(S("ckv_rsqrt"), 1)
                    nc.vector.scalar_tensor_tensor(out=ckv, in0=ckv, scalar=prm[:, G_KVN:G_KVN + 1], in1=rs[:],
                                                   op0=ALU.mult, op1=ALU.mult).then_inc(S("ckv"), 1)
                    for j, (t0, n) in enumerate(QT):
                        nc.vector.tensor_scalar(wi[0:n, j], tok[0:n, j, 0:H], 512.0 ** -0.5, None, ALU.mult)
                    v.wait_ge(S("ckv_turned"), 1)
                    for j, (t0, n) in enumerate(QT):
                        nc.vector.tensor_copy(ckv_tok[0:n, j], PS[0:n, j // 4, (j % 4) * P:(j % 4 + 1) * P])
            clear()

            with nc.Block() as block:
                @block.tensor
                def _(pe):
                    for j, (t0, n) in enumerate(QT):
                        nk = t0 + n
                        for hd in range(H if j else 0):
                            s, b, q = (j - 1) * H + hd, 64 * (hd % 2), hd % 2
                            if s >= 2:
                                pe.wait_ge(S("relu"), s - 1)
                            if hd < 2 and j > 1:
                                pe.wait_ge(S("logits_out"), (j - 1) * H + H)
                            elif hd < 2:
                                pe.wait_ge(S("logits_out"), H)
                            for k0, k1 in spans(nk):
                                last = nc.tensor.matmul(flat(2 * q)[0:n, k0:k1], pj[b:b + 64, QI + hd // 2, t0:t0 + n],
                                                        pj[b:b + 64, KI, k0:k1], start=True, stop=True)
                            last.then_inc(S("index"), 1)

                        def logits(hd):
                            e, q = j * H + hd, hd % 2
                            if j and hd < 2:
                                pe.wait_ge(S("relu"), j * H)
                            if e >= 2:
                                pe.wait_ge(S("logits_out"), e - 1)
                            for k0, k1 in spans(nk):
                                last = nc.tensor.matmul(flat(2 * q)[0:n, k0:k1], qlat[:, hd, t0:t0 + n],
                                                        pj[:, CKV, k0:k1], start=True, stop=True)
                            last.then_inc(S("logits"), 1)

                        def values(hd):
                            e, q = j * H + hd, hd % 2
                            pe.wait_ge(S("probs"), e + 1)
                            if e >= 1:
                                pe.wait_ge(S("probs_turned_out"), e)
                            for m in range(j + 1):
                                k0, kn = QT[m]
                                dst = PS[0:kn, 5, 0:n] if m == 0 else PS[0:kn, 4, (m - 1) * P:(m - 1) * P + n]
                                last = nc.tensor.transpose(dst, lg[0:n, q, k0:k0 + kn], ident[0:n, 0:n])
                            last.then_inc(S("probs_turned"), 1)
                            pe.wait_ge(S("probs_turned_out"), e + 1)
                            if e >= 1:
                                pe.wait_ge(S("value"), e)
                            for m in range(j + 1):
                                k0, kn = QT[m]
                                last = nc.tensor.matmul(PS[:, 6, 0:n], ckv_tok[0:kn, m], pt[0:kn, q, m, 0:n],
                                                        start=m == 0, stop=m == j)
                            last.then_inc(S("value_made"), 1)

                        logits(0)
                        for hd in range(H):
                            if hd + 1 < H:
                                logits(hd + 1)
                            values(hd)
                        pe.wait_ge(S("value"), (j + 1) * H)
                        if j:
                            pe.wait_ge(S("y"), j)
                        for hd in range(H):
                            b = 64 * (hd % 2)
                            last = nc.tensor.matmul(PS[b:b + 64, 7, (hd // 2) * P:(hd // 2) * P + n], wuv[:, hd],
                                                    ot[:, hd, 0:n], start=True, stop=True)
                        last.then_inc(S("y_made"), 1)

                @block.scalar
                def _(act):
                    for j, (t0, n) in enumerate(QT):
                        nk = t0 + n
                        for hd in range(H if j else 0):
                            s, q = (j - 1) * H + hd, hd % 2
                            act.wait_ge(S("index"), s + 1)
                            if s >= 2:
                                act.wait_ge(S("scored"), s - 1)
                            nc.scalar.activation(relu[0:n, q, 0:nk], flat(2 * q)[0:n, 0:nk], ACT.Relu
                                                 ).then_inc(S("relu"), 1)
                        for hd in range(H):
                            e, q = j * H + hd, hd % 2
                            act.wait_ge(S("max"), e + 1)
                            nc.scalar.activation(lg[0:n, q, 0:nk], lg[0:n, q, 0:nk], ACT.Exp,
                                                 bias=stat[0:n, q, 1:2], accum_out=stat[0:n, q, 2:3]
                                                 ).then_inc(S("exp"), 1)
                            act.wait_ge(S("probs_turned"), e + 1)
                            if e >= 2:
                                act.wait_ge(S("value_made"), e - 1)
                            if j:
                                nc.scalar.activation(pt[:, q, 1:j + 1, 0:n], PS[:, 4, 0:j * P].rearrange(
                                    "p (m n) -> p m n", n=P)[:, :, 0:n], ACT.Copy)
                            nc.scalar.activation(pt[0:N_META, q, 0, 0:n], PS[0:N_META, 5, 0:n], ACT.Copy
                                                 ).then_inc(S("probs_turned_out"), 1)
                            act.wait_ge(S("value_made"), e + 1)
                            if j and hd == 0:
                                act.wait_ge(S("y_made"), j)
                            nc.scalar.activation(ot[:, hd, 0:n], PS[:, 6, 0:n], ACT.Copy).then_inc(S("value"), 1)

                @block.vector
                def _(v):
                    own = Chain(v, dve_own)
                    for j, (t0, n) in enumerate(QT):
                        nk = t0 + n
                        for hd in range(H if j else 0):
                            s, q = (j - 1) * H + hd, hd % 2
                            v.wait_ge(S("relu"), s + 1)
                            if hd == 0:
                                own(nc.vector.tensor_scalar(score[0:n, 0:nk], relu[0:n, q, 0:nk], wi[0:n, j, hd:hd + 1],
                                                            None, ALU.mult))
                            else:
                                own(nc.vector.scalar_tensor_tensor(
                                    out=score[0:n, 0:nk], in0=relu[0:n, q, 0:nk], scalar=wi[0:n, j, hd:hd + 1],
                                    in1=score[0:n, 0:nk], op0=ALU.mult, op1=ALU.add))
                            v.sem_inc(S("scored"), 1)
                        if j:
                            own(nc.vector.memset(score[0:64, nk - 64:nk], FILL))
                            for _ in range(TOPK // 8):
                                own(nc.vector.max(best[0:n], score[0:n, 0:nk]))
                                own(nc.vector.match_replace(score[0:n, 0:nk], best[0:n], score[0:n, 0:nk], TAKEN))
                            own(nc.vector.tensor_scalar(bias[0:n, 0:nk], score[0:n, 0:nk], TAKEN, NEG,
                                                        ALU.not_equal, ALU.mult))
                            own(nc.vector.memset(bias[0:64, nk - 64:nk], NEG))
                        else:
                            own(nc.vector.memset(bias[:, 0:nk], 0.0))
                        for hd in range(H):
                            e, q = j * H + hd, hd % 2
                            v.wait_ge(S("logits"), e + 1)
                            if e >= 2:
                                v.wait_ge(S("probs_turned"), e - 1)
                            own(nc.vector.tensor_tensor_reduce(
                                out=lg[0:n, q, 0:nk], in0=flat(2 * q)[0:n, 0:nk], in1=bias[0:n, 0:nk], scale=1.0,
                                scalar=TAKEN, op0=ALU.add, op1=ALU.max, accum_out=stat[0:n, q, 0:1]))
                            v.sem_inc(S("logits_out"), 1)
                            own(nc.vector.tensor_scalar(stat[0:n, q, 1:2], stat[0:n, q, 0:1], -1.0, None, ALU.mult))
                            v.sem_inc(S("max"), 1)
                            v.wait_ge(S("exp"), e + 1)
                            own(nc.vector.reciprocal(stat[0:n, q, 3:4], stat[0:n, q, 2:3]))
                            own(nc.vector.tensor_scalar(lg[0:n, q, 0:nk], lg[0:n, q, 0:nk], stat[0:n, q, 3:4], None,
                                                        ALU.mult))
                            v.sem_inc(S("probs"), 1)
                        v.wait_ge(S("y_made"), j + 1)
                        nc.vector.tensor_copy(yb[:, 8:12, t0:t0 + n], PS[:, 7].rearrange(
                            "p (a n) -> p a n", n=P)[:, :, 0:n]).then_inc(S("y"), 1)

        def phase_mlstm(pj, tok, yb, l, st):
            H = 4
            MQ, MK, MV, MO = 0, 4, 8, 12
            NS = len(ST_)
            cv = sb(st, "cv", [P, 8, T])
            vt = sb(st, "vt", [P, NS, BW])
            gi, gf, bsum, msum, tmp4, one4, zer4 = (sb(st, n, [4, T]) for n in (
                "gi", "gf", "bsum", "msum", "tmp4", "one4", "zer4"))
            ibf = sb(st, "ibf", [4, 2])
            at = sb(st, "at", [P, NS, 4])
            nmb = sb(st, "nmb", [P, 2, T])
            dd = sb(st, "dd", [P, 2, T])
            ss = sb(st, "ss", [P, 2, T])
            den = sb(st, "den", [P, T])
            hq = sb(st, "hq", [P, 4, T])
            flat = lambda b: PS[:, b:b + 2].rearrange("p a n -> p (a n)")
            hy = yb[:, 4:8]

            def spans(j0):
                return ((j0, 512), (512, T)) if j0 < 512 else ((512, T),)

            with nc.Block() as block:
                @block.sync
                def _(sp):
                    for c, src in enumerate((ml_i_bias, ml_f_bias)):
                        sp.dma_start(ibf[:, c:c + 1], src[ds(l, 1)].rearrange("a h -> h a")).then_inc(loaded, 16)

                @block.tensor
                def _(pe):
                    for g in range(2):
                        for j, (t0, n) in enumerate(QT):
                            b, c = (1, 0) if j == 4 else (0, t0)
                            last = nc.tensor.transpose(PS[0:4, 2 * g + b, c:c + n], tok[0:n, j, 8 + 4 * g:12 + 4 * g],
                                                       ident[0:n, 0:n])
                    last.then_inc(S("gates_turned"), 1)
                    for j, (t0, n) in enumerate(ST_):
                        if j >= 2:
                            pe.wait_ge(S("v_out"), j - 1)
                        for m in range(4):
                            last = nc.tensor.transpose(PS[0:n, 4 + j % 2, m * P:(m + 1) * P],
                                                       pj[:, MV + m, t0:t0 + n], ident[:])
                        last.then_inc(S("v_turned"), 1)
                    pe.wait_ge(S("a"), 1)
                    for j, (t0, n) in enumerate(ST_):
                        last = nc.tensor.transpose(PS[0:n, 6, 4 * j:4 * j + 4], tmp4[:, t0:t0 + n], ident[0:4, 0:4])
                    last.then_inc(S("a_turned"), 1)

                @block.vector
                def _(v):
                    own = Chain(v, dve_own)
                    v.wait_ge(loaded, 32)
                    v.wait_ge(S("gates_turned"), 1)
                    for g, dst in ((0, gi), (1, gf)):
                        for c0, c1, b in ((0, 400, 0), (400, T, 1)):
                            last = nc.vector.tensor_scalar(dst[:, c0:c1], PS[0:4, 2 * g + b, 0:c1 - c0],
                                                           ibf[:, g:g + 1], None, ALU.add)
                    own(last)
                    v.sem_inc(S("gates_in"), 1)
                    nc.vector.memset(one4[:], 1.0)
                    nc.vector.memset(zer4[:], 0.0)
                    own(nc.vector.tensor_scalar(cv[:, 0], pj[:, 0], prm[:, G_CONVW + 24:G_CONVW + 25],
                                                prm[:, G_CONVB:G_CONVB + 1], ALU.mult, ALU.add))
                    for m in range(8):
                        if m:
                            own(nc.vector.tensor_scalar(cv[:, m], pj[:, m], prm[:, G_CONVW + 24 + m:G_CONVW + 25 + m],
                                                        prm[:, G_CONVB + m:G_CONVB + m + 1], ALU.mult, ALU.add))
                        for back in (1, 2, 3):
                            c = G_CONVW + 8 * (3 - back) + m
                            own(nc.vector.scalar_tensor_tensor(
                                out=cv[:, m, back:T], in0=pj[:, m, 0:T - back], scalar=prm[:, c:c + 1],
                                in1=cv[:, m, back:T], op0=ALU.mult, op1=ALU.add))
                        v.sem_inc(S("convolved"), 1)
                    v.wait_ge(S("softplus"), 1)
                    own(nc.vector.tensor_scalar(gf[:], gf[:], 0.0, None, ALU.min))
                    own(nc.vector.tensor_tensor(gf[:], gf[:], msum[:], ALU.subtract))
                    own(nc.vector.tensor_tensor_scan(bsum[:], one4[:], gf[:], 0.0, ALU.mult, ALU.add))
                    own(nc.vector.tensor_tensor(tmp4[:], gi[:], bsum[:], ALU.subtract))
                    v.sem_inc(S("a"), 1)
                    own(nc.vector.tensor_tensor_scan(msum[:], tmp4[:], tmp4[:], 0.0, ALU.max, ALU.max))
                    own(nc.vector.tensor_tensor(bsum[:], bsum[:], msum[:], ALU.add))
                    own(nc.vector.tensor_scalar(bsum[:], bsum[:], -1.0, 85.0, ALU.mult, ALU.min))
                    own(nc.vector.tensor_scalar(msum[:], msum[:], -1.0, None, ALU.mult))
                    v.sem_inc(S("m"), 1)
                    v.wait_ge(S("a_turned"), 1)
                    for j, (t0, n) in enumerate(ST_):
                        last = nc.vector.tensor_copy(at[0:n, j], PS[0:n, 6, 4 * j:4 * j + 4])
                    own(last)

                @block.scalar
                def _(act):
                    own = Chain(act, act_own)
                    act.wait_ge(S("gates_in"), 1)
                    own(nc.scalar.activation(msum[:], gf[:], ACT.Abs))
                    own(nc.scalar.activation(msum[:], msum[:], ACT.Exp, scale=-1.0))
                    own(nc.scalar.activation(msum[:], msum[:], ACT.Ln, bias=1.0))
                    act.sem_inc(S("softplus"), 1)
                    for j, (t0, n) in enumerate(ST_):
                        act.wait_ge(S("v_turned"), j + 1)
                        nc.scalar.activation(vt[0:n, j], PS[0:n, 4 + j % 2, :], ACT.Copy).then_inc(S("v_out"), 1)
                    for m in range(8):
                        act.wait_ge(S("convolved"), m + 1)
                        nc.scalar.activation(cv[:, m], cv[:, m], ACT.Silu)
                    nc.scalar.activation(pj[:, MO:MO + 4], pj[:, MO:MO + 4], ACT.Sigmoid)
                    act.wait_ge(S("m"), 1)
                    nc.scalar.activation(bsum[:], bsum[:], ACT.Exp).then_inc(act_own, 1)
            clear()

            with nc.Block() as block:
                @block.tensor
                def _(pe):
                    def spread(hd):
                        if hd:
                            pe.wait_ge(S("weighed"), NS * hd)
                        for a in range(2):
                            last = nc.tensor.matmul(PS[:, a, 0:H2], sel[0:4, hd], msum[:, a * H2:(a + 1) * H2],
                                                    start=True, stop=True)
                        last.then_inc(S("spread"), 1)

                    for hd in range(H):
                        spread(hd)
                        pe.wait_ge(S("spread_out"), hd + 1)

                        def scores(i):
                            e = hd * NS + i
                            s0, n = ST_[i]
                            if i >= 2:
                                pe.wait_ge(S("weighed"), e - 1)
                            for j0, j1 in spans(s0):
                                last = nc.tensor.matmul(flat(2 * (i % 2))[0:n, j0:j1], cv[:, MK + hd, s0:s0 + n],
                                                        cv[:, MQ + hd, j0:j1], start=True, stop=True)
                            last.then_inc(S("scores"), 1)

                        scores(0)
                        for i in range(NS):
                            if i + 1 < NS:
                                scores(i + 1)
                            e = hd * NS + i
                            s0, n = ST_[i]
                            pe.wait_ge(S("weighed"), e + 1)
                            if i == 0 and hd:
                                pe.wait_ge(S("head_out"), hd)
                            for bank, lhs in ((4, vt[0:n, i, hd * P:(hd + 1) * P]), (6, ones[0:n])):
                                for j0, j1 in spans(s0):
                                    last = nc.tensor.matmul(
                                        flat(bank)[:, j0:j1], lhs, ss[0:n, i % 2, j0:j1], start=i == 0,
                                        stop=i == (NS - 1 if j0 == 512 else NS - 2), skip_group_check=True)
                            last.then_inc(S("summed"), 1)
                        pe.wait_ge(S("weighed"), NS * (hd + 1))
                        for a in range(2):
                            last = nc.tensor.matmul(PS[:, a, 0:H2], sel[0:4, hd], bsum[:, a * H2:(a + 1) * H2],
                                                    start=True, stop=True)
                        last.then_inc(S("floor"), 1)
                        pe.wait_ge(S("head_out"), hd + 1)
                    pe.wait_ge(S("h_squares"), 1)
                    for m in range(4):
                        for a in range(2):
                            last = nc.tensor.matmul(PS[:, 2 * m + a, 0:H2], ones[:], hq[:, m, a * H2:(a + 1) * H2],
                                                    start=True, stop=True)
                    last.then_inc(S("h_sums"), 1)

                @block.vector
                def _(v):
                    own = Chain(v, dve_own)
                    for hd in range(H):
                        v.wait_ge(S("spread_out"), hd + 1)

                        def decay(i):
                            s0, n = ST_[i]
                            if hd * NS + i >= 2:
                                v.wait_ge(S("weighed"), hd * NS + i - 1)
                            nc.vector.tensor_scalar(dd[0:n, i % 2, s0:T], nmb[0:n, hd % 2, s0:T],
                                                    at[0:n, i, hd:hd + 1], 0.0, ALU.add, ALU.min
                                                    ).then_inc(S("decay_log"), 1)
                        decay(0)
                        for i in range(NS):
                            if i + 1 < NS:
                                decay(i + 1)
                            e = hd * NS + i
                            s0, n = ST_[i]
                            v.wait_ge(S("decay"), e + 1)
                            v.wait_ge(S("scores"), e + 1)
                            if e >= 2:
                                v.wait_ge(S("summed"), e - 1)
                            nc.vector.scalar_tensor_tensor(
                                out=ss[0:n, i % 2, s0:T], in0=flat(2 * (i % 2))[0:n, s0:T], scalar=P ** -0.5,
                                in1=dd[0:n, i % 2, s0:T], op0=ALU.mult, op1=ALU.mult).then_inc(S("weighed"), 1)
                        v.wait_ge(S("floor"), hd + 1)
                        v.wait_ge(S("den"), hd + 1)
                        own(nc.vector.tensor_tensor(halves(den[:]), PS[:, 0:2, 0:H2], halves(den[:]), ALU.max))
                        own(nc.vector.reciprocal(den[:], den[:]))
                        own(nc.vector.tensor_tensor(hy[:, hd], flat(4)[:, 0:T], den[:], ALU.mult))
                        v.sem_inc(S("head_out"), 1)
                    v.wait_ge(S("h_sums"), 1)
                    for m in range(4):
                        last = nc.vector.tensor_scalar(halves(hq[:, m]), PS[:, 2 * m:2 * m + 2, 0:H2], 1.0 / P, EPS,
                                                       ALU.mult, ALU.add)
                    own(last)
                    own(nc.vector.reciprocal(hq[:], hq[:]))
                    v.sem_inc(S("h_recip"), 1)
                    v.wait_ge(S("h_rsqrt"), 1)
                    own(nc.vector.tensor_tensor(hy, hy, hq[:], ALU.mult))
                    for m in range(4):
                        nc.vector.scalar_tensor_tensor(
                            out=hy[:, m], in0=hy[:, m], scalar=prm[:, G_MLN + m:G_MLN + m + 1], in1=pj[:, MO + m],
                            op0=ALU.mult, op1=ALU.mult)

                @block.scalar
                def _(act):
                    for hd in range(H):
                        act.wait_ge(S("spread"), hd + 1)
                        nc.scalar.activation(halves(nmb[:, hd % 2]), PS[:, 0:2, 0:H2], ACT.Copy
                                             ).then_inc(S("spread_out"), 1)
                        for i in range(NS):
                            e = hd * NS + i
                            s0, n = ST_[i]
                            act.wait_ge(S("decay_log"), e + 1)
                            nc.scalar.activation(dd[0:n, i % 2, s0:T], dd[0:n, i % 2, s0:T], ACT.Exp
                                                 ).then_inc(S("decay_exp"), 1)
                        act.wait_ge(S("summed"), NS * (hd + 1))
                        if hd:
                            act.wait_ge(S("head_out"), hd)
                        nc.scalar.activation(den[:], flat(6)[:, 0:T], ACT.Abs).then_inc(S("den"), 1)
                    act.wait_ge(S("head_out"), H)
                    nc.scalar.activation(hq[:], hy, ACT.Square).then_inc(S("h_squares"), 1)
                    act.wait_ge(S("h_recip"), 1)
                    nc.scalar.activation(hq[:], hq[:], ACT.Sqrt).then_inc(S("h_rsqrt"), 1)

                @block.gpsimd
                def _(g):
                    for e in range(H * NS):
                        s0, n = ST_[e % NS]
                        g.wait_ge(S("decay_exp"), e + 1)
                        d = dd[0:n, (e % NS) % 2, s0:s0 + n]
                        g.affine_select(out=d, in_=d, compare_op=ALU.is_ge, fill=0.0, base=0, pattern=[[1, n]],
                                        channel_multiplier=-1).then_inc(S("decay"), 1)

        def run(phase, *args):
            with ExitStack() as st:
                phase(st, *args)
            clear()

        run(phase_start)
        with nc.Fori(0, DEPTH) as l:
            run(phase_params, l)

            def ffn(which):
                run(phase_norm, h, G_NORM + KD * 4 * which, 1.0, "u")
                with ExitStack() as st:
                    hh = sb(st, "hidden_high", [P, KF, T], F32R)
                    hl = sb(st, "hidden_low", [P, KF, T], F32R)
                    phase_ffn_in(hh, hl, l, which)
                    fo = sb(st, "fo", [P, KD, T])
                    phase_ffn_out(hh, hl, fo, l, which)
                    run(phase_norm, fo, G_NORM + KD * (4 * which + 1), 0.5, "h")

            ffn(0)
            run(phase_norm, h, G_NORM + 2 * KD, 1.0, "u")
            with ExitStack() as outer:
                yb = sb(outer, "yb", [P, 12, T])
                if len(BR) < 3:
                    with nc.Block() as block:
                        @block.vector
                        def _(v):
                            nc.vector.memset(yb[:], 1.0)
                with ExitStack() as st:
                    pj = sb(st, "pj", [P, 16, T])
                    tok = sb(st, "tok", [P, 5, 16])
                    for name, branch, c0, n, small_too in (
                            ("rw", phase_rwkv, 0, 14, False), ("dsa", phase_dsa, C_DSA, 9, True),
                            ("ml", phase_mlstm, RW_COLS, 16, False)):
                        if name not in BR:
                            continue
                        phase_proj(pj, tok, l, c0, n, small_too)
                        with ExitStack() as st2:
                            branch(pj, tok, yb, l, st2)
                        clear()
                if debug is not None:
                    debug(nc, "yb", yb, l)
                mixed = sb(outer, "mixed", [P, KD, T])
                fo = sb(outer, "fo2", [P, KD, T])
                with ExitStack() as st:
                    phase_merge(yb, mixed, l, st)
                clear()
                with ExitStack() as st:
                    phase_out(mixed, fo, l, st)
                clear()
                run(phase_norm, fo, G_NORM + 3 * KD, 1.0, "h")
            ffn(1)
        run(phase_end)


_INS = ["x", "meta_tokens", "norm_gain", "ffn_w_in", "ffn_w_out", "w_in", "rw_mu", "rw_w0", "rw_w_up", "rw_a0",
        "rw_a_up", "rw_g_up", "rw_k_k", "rw_k_a", "rw_r_k", "rw_gn_gain", "rw_gn_bias", "ml_conv_w", "ml_conv_b",
        "ml_i_bias", "ml_f_bias", "ml_norm_gain", "dsa_kv_norm", "dsa_w_uk", "dsa_w_uv", "w_branch", "w_out"]


def kernel(**inputs):
    import concourse.bacc as bacc
    from concourse.bass_utils import run_bass_kernel_spmd

    nc = bacc.Bacc("TRN2", target_bir_lowering=False, num_devices=1)
    arrays, args = {}, []
    for name in _INS:
        a = np.ascontiguousarray(inputs[name])
        arrays[f"in_{name}"] = a
        args.append(nc.dram_tensor(f"in_{name}", a.shape, mybir.dt.from_np(a.dtype), kind="ExternalInput").ap())
    args.append(nc.dram_tensor("out_0", (1, SEQ, D_MODEL), F32, kind="ExternalOutput").ap())
    build_program(nc, *args)
    r = run_bass_kernel_spmd(nc, [arrays], core_ids=[0])
    return r.results[0]["out_0"]
```

```python
import math
from contextlib import ExitStack

import numpy as np

import concourse.bass as bass
from concourse import mybir

F32 = mybir.dt.float32
F32R = mybir.dt.float32r
ALU = mybir.AluOpType
ACT = mybir.ActivationFunctionType
AX = mybir.AxisListType.X
ds = bass.ds

P = 128
D_MODEL, SEQ, N_META, DEPTH, D_FF = 1024, 512, 16, 2, 2816
T = SEQ + N_META
H2 = T // 2
KD = D_MODEL // P
KF = D_FF // P
BW = 512
RW_COLS, ML_COLS = 1792, 2056
C_IG = RW_COLS + 2048
C_DSA = RW_COLS + ML_COLS
C_KIDX = C_DSA + BW + P + 512
C_GATE = C_KIDX + 64 + 8
N_IN = C_GATE + 3 * D_MODEL
EPS = 1e-6
GN_EPS = 64e-5
CH = 16
GC = 3
NG = T // (CH * GC)
TOPK = 128
FILL, TAKEN, NEG = -3.0e38, -3.3e38, -1.0e30
DECAY = -math.exp(-0.5)

G_NORM, G_CONVW, G_CONVB, G_MU, G_W0, G_A0, G_KK, G_KA, G_RK, G_GG, G_GB, G_MLN, G_KVN = (
    0, 48, 80, 88, 102, 106, 110, 114, 118, 122, 126, 130, 134)
G_END = 135

T_R, T_K, T_V, T_WA, T_G = 0, 4, 8, 12, 13
T_MQ, T_MK, T_MV, T_MO = 14, 18, 22, 26
T_DQ, T_CKV, T_QI = 30, 34, 35
NPROJ = 39

QT = [(0, N_META)] + [(N_META + P * j, P) for j in range(SEQ // P)]
ST_ = [(s, min(P, T - s)) for s in range(0, T, P)]


class Chain:

    def __init__(self, eng, s):
        self.eng, self.s, self.n, self.base = eng, s, 0, 0

    def __call__(self, ins):
        self.n += 1
        ins.then_inc(self.s, 1)
        self.eng.wait_ge(self.s, self.base + self.n)

    def enter(self, i, per):
        self.start, self.per = self.n, per
        self.base = i * per

    def leave(self, count):
        assert self.n - self.start == self.per, (self.n - self.start, self.per)
        self.n = self.start + count * self.per
        self.base = 0


def build_program(nc, x, meta_tokens, norm_gain, ffn_w_in, ffn_w_out, w_in, rw_mu, rw_w0, rw_w_up,
                  rw_a0, rw_a_up, rw_g_up, rw_k_k, rw_k_a, rw_r_k, rw_gn_gain, rw_gn_bias, ml_conv_w,
                  ml_conv_b, ml_i_bias, ml_f_bias, ml_norm_gain, dsa_kv_norm, dsa_w_uk, dsa_w_uv,
                  w_branch, w_out, out, debug=None):
    ctx = ExitStack()
    with ctx:
        sems, names, named = [], {}, {}

        def sem(name):
            s = ctx.enter_context(nc.semaphore(name))
            sems.append(s)
            return s

        def S(name):
            if name not in named:
                named[name] = sem(name)
            return named[name]

        def sb(stack, name, shape, dt=F32):
            names[name] = names.get(name, 0) + 1
            return stack.enter_context(nc.sbuf_tensor(f"{name}_{names[name]}", shape, dt))

        PS = ctx.enter_context(nc.psum_tensor("PS", [P, 8, 512], F32))
        h = sb(ctx, "h", [P, KD, T])
        fo = sb(ctx, "fo", [P, KD, T])
        uh = sb(ctx, "u_high", [P, KD, T], F32R)
        ul = sb(ctx, "u_low", [P, KD, T], F32R)
        ident = sb(ctx, "ident", [P, P])
        ones = sb(ctx, "ones", [P, P])
        half_ones = sb(ctx, "half_ones", [P, P])
        causal = sb(ctx, "causal", [P, 5, 64])
        pairmask = sb(ctx, "pairmask", [P, 4, 64])
        eye2 = sb(ctx, "eye2", [P, 64])
        sel = sb(ctx, "sel", [P, 4, P])
        prm = sb(ctx, "prm", [P, G_END])
        rs = sb(ctx, "rs", [P, T])

        dve_own, act_own, pool_own, pe_own = sem("dve_own"), sem("act_own"), sem("pool_own"), sem("pe_own")
        landed = [sem(f"weights_landed{i}") for i in range(4)]
        tile_done = sem("tile_done")
        act_evac, dve_evac = sem("act_evac"), sem("dve_evac")
        loaded, loaded2, stored = sem("loaded"), sem("loaded2"), sem("stored")
        ev = {n: sem(n) for n in (
            "pe_to_act", "pe_to_dve", "act_to_pe", "act_to_dve", "dve_to_pe", "dve_to_act",
            "pool_to_dve", "pool_to_pe", "dve_to_pool", "act_to_pool", "pool_to_act")}

        def weight_buffers(st, units):
            return (sb(st, "W", [P, 2, units, P]), sb(st, "W_high", [P, 2, units, P], F32R),
                    sb(st, "W_low", [P, 2, units, P], F32R))

        def exact(dst, wh, wl, xh, xl, first, final):
            nc.tensor.matmul(dst, wh, xh, start=first, stop=False)
            nc.tensor.matmul(dst, wh, xl, start=False, stop=False)
            return nc.tensor.matmul(dst, wl, xh, start=False, stop=final)

        def high_part(act, n, land, W, WH, w, k):
            act.wait_ge(landed[w], land)
            act.wait_ge(tile_done, n + 1)
            act.sem_inc(S("act_passed"), 1)
            nc.scalar.activation(WH[:, w, 0:k], W[:, w, 0:k], ACT.Copy).then_inc(S("high"), 1)

        def low_part(g, n, W, WH, WL, w, k):
            g.wait_ge(S("high"), n + 1)
            g.sem_inc(S("pool_passed"), 1)
            g.tensor_tensor(WL[:, w, 0:k], W[:, w, 0:k], WH[:, w, 0:k].bitcast(F32), ALU.subtract
                            ).then_inc(S("split"), 1)

        def clear():
            with nc.Block() as block:
                @block.sync
                def _(sp):
                    for s in sems:
                        sp.sem_clear(s)

        def token_sums(src, weights, nw):
            for m in range(4):
                for j, (t0, n) in enumerate(ST_):
                    c = 4 * nw * j + nw * m
                    last = nc.tensor.matmul(PS[0:n, 0, c:c + nw], src(m)[:, t0:t0 + n], weights, start=True, stop=True)
            return last

        def token_sums_out(rq, nw, a, b, op0, op1):
            c = 4 * nw * (len(ST_) - 1)
            n = ST_[-1][1]
            nc.vector.tensor_scalar(rq[:, 0:c], PS[:, 0, 0:c], a, b, op0, op1)
            return nc.vector.tensor_scalar(rq[0:n, c:c + 4 * nw], PS[0:n, 0, c:c + 4 * nw], a, b, op0, op1)

        def token_spread(lhs, m):
            for j, (t0, n) in enumerate(ST_):
                last = nc.tensor.matmul(spread(m)[:, t0:t0 + n], lhs(j)[0:n], ident[0:n, 0:n], start=True, stop=True)
            return last

        def spread(m):
            return PS[:, 2 * m:2 * m + 2].rearrange("p a n -> p (a n)")[:, 0:T]

        def halves(ap):
            return ap.rearrange("p (a n) -> p a n", a=2)

        def phase_start(st):
            xt = sb(st, "xt", [P, 5, D_MODEL])
            with nc.Block() as block:
                @block.sync
                def _(sp):
                    sp.dma_start(xt[0:N_META, 0, :], meta_tokens).then_inc(loaded, 16)
                    for j in range(4):
                        sp.dma_start(xt[:, 1 + j, :], x[0, j * P:(j + 1) * P, :]).then_inc(loaded, 16)

                @block.gpsimd
                def _(g):
                    own = Chain(g, pool_own)
                    own(g.memset(ident[:], 0.0))
                    own(g.affine_select(out=ident[:], in_=ident[:], compare_op=ALU.not_equal, fill=1.0,
                                        base=0, pattern=[[-1, P]], channel_multiplier=1))
                    g.memset(ones[:], 1.0)
                    own(g.memset(half_ones[:], 0.0))
                    for b in (0, 64):
                        own(g.memset(half_ones[b:b + 64, b:b + 64], 1.0))
                        own(g.tensor_copy(eye2[b:b + 64, :], ident[b:b + 64, b:b + 64]))
                    own(g.memset(pairmask[:], 1.0))
                    for b in (0, 64):
                        v = pairmask[b:b + 64]
                        own(g.affine_select(out=v, in_=v, compare_op=ALU.is_ge, fill=0.0, base=0,
                                            pattern=[[-16, 4], [0, 64]], channel_multiplier=1))
                        own(g.affine_select(out=v, in_=v, compare_op=ALU.is_ge, fill=0.0, base=15,
                                            pattern=[[16, 4], [0, 64]], channel_multiplier=-1))
                    own(g.memset(sel[:], 0.0))
                    own(g.affine_select(out=sel[:], in_=sel[:], compare_op=ALU.not_equal, fill=1.0, base=0,
                                        pattern=[[-1, 4], [0, P]], channel_multiplier=1))
                    for kind, (value, step, base) in enumerate(
                            ((-1.0, 1, -1), (-1.0, 1, 0), (1.0, 1, -1), (1.0, 1, 0), (-1.0, -1, -1))):
                        own(g.memset(causal[:, kind, :], value))
                        for b in (0, 64):
                            v = causal[b:b + 64, kind, :]
                            own(g.affine_select(out=v, in_=v, compare_op=ALU.is_ge, fill=0.0, base=base,
                                                pattern=[[step, 64]], channel_multiplier=-step))
                            vv = v.rearrange("p (a b) -> p a b", a=4)
                            own(g.tensor_tensor(vv, vv, pairmask[b:b + 64, :, 0:16], ALU.mult))
                    g.drain().then_inc(ev["pool_to_pe"], 1)

                @block.tensor
                def _(pe):
                    pe.wait_ge(ev["pool_to_pe"], 1)
                    pe.wait_ge(loaded, 80)
                    for f in range(KD):
                        if f >= 4:
                            pe.wait_ge(ev["dve_to_pe"], f - 3)
                        b = 2 * (f % 4)
                        for j, (t0, n) in enumerate(QT):
                            last = nc.tensor.transpose(PS[:, b, t0:t0 + n] if t0 + n <= 400 else
                                                       PS[:, b + 1, t0 - 400:t0 - 400 + n],
                                                       xt[0:n, j, f * P:(f + 1) * P], ident[0:n, 0:n])
                        last.then_inc(ev["pe_to_dve"], 1)

                @block.vector
                def _(v):
                    for f in range(KD):
                        v.wait_ge(ev["pe_to_dve"], f + 1)
                        b = 2 * (f % 4)
                        nc.vector.tensor_copy(h[:, f, 0:400], PS[:, b, 0:400])
                        nc.vector.tensor_copy(h[:, f, 400:T], PS[:, b + 1, 0:T - 400]).then_inc(ev["dve_to_pe"], 1)

        def phase_params(st, l):
            pa = sb(st, "pa", [P, P])
            pb = sb(st, "pb", [P, P])

            def rows(src, n):
                return src.rearrange("a n -> (a n)").rearrange("(k p) -> k p", p=P)

            with nc.Block() as block:
                @block.sync
                def _(sp):
                    sp.dma_start(pa[0:48, :], norm_gain[ds(l, 1)].rearrange("a g (k p) -> (a g k) p", p=P)
                                 ).then_inc(loaded, 16)
                    sp.dma_start(pa[48:80, :], ml_conv_w[ds(l, 1)].rearrange("a g (k p) -> (a g k) p", p=P)
                                 ).then_inc(loaded, 16)
                    sp.dma_start(pa[80:88, :], ml_conv_b[ds(l, 1)].rearrange("a (k p) -> (a k) p", p=P)
                                 ).then_inc(loaded, 16)
                    at = 0
                    for src in (rw_mu, rw_w0, rw_a0, rw_k_k, rw_k_a, None, rw_gn_gain, rw_gn_bias,
                                ml_norm_gain, dsa_kv_norm):
                        if src is None:
                            sp.dma_start(pb[at:at + 4, :], rw_r_k[ds(l, 1)].rearrange(
                                "a (k b) p -> (a k) (b p)", b=2)).then_inc(loaded, 16)
                            at += 4
                            continue
                        n = src.shape[-1] // P
                        sp.dma_start(pb[at:at + n, :], src[ds(l, 1)].rearrange("a (k p) -> (a k) p", p=P)
                                     ).then_inc(loaded, 16)
                        at += n
                    assert at == G_END - G_MU

                @block.tensor
                def _(pe):
                    pe.wait_ge(loaded, 13 * 16)
                    nc.tensor.transpose(PS[:, 0, 0:G_MU], pa[0:G_MU, :], ident[0:G_MU, 0:G_MU])
                    n = G_END - G_MU
                    nc.tensor.transpose(PS[:, 0, G_MU:G_END], pb[0:n, :], ident[0:n, 0:n]
                                        ).then_inc(ev["pe_to_dve"], 1)

                @block.vector
                def _(v):
                    v.wait_ge(ev["pe_to_dve"], 1)
                    nc.vector.tensor_copy(prm[:], PS[:, 0, 0:G_END]).then_inc(dve_own, 1)

        class Norms:

            def __init__(self, st, ring, post, pre):
                self.ring, self.post, self.pre = ring, post, pre
                self.parts = ([fo] if post else []) + ([h] if pre is not None else [])
                self.gs = sb(st, "gs", [P, KD])
                self.rq = sb(st, "rq", [P, 8])
                self.diag = sb(st, "diag", [P, len(ST_), P])
                self.spread = PS[:, 2:4].rearrange("p a n -> p (a n)")[:, 0:T]

            def scalar(self, act):
                for x, src in enumerate(self.parts):
                    for k in range(KD):
                        if x:
                            act.wait_ge(S("h_odd" if k % 2 else "h_even"), k // 2 + 1)
                        if k >= 4:
                            act.wait_ge(S("added_odd" if k % 2 else "added_even"), 3 * x + k // 2 - 1)
                        nc.scalar.activation(self.ring[k if k < 2 else 2 + k % 2], src[:, k], ACT.Square
                                             ).then_inc(S("squares"), 1)
                    act.wait_ge(S("recip"), x + 1)
                    nc.scalar.activation(self.rq[:], self.rq[:], ACT.Sqrt).then_inc(S("rsqrt"), 1)
                if self.pre is not None:
                    for k in range(KD):
                        act.wait_ge(S("normed"), k + 1)
                        nc.scalar.activation(uh[:, k], self.ring[k % 4], ACT.Copy).then_inc(S("u_high"), 1)

            def tensor(self, pe):
                for x in range(len(self.parts)):
                    for k in range(2):
                        pe.wait_ge(S("added_odd" if k else "added_even"), 3 * x + 3)
                        for j, (t0, n) in enumerate(ST_):
                            last = nc.tensor.matmul(PS[0:n, 0, j:j + 1], self.ring[k][:, t0:t0 + n], ones[:, 0:1],
                                                    start=k == 0 and j == 0, stop=k == 1, skip_group_check=True)
                    last.then_inc(S("summed"), 1)
                    pe.wait_ge(S("diagonal"), x + 1)
                    for j, (t0, n) in enumerate(ST_):
                        last = nc.tensor.matmul(self.spread[:, t0:t0 + n], ones[0:n], self.diag[0:n, j, 0:n],
                                                start=True, stop=True)
                    last.then_inc(S("spread"), 1)
                if self.pre is not None:
                    pe.wait_ge(S("u_even"), KD // 2)
                    pe.wait_ge(S("u_odd"), KD // 2)

            def add_even(self, v, x, k):
                v.wait_ge(S("squares"), KD * x + k + 1)
                if k > 2:
                    v.wait_ge(S("added_even"), 3 * x + k // 2 - 1)
                nc.vector.tensor_tensor(self.ring[0], self.ring[0], self.ring[2], ALU.add
                                        ).then_inc(S("added_even"), 1)

            def add_odd(self, g, x, k):
                g.wait_ge(S("squares"), KD * x + k + 1)
                if k > 3:
                    g.wait_ge(S("added_odd"), 3 * x + k // 2 - 1)
                g.tensor_tensor(self.ring[1], self.ring[1], self.ring[3], ALU.add).then_inc(S("added_odd"), 1)

            def vector(self, v):
                own = Chain(v, S("norm_own"))
                rq, ring = self.rq, self.ring
                full = len(ST_) - 1
                m = ST_[full][1]
                if self.post:
                    gain, scale = self.post
                    nc.vector.tensor_scalar(self.gs[:], prm[:, gain:gain + KD], scale, None, ALU.mult)
                own(nc.vector.memset(rq[:], 1.0))
                for x, src in enumerate(self.parts):
                    if x == 0:
                        for k in range(2, KD, 2):
                            self.add_even(v, x, k)
                    v.wait_ge(S("summed"), x + 1)
                    nc.vector.tensor_scalar(rq[:, 0:full], PS[:, 0, 0:full], 1.0 / D_MODEL, EPS, ALU.mult, ALU.add)
                    own(nc.vector.tensor_scalar(rq[0:m, full:full + 1], PS[0:m, 0, full:full + 1], 1.0 / D_MODEL, EPS,
                                                ALU.mult, ALU.add))
                    nc.vector.reciprocal(rq[:], rq[:]).then_inc(S("recip"), 1)
                    v.wait_ge(S("rsqrt"), x + 1)
                    for j, (t0, n) in enumerate(ST_):
                        last = nc.vector.tensor_scalar(self.diag[0:n, j, 0:n], ident[0:n, 0:n], rq[0:n, j:j + 1],
                                                       None, ALU.mult)
                    last.then_inc(S("diagonal"), 1)
                    v.wait_ge(S("spread"), x + 1)
                    if src is fo:
                        for k in range(KD):
                            nc.vector.scalar_tensor_tensor(out=fo[:, k], in0=fo[:, k], scalar=self.gs[:, k:k + 1],
                                                           in1=self.spread, op0=ALU.mult, op1=ALU.mult
                                                           ).then_inc(S("scaled"), 1)
                            if k % 2:
                                v.wait_ge(S("scaled"), k)
                                nc.vector.tensor_tensor(h[:, k - 1], h[:, k - 1], fo[:, k - 1], ALU.add
                                                        ).then_inc(S("h_even"), 1)
                                if self.pre is not None and k > 4:
                                    self.add_even(v, 1, k - 3)
                        if self.pre is not None:
                            self.add_even(v, 1, KD - 2)
                    else:
                        for k in range(KD):
                            if k >= 4:
                                v.wait_ge(S("u_odd" if k % 2 else "u_even"), (k - 4) // 2 + 1)
                            nc.vector.scalar_tensor_tensor(
                                out=ring[k % 4], in0=h[:, k], scalar=prm[:, self.pre + k:self.pre + k + 1],
                                in1=self.spread, op0=ALU.mult, op1=ALU.mult).then_inc(S("normed"), 1)
                            if k % 2:
                                v.wait_ge(S("u_high"), k)
                                nc.vector.tensor_tensor(ul[:, k - 1], ring[(k - 1) % 4], uh[:, k - 1].bitcast(F32),
                                                        ALU.subtract).then_inc(S("u_even"), 1)

            def gpsimd(self, g):
                for k in range(3, KD, 2):
                    self.add_odd(g, 0, k)
                if self.post:
                    for k in range(1, KD, 2):
                        g.wait_ge(S("scaled"), k + 1)
                        g.tensor_tensor(h[:, k], h[:, k], fo[:, k], ALU.add).then_inc(S("h_odd"), 1)
                        if self.pre is not None and k > 4:
                            self.add_odd(g, 1, k - 2)
                    if self.pre is not None:
                        self.add_odd(g, 1, KD - 1)
                if self.pre is not None:
                    for k in range(1, KD, 2):
                        g.wait_ge(S("u_high"), k + 1)
                        g.tensor_tensor(ul[:, k], self.ring[k % 4], uh[:, k].bitcast(F32), ALU.subtract
                                        ).then_inc(S("u_odd"), 1)

        def phase_post_norm(st, post):
            ring = sb(st, "ring", [P, 4, T])
            norms = Norms(st, [ring[:, i] for i in range(4)], post, None)
            with nc.Block() as block:
                @block.scalar
                def _(act):
                    norms.scalar(act)

                @block.tensor
                def _(pe):
                    norms.tensor(pe)

                @block.vector
                def _(v):
                    norms.vector(v)

                @block.gpsimd
                def _(g):
                    norms.gpsimd(g)

        def phase_ffn_in(hh, hl, l, which, post, pre):
            with ExitStack() as st:
                W, WH, WL = weight_buffers(st, KD)
                sg = sb(st, "sg", [P, 2, T])
                hid = sb(st, "hid", [P, 2, T])
                wi = ffn_w_in[ds(l, 1), which].rearrange("a (k p) n -> p (a k) n", p=P)
                NI = KF // 2
                norms = Norms(st, [sg[:, 0], sg[:, 1], hid[:, 0], hid[:, 1]], post, pre)
                with nc.Block() as block:
                    @block.sync
                    def _(sp):
                        sp.sem_inc(S("split"), 2)
                        with sp.Fori(0, NI) as i:
                            for s in range(4):
                                c = sp.snap((2 * i + s // 2) * P + (s % 2) * D_FF)
                                sp.wait_ge(S("split"), 4 * i + s + 1)
                                sp.sem_inc(S("asked"), 1)
                                sp.dma_start(W[:, s % 2], wi[:, :, ds(c, P)]).then_inc(landed[s % 2], 16)

                    @block.gpsimd
                    def _(g):
                        norms.gpsimd(g)
                        with g.Fori(0, NI) as i:
                            for s in range(4):
                                low_part(g, 4 * i + s, W, WH, WL, s % 2, KD)

                    @block.tensor
                    def _(pe):
                        norms.tensor(pe)
                        pe.sem_inc(tile_done, 2)
                        pe.sem_inc(act_evac, 2)
                        pe.sem_inc(dve_evac, 2)
                        with pe.Fori(0, NI) as i:
                            for s in range(4):
                                pe.wait_ge(S("split"), 4 * i + s + 3)
                                pe.wait_ge(dve_evac if s % 2 else act_evac, 2 * i + s // 2 + 1)
                                for k in range(KD):
                                    for a in range(2):
                                        half = slice(a * H2, (a + 1) * H2)
                                        last = exact(PS[:, 2 * s + a, 0:H2], WH[:, s % 2, k], WL[:, s % 2, k],
                                                     uh[:, k, half], ul[:, k, half], k == 0, k == KD - 1)
                                last.then_inc(tile_done, 1)

                    @block.scalar
                    def _(act):
                        norms.scalar(act)
                        with act.Fori(0, NI) as i:
                            for s in range(4):
                                high_part(act, 4 * i + s, 32 * i + 16 * (s // 2) + 16, W, WH, s % 2, KD)
                                if s % 2:
                                    j = s // 2
                                    act.wait_ge(tile_done, 4 * i + 2 * j + 3)
                                    act.wait_ge(dve_evac, 2 * i + j + 1)
                                    nc.scalar.activation(halves(sg[:, j]), PS[:, 4 * j:4 * j + 2, 0:H2], ACT.Silu
                                                         ).then_inc(act_evac, 1)

                    @block.vector
                    def _(v):
                        norms.vector(v)
                        v.sem_inc(S("hidden_low"), 2)
                        with v.Fori(0, NI) as i:
                            for j in range(2):
                                v.wait_ge(tile_done, 4 * i + 2 * j + 4)
                                v.wait_ge(act_evac, 2 * i + j + 3)
                                v.wait_ge(S("hidden_low"), 2 * i + j + 1)
                                nc.vector.tensor_tensor(halves(hid[:, j]), PS[:, 4 * j + 2:4 * j + 4, 0:H2],
                                                        halves(sg[:, j]), ALU.mult).then_inc(dve_evac, 1)
                                v.wait_ge(dve_evac, 2 * i + j + 3)
                                part = lambda t: t[:, ds(2 * i + j, 1), :].rearrange("p a n -> p (a n)")
                                nc.vector.tensor_copy(part(hh), hid[:, j]).then_inc(S("hidden_high"), 1)
                                v.wait_ge(S("hidden_high"), 2 * i + j + 1)
                                nc.vector.tensor_tensor(part(hl), hid[:, j], part(hh).bitcast(F32), ALU.subtract
                                                        ).then_inc(S("hidden_low"), 1)
            clear()

        def phase_ffn_out(hh, hl, l, which):
            with ExitStack() as st:
                KH = KF // 2
                W, WH, WL = weight_buffers(st, KH)
                wo = ffn_w_out[ds(l, 1), which].rearrange("a (k p) n -> p (a k) n", p=P)
                NI = KD // 2
                with nc.Block() as block:
                    @block.sync
                    def _(sp):
                        sp.sem_inc(S("split"), 2)
                        with sp.Fori(0, NI) as i:
                            for s in range(4):
                                c = sp.snap((2 * i + s // 2) * P)
                                sp.wait_ge(S("split"), 4 * i + s + 1)
                                sp.sem_inc(S("asked"), 1)
                                k0 = (s % 2) * KH
                                sp.dma_start(W[:, s % 2], wo[:, k0:k0 + KH, ds(c, P)]).then_inc(landed[s % 2], 16)

                    @block.gpsimd
                    def _(g):
                        with g.Fori(0, NI) as i:
                            for s in range(4):
                                low_part(g, 4 * i + s, W, WH, WL, s % 2, KH)

                    @block.scalar
                    def _(act):
                        with act.Fori(0, NI) as i:
                            for s in range(4):
                                high_part(act, 4 * i + s, 32 * i + 16 * (s // 2) + 16, W, WH, s % 2, KH)

                    @block.tensor
                    def _(pe):
                        pe.sem_inc(tile_done, 2)
                        pe.sem_inc(dve_evac, 2)
                        with pe.Fori(0, NI) as i:
                            for s in range(4):
                                pe.wait_ge(S("split"), 4 * i + s + 3)
                                if s % 2 == 0:
                                    pe.wait_ge(dve_evac, 2 * i + s // 2 + 1)
                                for k in range(KH):
                                    for a in range(2):
                                        half = slice(a * H2, (a + 1) * H2)
                                        kk = (s % 2) * KH + k
                                        last = exact(PS[:, 2 * (s // 2) + a, 0:H2], WH[:, s % 2, k], WL[:, s % 2, k],
                                                     hh[:, kk, half], hl[:, kk, half], kk == 0, kk == KF - 1)
                                last.then_inc(tile_done, 1)

                    @block.vector
                    def _(v):
                        with v.Fori(0, NI) as i:
                            for j in range(2):
                                v.wait_ge(tile_done, 4 * i + 2 * j + 4)
                                nc.vector.tensor_copy(
                                    fo[:, ds(2 * i + j, 1), :].rearrange("p a (b n) -> p (a b) n", b=2),
                                    PS[:, 2 * j:2 * j + 2, 0:H2]).then_inc(dve_evac, 1)
            clear()

        def phase_proj(pj, tok, w, xh, xl, l, c0, n, small_too, post=None, pre=None):
            with ExitStack() as st:
                W, WH, WL = weight_buffers(st, KD + 1)
                wv = w[ds(l, 1)].rearrange("a (k p) n -> p (a k) n", p=P)
                NI = n // 2
                flatw = lambda t, w: t[:, w].rearrange("p a b -> p (a b)").rearrange("p (k c) -> p k c", k=KD)
                w_small = n % 2
                if post:
                    ring = sb(st, "ring", [P, 4, T])
                    norms = Norms(st, [ring[:, i] for i in range(4)], post, pre)
                with nc.Block() as block:
                    @block.sync
                    def _(sp):
                        sp.sem_inc(S("split"), 2)
                        with sp.Fori(0, NI) as i:
                            for s in range(2):
                                c = sp.snap((2 * i + s) * P + c0)
                                sp.wait_ge(S("split"), 2 * i + s + 1)
                                sp.sem_inc(S("asked"), 1)
                                sp.dma_start(W[:, s, 0:KD], wv[:, :, ds(c, P)]).then_inc(landed[s], 16)
                        if n % 2:
                            sp.wait_ge(S("split"), n)
                            sp.dma_start(W[:, 0, 0:KD], wv[:, :, c0 + (n - 1) * P:c0 + n * P]
                                         ).then_inc(landed[0], 16)
                        if small_too:
                            sp.wait_ge(S("split"), n + 1)
                            for a, b, c in ((0, 64, C_KIDX), (64, 136, C_KIDX), (136, 144, C_IG)):
                                sp.dma_start(flatw(W, w_small)[:, :, a:b], wv[:, :, c:c + b - a]
                                             ).then_inc(landed[w_small], 16)

                    @block.gpsimd
                    def _(g):
                        if post:
                            norms.gpsimd(g)
                        with g.Fori(0, NI) as i:
                            for s in range(2):
                                low_part(g, 2 * i + s, W, WH, WL, s, KD)
                        if n % 2:
                            low_part(g, n - 1, W, WH, WL, 0, KD)
                        if small_too:
                            low_part(g, n, W, WH, WL, w_small, KD + 1)

                    @block.scalar
                    def _(act):
                        if post:
                            norms.scalar(act)
                        with act.Fori(0, NI) as i:
                            for s in range(2):
                                high_part(act, 2 * i + s, 16 * i + 16, W, WH, s, KD)
                        if n % 2:
                            high_part(act, n - 1, 16 * NI + 16, W, WH, 0, KD)
                        if small_too:
                            high_part(act, n, 16 * (n // 2) + 48, W, WH, w_small, KD + 1)

                    @block.tensor
                    def _(pe):
                        if post:
                            norms.tensor(pe)
                        pe.sem_inc(tile_done, 2)
                        pe.sem_inc(dve_evac, 2)

                        def tile(t, s, weights):
                            pe.wait_ge(S("split"), t + 3)
                            pe.wait_ge(dve_evac, t + 1)
                            for k in range(KD):
                                for a in range(2):
                                    half = slice(a * H2, (a + 1) * H2)
                                    last = exact(PS[:, 2 * s + a, 0:H2], weights(WH, k), weights(WL, k),
                                                 xh[:, k, half], xl[:, k, half], k == 0, k == KD - 1)
                            last.then_inc(tile_done, 1)

                        with pe.Fori(0, NI) as i:
                            for s in range(2):
                                tile(2 * i + s, s, lambda t, k: t[:, s, k])
                        if n % 2:
                            tile(n - 1, 0, lambda t, k: t[:, 0, k])
                        if small_too:
                            tile(n, w_small, lambda t, k: flatw(t, w_small)[:, k, 0:P])
                            for j, (t0, m) in enumerate(QT):
                                for k in range(KD):
                                    sm = lambda t: flatw(t, w_small)[:, k, P:P + 16]
                                    tk = lambda t: t[:, k, t0:t0 + P]
                                    last = exact(PS[:, 4, 16 * j:16 * j + 16], tk(xh), tk(xl), sm(WH), sm(WL),
                                                 k == 0, k == KD - 1)
                            last.then_inc(tile_done, 1)

                    @block.vector
                    def _(v):
                        if post:
                            norms.vector(v)
                        with v.Fori(0, NI) as i:
                            for s in range(2):
                                v.wait_ge(tile_done, 2 * i + s + 3)
                                nc.vector.tensor_copy(
                                    pj[:, ds(2 * i + s, 1), :].rearrange("p a (b n) -> p (a b) n", b=2),
                                    PS[:, 2 * s:2 * s + 2, 0:H2]).then_inc(dve_evac, 1)
                        for t in range(2 * NI, n + small_too):
                            v.wait_ge(tile_done, t + 3)
                            s = t % 2
                            nc.vector.tensor_copy(halves(pj[:, t]), PS[:, 2 * s:2 * s + 2, 0:H2]
                                                  ).then_inc(dve_evac, 1)
                        if small_too:
                            v.wait_ge(tile_done, n + 4)
                            for j, (t0, m) in enumerate(QT):
                                nc.vector.tensor_copy(tok[0:m, j, :], PS[0:m, 4, 16 * j:16 * j + 16]
                                                      ).then_inc(dve_evac, 1)
            clear()

        def phase_merge(y_of, mh, ml, l, st):
            acc = sb(st, "acc", [P, 3, T])
            gt = sb(st, "gt", [P, 3, T])
            W, WH, WL = weight_buffers(st, KD)
            WB = sb(st, "W_branch", [P, 2, 3 * BW // P, P])
            wv = w_in[ds(l, 1)].rearrange("a (k p) n -> p (a k) n", p=P)
            wb = w_branch[ds(l, 1)].rearrange("a g (k p) n -> p (a g k) n", p=P)
            NI = KD // 2
            with nc.Block() as block:
                @block.sync
                def _(sp):
                    sp.sem_inc(S("split"), 2)
                    sp.sem_inc(S("projected"), 2)
                    with sp.Fori(0, NI) as i:
                        for s in range(6):
                            c = sp.snap(2 * P * i + (s // 3) * P + C_GATE + (s % 3) * D_MODEL)
                            sp.wait_ge(S("split"), 6 * i + s + 1)
                            sp.sem_inc(S("asked"), 1)
                            sp.dma_start(W[:, s % 2], wv[:, :, ds(c, P)]).then_inc(landed[s % 2], 16)
                            if s % 3 == 0:
                                c = sp.snap(2 * P * i + (s // 3) * P)
                                sp.wait_ge(S("projected"), 2 * i + s // 3 + 1)
                                sp.sem_inc(S("asked"), 1)
                                sp.dma_start(WB[:, s // 3], wb[:, :, ds(c, P)]).then_inc(landed[2 + s // 3], 16)

                @block.gpsimd
                def _(g):
                    with g.Fori(0, NI) as i:
                        for s in range(6):
                            low_part(g, 6 * i + s, W, WH, WL, s % 2, KD)

                @block.scalar
                def _(act):
                    def gate(i, s):
                        act.wait_ge(tile_done, 6 * i + s + 3)
                        act.wait_ge(dve_evac, 6 * i + 3 * (s // 3) + 2)
                        nc.scalar.activation(halves(gt[:, s % 3]), PS[:, 2 * (s % 3):2 * (s % 3) + 2, 0:H2],
                                             ACT.Sigmoid).then_inc(act_evac, 1)

                    with act.Fori(0, NI) as i:
                        for s in range(6):
                            high_part(act, 6 * i + s, 48 * i + 16 * (s // 2) + 16, W, WH, s % 2, KD)
                            if s:
                                gate(i, s - 1)
                        gate(i, 5)

                @block.tensor
                def _(pe):
                    pe.sem_inc(tile_done, 2)
                    pe.sem_inc(act_evac, 3)
                    pe.sem_inc(dve_evac, 2)
                    with pe.Fori(0, NI) as i:
                        for m in range(2):
                            for s in range(3):
                                n, w = 3 * m + s, (3 * m + s) % 2
                                pe.wait_ge(S("split"), 6 * i + n + 3)
                                pe.wait_ge(act_evac, 6 * i + n + 1)
                                if s < 2:
                                    pe.wait_ge(dve_evac, 6 * i + 3 * m + s + 1)
                                for k in range(KD):
                                    for a in range(2):
                                        half = slice(a * H2, (a + 1) * H2)
                                        last = exact(PS[:, 2 * s + a, 0:H2], WH[:, w, k], WL[:, w, k],
                                                     uh[:, k, half], ul[:, k, half], k == 0, k == KD - 1)
                                last.then_inc(tile_done, 1)
                            pe.wait_ge(landed[2 + m], 16 * i + 16)
                            for s in range(3):
                                if s:
                                    pe.wait_ge(act_evac, 6 * i + 3 * m + s + 3)
                                for k in range(4):
                                    for a in range(2):
                                        last = nc.tensor.matmul(PS[:, (6, 0, 2)[s] + a, 0:H2], WB[:, m, 4 * s + k],
                                                                y_of[s][:, k, a * H2:(a + 1) * H2],
                                                                start=k == 0, stop=k == 3)
                                last.then_inc(S("projected") if s == 2 else S("product"), 1)

                @block.vector
                def _(v):
                    with v.Fori(0, NI) as i:
                        for m in range(2):
                            for s in range(3):
                                if s < 2:
                                    v.wait_ge(S("product"), 4 * i + 2 * m + s + 1)
                                else:
                                    v.wait_ge(S("projected"), 2 * i + m + 3)
                                v.wait_ge(act_evac, 6 * i + 3 * m + s + 4)
                                b = (6, 0, 2)[s]
                                nc.vector.tensor_tensor(halves(acc[:, s]), PS[:, b:b + 2, 0:H2], halves(gt[:, s]),
                                                        ALU.mult).then_inc(dve_evac, 1)
                            v.wait_ge(dve_evac, 6 * i + 3 * m + 4)
                            nc.vector.tensor_tensor(acc[:, 0], acc[:, 0], acc[:, 1], ALU.add).then_inc(dve_own, 1)
                            v.wait_ge(dve_own, 2 * i + m + 1)
                            v.wait_ge(dve_evac, 6 * i + 3 * m + 5)
                            nc.vector.tensor_tensor(acc[:, 1], acc[:, 0], acc[:, 2], ALU.add
                                                    ).then_inc(S("mixed"), 1)
                            v.wait_ge(S("mixed"), 2 * i + m + 1)
                            part = lambda t: t[:, ds(2 * i + m, 1), :].rearrange("p a n -> p (a n)")
                            nc.vector.tensor_copy(part(mh), acc[:, 1]).then_inc(S("mixed_high"), 1)
                            v.wait_ge(S("mixed_high"), 2 * i + m + 1)
                            nc.vector.tensor_tensor(part(ml), acc[:, 1], part(mh).bitcast(F32), ALU.subtract
                                                    ).then_inc(S("mixed_low"), 1)
                            v.wait_ge(S("mixed_low"), 2 * i + m + 1)

        def phase_end(st):
            ot = sb(st, "ot", [P, 4, D_MODEL])
            with nc.Block() as block:
                @block.tensor
                def _(pe):
                    for j in range(4):
                        for q in range(2):
                            n = 2 * j + q
                            if n >= 4:
                                pe.wait_ge(ev["dve_to_pe"], n - 3)
                            for f in range(4):
                                last = nc.tensor.transpose(PS[:, n % 4, f * P:(f + 1) * P],
                                                           h[:, 4 * q + f, N_META + j * P:N_META + (j + 1) * P],
                                                           ident[:])
                            last.then_inc(ev["pe_to_dve"], 1)

                @block.vector
                def _(v):
                    for n in range(8):
                        v.wait_ge(ev["pe_to_dve"], n + 1)
                        nc.vector.tensor_copy(ot[:, n // 2, (n % 2) * 512:(n % 2) * 512 + 512], PS[:, n % 4, :]
                                              ).then_inc(ev["dve_to_pe"], 1)

                @block.sync
                def _(sp):
                    for j in range(4):
                        sp.wait_ge(ev["dve_to_pe"], 2 * j + 2)
                        sp.dma_start(out[0, j * P:(j + 1) * P, :], ot[:, j, :]).then_inc(stored, 16)
                    sp.wait_ge(stored, 64)

        def phase_rwkv(pj, tok, y_of, l, st):
            s1, s2, s3 = (sb(st, f"rw_s{i}", [P, 4, T]) for i in range(3))
            gup = sb(st, "gup", [P, BW])
            rq = sb(st, "rw_rq", [P, 8 * len(ST_)])
            early = st.enter_context(ExitStack())
            s4 = sb(early, "rw_s3", [P, 4, T])
            lora = sb(early, "lora", [P, BW])
            th = sb(early, "th", [P, T])
            omka = sb(early, "omka", [P, 4])
            wide = sb(early, "wide", [P, 4, len(ST_), P])
            def widen(wide, name):
                for m in range(4):
                    nc.vector.tensor_copy(
                        wide[:, m].rearrange("p j (b n) -> p j b n", b=2),
                        rq[:].rearrange("p (j c) -> p j c", c=8)[:, :, 2 * m:2 * m + 2].unsqueeze(3)
                        .broadcast_to([P, len(ST_), 2, 64])).then_inc(S(name), 1)

            per_parity = half_ones[:].rearrange("p (a b) -> p a b", b=64)[:, :, 0]
            r_, k_, v_ = pj[:, T_R:T_R + 4], pj[:, T_K:T_K + 4], pj[:, T_V:T_V + 4]
            yb, a_, kh = y_of
            fl = lambda t: t.rearrange("p a n -> p (a n)")
            col = lambda c, m: prm[:, c + m:c + m + 1]
            bank2 = lambda m: PS[:, 2 * m:2 * m + 2, 0:H2]

            with nc.Block() as block:
                @block.sync
                def _(sp):
                    for dst, src in ((lora[0:64], rw_w_up), (lora[64:P], rw_a_up), (gup[:], rw_g_up)):
                        sp.dma_start(dst, src[ds(l, 1)].rearrange("a k n -> (a k) n")).then_inc(loaded, 16)

                @block.vector
                def _(v):
                    own = Chain(v, dve_own)
                    for t0, n in ((T_WA, 2), (T_R, 4), (T_K, 4), (T_V, 4)):
                        p = pj[:, t0:t0 + n]
                        own(nc.vector.tensor_tensor(s1[:, 0:n, 1:T], p[:, :, 0:T - 1], p[:, :, 1:T], ALU.subtract))
                        own(nc.vector.tensor_scalar(s1[:, 0:n, 0:1], p[:, :, 0:1], -1.0, None, ALU.mult))
                        for m in range(n):
                            own(nc.vector.scalar_tensor_tensor(
                                out=pj[:, t0 + m], in0=s1[:, m], scalar=col(G_MU, t0 + m), in1=pj[:, t0 + m],
                                op0=ALU.mult, op1=ALU.add))
                        if t0 == T_WA:
                            v.sem_inc(S("inner_mixed"), 1)
                    own(nc.vector.memset(s3[:], 1.0))
                    own(nc.vector.memset(fl(s3[:]).rearrange("p (c t) -> p c t", t=CH)[:, :, 0:1], 0.0))
                    for m in range(4):
                        own(nc.vector.tensor_scalar(kh[:, m], k_[:, m], col(G_KK, m), None, ALU.mult))
                    v.sem_inc(S("kappa"), 1)
                    v.wait_ge(S("sigmoid_w"), 4)
                    own(nc.vector.tensor_scalar(s1[:], s1[:], DECAY, None, ALU.mult))
                    own(nc.vector.tensor_tensor_scan(fl(s2[:]), fl(s3[:]), fl(s1[:]), 0.0, ALU.mult, ALU.add))
                    own(nc.vector.tensor_tensor(s1[:], s2[:], s1[:], ALU.subtract))
                    v.sem_inc(S("logs"), 1)
                    own(nc.vector.memset(rq[:], 1.0))
                    v.wait_ge(S("kappa_sums"), 1)
                    own(token_sums_out(rq, 2, 1e-24, 0.0, ALU.max, ALU.add))
                    own(nc.vector.reciprocal(rq[:], rq[:]))
                    v.sem_inc(S("kappa_recip"), 1)
                    v.wait_ge(S("kappa_rsqrt"), 1)
                    widen(wide, "kappa_wide")
                    for m in range(4):
                        v.wait_ge(S("kappa_spread"), m + 1)
                        own(nc.vector.tensor_tensor(kh[:, m], kh[:, m], spread(m), ALU.mult))
                    own(nc.vector.tensor_scalar(omka[:], prm[:, G_KA:G_KA + 4], -1.0, 1.0, ALU.mult, ALU.add))
                    v.wait_ge(S("sigmoid_a"), 4)
                    for m in range(4):
                        own(nc.vector.tensor_scalar(s4[:, m], a_[:, m], col(G_KA, m), omka[:, m:m + 1],
                                                    ALU.mult, ALU.add))
                    own(nc.vector.tensor_tensor(k_, k_, s4[:], ALU.mult))
                    own(nc.vector.tensor_tensor(a_, a_, kh, ALU.mult))

                @block.scalar
                def _(act):
                    own = Chain(act, act_own)
                    act.wait_ge(S("inner_mixed"), 1)
                    nc.scalar.activation(th[64:P], pj[64:P, T_WA], ACT.Copy)
                    nc.scalar.activation(th[0:64], pj[0:64, T_WA], ACT.Tanh).then_inc(S("th"), 1)
                    nc.scalar.activation(pj[:, T_G], pj[:, T_G], ACT.Sigmoid)
                    act.wait_ge(S("kappa"), 1)
                    for m in range(4):
                        act.wait_ge(S("lora_w"), m + 1)
                        nc.scalar.activation(halves(s1[:, m]), bank2(m), ACT.Sigmoid, bias=col(G_W0, m)
                                             ).then_inc(S("sigmoid_w"), 1)
                    for m in range(4):
                        act.wait_ge(S("lora_a"), m + 1)
                        nc.scalar.activation(halves(a_[:, m]), bank2(m), ACT.Sigmoid, bias=col(G_A0, m)
                                             ).then_inc(S("sigmoid_a"), 1)
                    nc.scalar.activation(s4[:], kh, ACT.Square).then_inc(S("kappa_squares"), 1)
                    act.wait_ge(S("logs"), 1)
                    nc.scalar.activation(s3[:], s2[:], ACT.Exp, scale=-1.0).then_inc(S("exps"), 1)
                    act.wait_ge(S("exps"), 1)
                    nc.scalar.activation(s2[:], s2[:], ACT.Exp)
                    nc.scalar.activation(s1[:], s1[:], ACT.Exp)
                    act.wait_ge(S("kappa_recip"), 1)
                    nc.scalar.activation(rq[:], rq[:], ACT.Sqrt).then_inc(S("kappa_rsqrt"), 1)

                @block.tensor
                def _(pe):
                    pe.wait_ge(loaded, 48)
                    pe.wait_ge(S("th"), 1)
                    for b, name in ((0, "lora_w"), (64, "lora_a")):
                        for m in range(4):
                            if b:
                                pe.wait_ge(S("sigmoid_w"), m + 1)
                            for a in range(2):
                                last = nc.tensor.matmul(PS[:, 2 * m + a, 0:H2], lora[b:b + 64, m * P:(m + 1) * P],
                                                        th[b:b + 64, a * H2:(a + 1) * H2], start=True, stop=True)
                            last.then_inc(S(name), 1)
                    pe.wait_ge(S("kappa_squares"), 1)
                    pe.wait_ge(S("sigmoid_a"), 4)
                    token_sums(lambda m: s4[:, m], per_parity, 2).then_inc(S("kappa_sums"), 1)
                    for m in range(4):
                        pe.wait_ge(S("kappa_wide"), m + 1)
                        token_spread(lambda j: wide[:, m, j], m).then_inc(S("kappa_spread"), 1)
            clear()

            early.close()

            rec = st.enter_context(ExitStack())
            stage = sb(rec, "stage", [P, 2, GC, 7, 64])
            stage_bd = sb(rec, "stage_bd", [P, GC, 3, P])
            sg = sb(rec, "sg", [P, 2, GC, 5, 64])
            tk = sb(rec, "tk", [P, GC, 2, 64])
            v_bd = sb(rec, "v_bd", [P, 2, GC, P])
            tk_bd = sb(rec, "tk_bd", [P, GC, 2, P])
            rr = sb(rec, "rr", [P, GC, P])
            bm, vm, um, mm, nn = (sb(rec, n, [P, GC, 4, 64]) for n in ("bm", "vm", "um", "mm", "nn"))
            n2, n4 = (sb(rec, n, [P, GC, 2, 64]) for n in ("n2", "n4"))
            n8, za, zb, qp = (sb(rec, n, [P, GC, 64]) for n in ("n8", "za", "zb", "qp"))
            xx = sb(rec, "xx", [P, GC, P])
            xx_bd = sb(rec, "xx_bd", [P, GC, 2, P])
            state = sb(rec, "state", [P, 4, 64])
            kC, kB, kP, kQ, kV, kBt, kCt = range(7)
            PAR = ((0, slice(0, 64)), (1, slice(64, P)))
            gw = GC * CH
            tps = PS[:, 3:5].rearrange("p a b -> p (a b)")[:, 0:768].rearrange("p (c k n) -> p c k n", c=GC, k=4)
            nps = PS[:, 5, 0:GC * P].rearrange("p (c k n) -> p c k n", c=GC, k=2)
            wps = PS[:, 0, 0:GC * 64].rearrange("p (c n) -> p c n", c=GC)
            zps = PS[:, 1, 256:256 + GC * 64].rearrange("p (c n) -> p c n", c=GC)
            sps = PS[:, 6, 0:256].rearrange("p (a n) -> p a n", a=4)
            yps = PS[:, 7, 0:GC * 64].rearrange("p (c n) -> p c n", c=GC)
            n_ps = (PS[:, 3, 0:256], PS[:, 3, 256:512], PS[:, 4, 0:256])
            flat = lambda t: t.rearrange("p a n -> p (a n)")

            with nc.Block() as block:
                @block.vector
                def _(v):
                    own = Chain(v, dve_own)
                    tt = nc.vector.tensor_tensor

                    def stage_now(g, s):
                        grp = lambda t: t[:, :, ds(g * gw, gw)].rearrange("p a (c t) -> p c a t", c=GC)
                        for kind, a, b in ((kC, k_, s3[:]), (kB, a_, s3[:]), (kP, kh, s1[:]), (kQ, r_, s2[:])):
                            for c in range(GC):
                                last = tt(stage[:, s, c, kind].rearrange("p (a t) -> p a t", a=4),
                                          grp(a)[:, c], grp(b)[:, c], ALU.mult)
                        own(last)
                        v.sem_inc(S("staged"), 1)

                    def stage_rest(g, s):
                        grp = lambda t: t[:, :, ds(g * gw, gw)].rearrange("p a (c t) -> p c a t", c=GC)
                        stg = lambda c, kind: stage[:, s, c, kind].rearrange("p (a t) -> p a t", a=4)
                        for c in range(GC):
                            w = grp(s2[:])[:, c, :, CH - 1:CH].broadcast_to([P, 4, CH])
                            nc.vector.tensor_copy(stg(c, kV), grp(v_)[:, c])
                            nc.vector.scalar_tensor_tensor(out=stg(c, kBt), in0=stg(c, kB), scalar=-1.0, in1=w,
                                                           op0=ALU.mult, op1=ALU.mult)
                            last = tt(stg(c, kCt), stg(c, kC), w, ALU.mult)
                        last.then_inc(S("staged_rest"), 1)

                    def add_inputs(p, c):
                        v.wait_ge(S("stepped"), GC * p + c + 1)
                        if c == 0:
                            v.wait_ge(S("inputs_out"), p + 1)
                        tt(state[:], sps, nn[:, c], ALU.add).then_inc(S("state"), 1)

                    def group(g, s, prev, nxt):
                        if nxt:
                            if prev:
                                v.wait_ge(S("turned"), g)
                            stage_now(g + 1, 1 - s)
                        if prev:
                            add_inputs(g - 1, 0)
                        v.wait_ge(S("products"), g + 1)
                        tt(sg[:, s].rearrange("p c k n -> p c (k n)"), PS[:, 0:GC, 0:320],
                           flat(causal[:]).unsqueeze(1).broadcast_to([P, GC, 320]), ALU.mult
                           ).then_inc(S("masked"), 1)
                        v.wait_ge(S("masked"), g + 1)
                        own(tt(za[:], sg[:, s, :, 0], eye2[:].unsqueeze(1).broadcast_to([P, GC, 64]), ALU.add))
                        if prev:
                            add_inputs(g - 1, 1)
                        v.wait_ge(S("squared"), 3 * g + 1)
                        own(nc.vector.tensor_copy(n2[:], nps))
                        v.sem_inc(S("powers"), 1)
                        v.wait_ge(S("squared"), 3 * g + 2)
                        nc.vector.tensor_copy(n4[:], nps)
                        own(tt(zb[:], zps, za[:], ALU.add))
                        v.sem_inc(S("powers"), 1)
                        if prev:
                            add_inputs(g - 1, 2)
                        for c in range(GC):
                            w = s2[:, :, ds(g * gw + (c + 1) * CH - 1, 1)]
                            tt(mm[:, c], eye2[:].unsqueeze(1).broadcast_to([P, 4, 64]),
                               w.broadcast_to([P, 4, 64]), ALU.mult)
                        v.wait_ge(S("squared"), 3 * g + 3)
                        nc.vector.tensor_copy(n8[:], nps[:, :, 0])
                        own(tt(za[:], zps, zb[:], ALU.add))
                        v.sem_inc(S("powers"), 1)
                        v.wait_ge(S("last_factor"), g + 1)
                        tt(zb[:], zps, za[:], ALU.add).then_inc(S("inverse"), 1)
                        if nxt:
                            stage_rest(g + 1, 1 - s)
                        v.wait_ge(S("solution"), g + 1)
                        tt(um[:], xx[:, :, 64:P].unsqueeze(2).broadcast_to([P, GC, 4, 64]),
                           pairmask[:].unsqueeze(1).broadcast_to([P, GC, 4, 64]), ALU.mult
                           ).then_inc(S("solution_masked"), 1)
                        v.wait_ge(S("transfer"), g + 1)
                        tt(qp[:], zps, stage[:, s, :, kQ], ALU.add)
                        own(tt(mm[:].rearrange("p c a n -> p c (a n)"), mm[:].rearrange("p c a n -> p c (a n)"),
                               PS[:, 0:GC, 0:256], ALU.add))
                        v.sem_inc(S("transfer_out"), 1)

                    nc.vector.memset(state[:], 0.0).then_inc(S("state"), 1)
                    stage_now(0, 0)
                    stage_rest(0, 0)
                    group(0, 0, False, True)
                    with v.Fori(0, (NG - 3) // 2) as i:
                        own.enter(i, 12)
                        group(2 * i + 1, 1, True, True)
                        group(2 * i + 2, 0, True, True)
                    own.leave((NG - 3) // 2)
                    group(NG - 2, 1, True, True)
                    group(NG - 1, 0, True, False)
                    for c in range(GC):
                        add_inputs(NG - 1, c)

                @block.scalar
                def _(act):
                    copy = lambda dst, src: nc.scalar.activation(dst, src, ACT.Copy)

                    def stage_diagonal(g, s):
                        act.wait_ge(S("staged"), g + 1)
                        for b, sl in PAR:
                            last = copy(stage_bd[sl, :, :, sl], stage[sl, s, :, kC:kP + 1])
                        last.then_inc(S("staged_diagonal"), 1)

                    def y_out(p):
                        act.wait_ge(S("stepped"), GC * p + GC)
                        for c in range(GC):
                            last = copy(yb[:, 0:4, ds(p * gw + c * CH, CH)],
                                        yps[:, c].rearrange("p (a t) -> p a t", a=4))
                        last.then_inc(S("y_out"), 1)

                    def group(g, s, prev, nxt):
                        act.wait_ge(S("turned"), g + 1)
                        copy(tk[:], tps[:, :, 1:3])
                        copy(rr[:, :, 0:64], tps[:, :, 0]).then_inc(S("rows"), 1)
                        for b, sl in PAR:
                            copy(v_bd[sl, s, :, sl], tps[sl, :, 1])
                            last = copy(tk_bd[sl, :, :, sl], tps[sl, :, 2:4])
                        last.then_inc(S("rows_diagonal"), 1)
                        act.wait_ge(S("read_in"), g + 1)
                        copy(rr[:, :, 64:P], wps).then_inc(S("sides"), 1)
                        if prev:
                            y_out(g - 1)
                        if nxt:
                            stage_diagonal(g + 1, 1 - s)
                        act.wait_ge(S("solved"), g + 1)
                        solved = PS[:, 5, 0:GC * P].rearrange("p (c n) -> p c n", c=GC)
                        copy(xx[:], solved).then_inc(S("solution"), 1)
                        for b, sl in PAR:
                            last = copy(xx_bd[sl, :, :, sl], solved[sl].rearrange("p c (k n) -> p c k n", k=2))
                        last.then_inc(S("solution_diagonal"), 1)
                        act.wait_ge(S("inputs"), g + 1)
                        copy(nn[:].rearrange("p c a n -> p (c a n)"),
                             PS[:, 3:5].rearrange("p a b -> p (a b)")[:, 0:768]).then_inc(S("inputs_out"), 1)

                    act.wait_ge(S("zeros"), 1)
                    stage_diagonal(0, 0)
                    group(0, 0, False, True)
                    with act.Fori(0, (NG - 3) // 2) as i:
                        group(2 * i + 1, 1, True, True)
                        group(2 * i + 2, 0, True, True)
                    group(NG - 2, 1, True, True)
                    group(NG - 1, 0, True, False)
                    y_out(NG - 1)

                @block.gpsimd
                def _(g):
                    for t in (stage_bd, v_bd, tk_bd, xx_bd):
                        last = g.memset(t[:], 0.0)
                    last.then_inc(S("zeros"), 1)
                    msk = pairmask[:].unsqueeze(1).broadcast_to([P, GC, 4, 64])
                    with g.Fori(0, NG) as i:
                        g.wait_ge(S("rows"), i + 1)
                        g.sem_inc(S("pool_passed"), 1)
                        g.tensor_tensor(bm[:], tk[:, :, 1].unsqueeze(2).broadcast_to([P, GC, 4, 64]), msk, ALU.mult)
                        g.tensor_tensor(vm[:], tk[:, :, 0].unsqueeze(2).broadcast_to([P, GC, 4, 64]), msk, ALU.mult
                                        ).then_inc(S("rows_masked"), 1)

                @block.tensor
                def _(pe):
                    mmul = nc.tensor.matmul

                    def whole(dst, lhs, rhs, start=True, stop=True):
                        return mmul(dst, lhs, rhs, start=start, stop=stop, skip_group_check=True)

                    def both(fn):
                        for b, sl in PAR:
                            last = fn(sl)
                        return last

                    def wait(name, value):
                        pe.wait_ge(S(name), value)
                        pe.sem_inc(S("pe_passed"), 1)

                    def step(p, s, c):
                        if c == 0:
                            wait("y_out", p + 1)
                            wait("transfer_out", p + 1)
                        whole(yps[:, c], v_bd[:, s, c], sg[:, s, c, 3], stop=False)
                        whole(yps[:, c], xx_bd[:, c, 1], sg[:, s, c, 1], start=False, stop=False)
                        wait("state", GC * p + c + 1)
                        for a in range(4):
                            both(lambda sl: mmul(sps[sl, a], mm[sl, c, a], state[sl, a],
                                                 start=True, stop=True))
                        for a in range(4):
                            last = both(lambda sl: mmul(yps[sl, c, a * CH:(a + 1) * CH], state[sl, a],
                                                        qp[sl, c, a * CH:(a + 1) * CH], start=False,
                                                        stop=a == 3, skip_group_check=True))
                        last.then_inc(S("stepped"), 1)

                    def group(g, s, prev, nxt):
                        if prev:
                            step(g - 1, 1 - s, 0)
                        wait("staged_diagonal", g + 1)
                        for c in range(GC):
                            for k, rhs, c0, n in ((1, slice(kP, kQ + 1), 0, 128), (0, slice(kP, kQ + 1), 128, 128),
                                                  (2, slice(kB, kB + 1), 256, 64)):
                                last = whole(PS[:, c, c0:c0 + n], stage_bd[:, c, k], flat(stage[:, s, c, rhs]))
                        last.then_inc(S("products"), 1)
                        if prev:
                            wait("inputs_out", g)
                        wait("staged_rest", g + 1)
                        for c in range(GC):
                            whole(tps[:, c, 0], stage_bd[:, c, 2], eye2[:])
                            for k, kind in ((1, kV), (2, kBt), (3, kCt)):
                                last = both(lambda sl: mmul(tps[sl, c, k], stage[sl, s, c, kind], eye2[sl],
                                                            start=True, stop=True))
                        last.then_inc(S("turned"), 1)
                        if prev:
                            step(g - 1, 1 - s, 1)
                        wait("masked", g + 1)
                        for c in range(GC):
                            both(lambda sl: mmul(nps[sl, c, 0], sg[sl, s, c, 0], sg[sl, s, c, 4],
                                                 start=True, stop=True))
                            last = both(lambda sl: mmul(nps[sl, c, 1], sg[sl, s, c, 4], sg[sl, s, c, 0],
                                                        start=True, stop=True))
                        last.then_inc(S("squared"), 1)
                        wait("rows", g + 1)
                        for c in range(GC):
                            last = both(lambda sl: mmul(wps[sl, c], sg[sl, s, c, 2], tk[sl, c, 0],
                                                        start=True, stop=True))
                        last.then_inc(S("read_in"), 1)
                        wait("powers", 3 * g + 1)
                        for c in range(GC):
                            both(lambda sl: mmul(nps[sl, c, 0], n2[sl, c, 1], n2[sl, c, 0], start=True, stop=True))
                            both(lambda sl: mmul(nps[sl, c, 1], n2[sl, c, 0], n2[sl, c, 1], start=True, stop=True))
                            last = both(lambda sl: mmul(zps[sl, c], n2[sl, c, 0], za[sl, c], start=True, stop=True))
                        last.then_inc(S("squared"), 1)
                        if prev:
                            step(g - 1, 1 - s, 2)
                        wait("powers", 3 * g + 2)
                        for c in range(GC):
                            both(lambda sl: mmul(nps[sl, c, 0], n4[sl, c, 1], n4[sl, c, 0], start=True, stop=True))
                            last = both(lambda sl: mmul(zps[sl, c], n4[sl, c, 0], zb[sl, c], start=True, stop=True))
                        last.then_inc(S("squared"), 1)
                        wait("powers", 3 * g + 3)
                        for c in range(GC):
                            last = both(lambda sl: mmul(zps[sl, c], n8[sl, c], za[sl, c], start=True, stop=True))
                        last.then_inc(S("last_factor"), 1)
                        wait("sides", g + 1)
                        wait("inverse", g + 1)
                        for c in range(GC):
                            last = both(lambda sl: mmul(PS[sl, 5, c * P:(c + 1) * P], zb[sl, c], rr[sl, c],
                                                        start=True, stop=True))
                        last.then_inc(S("solved"), 1)
                        wait("rows_diagonal", g + 1)
                        wait("rows_masked", g + 1)
                        for c in range(GC):
                            whole(n_ps[c], tk_bd[:, c, 1], flat(vm[:, c]), start=c != 1, stop=False)
                        wait("solution_diagonal", g + 1)
                        for c in range(GC):
                            whole(zps[:, c], xx_bd[:, c, 0], sg[:, s, c, 1])
                            last = whole(PS[:, c, 0:256], xx_bd[:, c, 0], flat(bm[:, c]))
                        last.then_inc(S("transfer"), 1)
                        wait("solution_masked", g + 1)
                        for c in range(GC):
                            last = whole(n_ps[c], tk_bd[:, c, 0], flat(um[:, c]),
                                         start=False)
                        last.then_inc(S("inputs"), 1)

                    pe.sem_inc(S("y_out"), 1)
                    group(0, 0, False, True)
                    with pe.Fori(0, (NG - 3) // 2) as i:
                        group(2 * i + 1, 1, True, True)
                        group(2 * i + 2, 0, True, True)
                    group(NG - 2, 1, True, True)
                    group(NG - 1, 0, True, False)
                    for c in range(GC):
                        step(NG - 1, 0, c)
            clear()
            rec.close()
            wide = sb(st, "wide", [P, 4, len(ST_), P])

            with nc.Block() as block:
                y = yb

                @block.vector
                def _(v):
                    own = Chain(v, dve_own)
                    v.wait_ge(S("sum_y"), 1)
                    for m in range(4):
                        own(nc.vector.tensor_scalar(halves(s1[:, m]), bank2(m), -1.0 / 64, None, ALU.mult))
                    v.sem_inc(S("sum_y_out"), 1)
                    own(nc.vector.tensor_tensor(y, y, s1[:], ALU.add))
                    v.sem_inc(S("centred"), 1)
                    for m in range(4):
                        own(nc.vector.scalar_tensor_tensor(out=s2[:, m], in0=r_[:, m], scalar=col(G_RK, m),
                                                           in1=k_[:, m], op0=ALU.mult, op1=ALU.mult))
                    v.sem_inc(S("bonus_terms"), 1)
                    v.wait_ge(S("sum_sq"), 1)
                    own(token_sums_out(rq, 2, 1.0 / 64, GN_EPS, ALU.mult, ALU.add))
                    own(nc.vector.reciprocal(rq[:], rq[:]))
                    v.sem_inc(S("var_recip"), 1)
                    v.wait_ge(S("var_rsqrt"), 1)
                    widen(wide, "var_wide")
                    for m in range(4):
                        v.wait_ge(S("var_spread"), m + 1)
                        own(nc.vector.tensor_tensor(y[:, m], y[:, m], spread(m), ALU.mult))
                    v.sem_inc(S("scaled_out"), 1)
                    for m in range(4):
                        own(nc.vector.tensor_scalar(y[:, m], y[:, m], col(G_GG, m), col(G_GB, m), ALU.mult, ALU.add))
                    v.wait_ge(S("sum_bonus"), 1)
                    for m in range(4):
                        own(nc.vector.tensor_tensor(halves(s1[:, m]), bank2(m), halves(v_[:, m]), ALU.mult))
                    v.sem_inc(S("sum_bonus_out"), 1)
                    own(nc.vector.tensor_tensor(y, y, s1[:], ALU.add))
                    v.wait_ge(S("gates"), 1)
                    for m in range(4):
                        own(nc.vector.tensor_tensor(halves(y[:, m]), bank2(m), halves(y[:, m]), ALU.mult))

                @block.scalar
                def _(act):
                    act.wait_ge(S("centred"), 1)
                    nc.scalar.activation(s3[:], y, ACT.Square).then_inc(S("y_squares"), 1)
                    act.wait_ge(S("var_recip"), 1)
                    nc.scalar.activation(rq[:], rq[:], ACT.Sqrt).then_inc(S("var_rsqrt"), 1)

                @block.tensor
                def _(pe):
                    def sums(src, weights, name):
                        for m in range(4):
                            for a in range(2):
                                last = nc.tensor.matmul(PS[:, 2 * m + a, 0:H2], weights(m),
                                                        src(m)[:, a * H2:(a + 1) * H2], start=True, stop=True)
                        last.then_inc(S(name), 1)
                    sums(lambda m: y[:, m], lambda m: half_ones[:], "sum_y")
                    pe.wait_ge(S("y_squares"), 1)
                    pe.wait_ge(S("sum_y_out"), 1)
                    token_sums(lambda m: s3[:, m], per_parity, 2).then_inc(S("sum_sq"), 1)
                    for m in range(4):
                        pe.wait_ge(S("var_wide"), m + 1)
                        token_spread(lambda j: wide[:, m, j], m).then_inc(S("var_spread"), 1)
                    pe.wait_ge(S("bonus_terms"), 1)
                    pe.wait_ge(S("scaled_out"), 1)
                    sums(lambda m: s2[:, m], lambda m: half_ones[:], "sum_bonus")
                    pe.wait_ge(S("sum_bonus_out"), 1)
                    sums(lambda m: pj[:, T_G], lambda m: gup[:, m * P:(m + 1) * P], "gates")

        def phase_dsa(pj, tok, y_of, l, st):
            H = 8
            Q0, CKV, QI, KI = 0, 4, 5, 9
            qlat = sb(st, "qlat", [P, H, T])
            wuk = sb(st, "wuk", [P, 4, P])
            wuv = sb(st, "wuv", [P, H, 64])
            sq = sb(st, "dsa_sq", [P, T])
            ckv_tok = sb(st, "ckv_tok", [P, 5, P])
            wi = sb(st, "wi", [P, 5, H])
            relu = sb(st, "relu", [P, 2, T])
            score = sb(st, "score", [P, T])
            best = sb(st, "best", [P, 8])
            bias = sb(st, "bias", [P, 2, T])
            lg = sb(st, "lg", [P, 2, T])
            pt = sb(st, "pt", [P, 2, 5, P])
            ot = sb(st, "ot_dsa", [P, H, P])
            stat = sb(st, "stat", [P, 2, 4])
            flat = lambda b: PS[:, b:b + 2].rearrange("p a n -> p (a n)")
            ckv = pj[:, CKV]
            NQ = len(QT)

            def spans(nk):
                return ((0, min(nk, 512)),) + (((512, nk),) if nk > 512 else ())

            with nc.Block() as block:
                @block.sync
                def _(sp):
                    for b in range(2):
                        sp.dma_start(wuk[64 * b:64 * b + 64],
                                     dsa_w_uk[ds(l, 1)].rearrange("o (a b) d c -> b d (o a) c", b=2)[b]
                                     ).then_inc(loaded, 16)
                    sp.dma_start(wuv[:], dsa_w_uv[ds(l, 1)].rearrange("o h c d -> c (o h) d")).then_inc(loaded, 16)

                @block.tensor
                def _(pe):
                    pe.wait_ge(S("ckv_squares"), 1)
                    for a in range(2):
                        last = nc.tensor.matmul(PS[:, a, 0:H2], ones[:], sq[:, a * H2:(a + 1) * H2],
                                                start=True, stop=True)
                    last.then_inc(S("ckv_sum"), 1)
                    pe.wait_ge(loaded, 48)
                    for hd in range(H):
                        b, m = 64 * (hd % 2), hd % 3 + 1
                        if hd >= 3:
                            pe.wait_ge(S("qlat"), hd - 2)
                        for a in range(2):
                            last = nc.tensor.matmul(PS[:, 2 * m + a, 0:H2], wuk[b:b + 64, hd // 2],
                                                    pj[b:b + 64, Q0 + hd // 2, a * H2:(a + 1) * H2],
                                                    start=True, stop=True)
                        last.then_inc(S("qlat_made"), 1)
                    pe.wait_ge(S("ckv"), 1)
                    for j, (t0, n) in enumerate(QT):
                        last = nc.tensor.transpose(PS[0:n, j // 4, (j % 4) * P:(j % 4 + 1) * P],
                                                   pj[:, CKV, t0:t0 + n], ident[:])
                    last.then_inc(S("ckv_turned"), 1)

                @block.scalar
                def _(act):
                    nc.scalar.activation(sq[:], ckv, ACT.Square).then_inc(S("ckv_squares"), 1)
                    act.wait_ge(S("ckv_recip"), 1)
                    nc.scalar.activation(rs[:], rs[:], ACT.Sqrt).then_inc(S("ckv_rsqrt"), 1)
                    for hd in range(H):
                        act.wait_ge(S("qlat_made"), hd + 1)
                        m = hd % 3 + 1
                        nc.scalar.activation(halves(qlat[:, hd]), PS[:, 2 * m:2 * m + 2, 0:H2], ACT.Copy,
                                             scale=0.125).then_inc(S("qlat"), 1)

                @block.vector
                def _(v):
                    own = Chain(v, dve_own)
                    v.wait_ge(S("ckv_sum"), 1)
                    own(nc.vector.tensor_scalar(halves(rs[:]), PS[:, 0:2, 0:H2], 1.0 / P, EPS, ALU.mult, ALU.add))
                    nc.vector.reciprocal(rs[:], rs[:]).then_inc(S("ckv_recip"), 1)
                    v.wait_ge(S("ckv_rsqrt"), 1)
                    nc.vector.scalar_tensor_tensor(out=ckv, in0=ckv, scalar=prm[:, G_KVN:G_KVN + 1], in1=rs[:],
                                                   op0=ALU.mult, op1=ALU.mult).then_inc(S("ckv"), 1)
                    for j, (t0, n) in enumerate(QT):
                        nc.vector.tensor_scalar(wi[0:n, j], tok[0:n, j, 0:H], 512.0 ** -0.5, None, ALU.mult)
                    v.wait_ge(S("ckv_turned"), 1)
                    for j, (t0, n) in enumerate(QT):
                        nc.vector.tensor_copy(ckv_tok[0:n, j], PS[0:n, j // 4, (j % 4) * P:(j % 4 + 1) * P])
            clear()

            with nc.Block() as block:
                @block.tensor
                def _(pe):
                    def index(j):
                        t0, n = QT[j]
                        for hd in range(H):
                            s, b, q = (j - 1) * H + hd, 64 * (hd % 2), hd % 2
                            if s >= 2:
                                pe.wait_ge(S("relu"), s - 1)
                            if hd < 2 and j > 1:
                                pe.wait_ge(S("logits_out"), (j - 1) * H)
                            for k0, k1 in spans(t0 + n):
                                last = nc.tensor.matmul(flat(2 * q)[0:n, k0:k1], pj[b:b + 64, QI + hd // 2, t0:t0 + n],
                                                        pj[b:b + 64, KI, k0:k1], start=True, stop=True)
                            last.then_inc(S("index"), 1)

                    for j, (t0, n) in enumerate(QT):
                        nk = t0 + n
                        if j + 1 < NQ:
                            index(j + 1)

                        def logits(hd):
                            e, q = j * H + hd, hd % 2
                            if j + 1 < NQ and hd < 2:
                                pe.wait_ge(S("relu"), (j + 1) * H)
                            if e >= 2:
                                pe.wait_ge(S("logits_out"), e - 1)
                            for k0, k1 in spans(nk):
                                last = nc.tensor.matmul(flat(2 * q)[0:n, k0:k1], qlat[:, hd, t0:t0 + n],
                                                        pj[:, CKV, k0:k1], start=True, stop=True)
                            last.then_inc(S("logits"), 1)

                        def values(hd):
                            e, q = j * H + hd, hd % 2
                            pe.wait_ge(S("probs"), e + 1)
                            if e >= 1:
                                pe.wait_ge(S("probs_turned_out"), e)
                            for m in range(j + 1):
                                k0, kn = QT[m]
                                dst = PS[0:kn, 5, 0:n] if m == 0 else PS[0:kn, 4, (m - 1) * P:(m - 1) * P + n]
                                last = nc.tensor.transpose(dst, lg[0:n, q, k0:k0 + kn], ident[0:n, 0:n])
                            last.then_inc(S("probs_turned"), 1)
                            pe.wait_ge(S("probs_turned_out"), e + 1)
                            if e >= 1:
                                pe.wait_ge(S("value"), e)
                            for m in range(j + 1):
                                k0, kn = QT[m]
                                last = nc.tensor.matmul(PS[:, 6, 0:n], ckv_tok[0:kn, m], pt[0:kn, q, m, 0:n],
                                                        start=m == 0, stop=m == j)
                            last.then_inc(S("value_made"), 1)

                        logits(0)
                        logits(1)
                        for hd in range(H):
                            if hd + 2 < H:
                                logits(hd + 2)
                            values(hd)
                        pe.wait_ge(S("value"), (j + 1) * H)
                        if j:
                            pe.wait_ge(S("y"), j)
                        for hd in range(H):
                            b = 64 * (hd % 2)
                            last = nc.tensor.matmul(PS[b:b + 64, 7, (hd // 2) * P:(hd // 2) * P + n], wuv[:, hd],
                                                    ot[:, hd, 0:n], start=True, stop=True)
                        last.then_inc(S("y_made"), 1)

                @block.scalar
                def _(act):
                    for j, (t0, n) in enumerate(QT):
                        nk = t0 + n
                        for hd in range(H if j + 1 < NQ else 0):
                            s, q = j * H + hd, hd % 2
                            n1, nk1 = QT[j + 1][1], QT[j + 1][0] + QT[j + 1][1]
                            act.wait_ge(S("index"), s + 1)
                            if s >= 2:
                                act.wait_ge(S("scored"), s - 1)
                            nc.scalar.activation(relu[0:n1, q, 0:nk1], flat(2 * q)[0:n1, 0:nk1], ACT.Relu
                                                 ).then_inc(S("relu"), 1)

                        def exponentials(hd):
                            q = hd % 2
                            act.wait_ge(S("max"), j * H + hd + 1)
                            nc.scalar.activation(lg[0:n, q, 0:nk], lg[0:n, q, 0:nk], ACT.Exp,
                                                 bias=stat[0:n, q, 1:2], accum_out=stat[0:n, q, 2:3]
                                                 ).then_inc(S("exp"), 1)

                        exponentials(0)
                        for hd in range(H):
                            e, q = j * H + hd, hd % 2
                            if hd + 1 < H:
                                exponentials(hd + 1)
                            act.wait_ge(S("probs_turned"), e + 1)
                            if e >= 2:
                                act.wait_ge(S("value_made"), e - 1)
                            if j:
                                nc.scalar.activation(pt[:, q, 1:j + 1, 0:n], PS[:, 4, 0:j * P].rearrange(
                                    "p (m n) -> p m n", n=P)[:, :, 0:n], ACT.Copy)
                            nc.scalar.activation(pt[0:N_META, q, 0, 0:n], PS[0:N_META, 5, 0:n], ACT.Copy
                                                 ).then_inc(S("probs_turned_out"), 1)
                            act.wait_ge(S("value_made"), e + 1)
                            if j and hd == 0:
                                act.wait_ge(S("y_made"), j)
                            nc.scalar.activation(ot[:, hd, 0:n], PS[:, 6, 0:n], ACT.Copy).then_inc(S("value"), 1)

                @block.vector
                def _(v):
                    own = Chain(v, dve_own)
                    assert TOPK == 16 * H

                    def scores(j):
                        n, nk = QT[j][1], sum(QT[j])
                        for hd in range(H):
                            s, q = (j - 1) * H + hd, hd % 2
                            v.wait_ge(S("relu"), s + 1)
                            if hd == 0:
                                own(nc.vector.tensor_scalar(score[0:n, 0:nk], relu[0:n, q, 0:nk], wi[0:n, j, hd:hd + 1],
                                                            None, ALU.mult))
                            else:
                                own(nc.vector.scalar_tensor_tensor(
                                    out=score[0:n, 0:nk], in0=relu[0:n, q, 0:nk], scalar=wi[0:n, j, hd:hd + 1],
                                    in1=score[0:n, 0:nk], op0=ALU.mult, op1=ALU.add))
                            v.sem_inc(S("scored"), 1)
                        own(nc.vector.memset(score[0:64, nk - 64:nk], FILL))

                    def select(j):
                        n, nk = QT[j][1], sum(QT[j])
                        own(nc.vector.max(best[0:n], score[0:n, 0:nk]))
                        own(nc.vector.match_replace(score[0:n, 0:nk], best[0:n], score[0:n, 0:nk], TAKEN))

                    own(nc.vector.memset(bias[:, 0, 0:N_META], 0.0))
                    for j, (t0, n) in enumerate(QT):
                        nk = t0 + n
                        more = j + 1 < NQ
                        if more:
                            scores(j + 1)

                        def maxima(hd):
                            e, q = j * H + hd, hd % 2
                            v.wait_ge(S("logits"), e + 1)
                            if e >= 2:
                                v.wait_ge(S("probs_turned"), e - 1)
                            own(nc.vector.tensor_tensor_reduce(
                                out=lg[0:n, q, 0:nk], in0=flat(2 * q)[0:n, 0:nk], in1=bias[0:n, j % 2, 0:nk],
                                scale=1.0, scalar=TAKEN, op0=ALU.add, op1=ALU.max, accum_out=stat[0:n, q, 0:1]))
                            v.sem_inc(S("logits_out"), 1)
                            own(nc.vector.tensor_scalar(stat[0:n, q, 1:2], stat[0:n, q, 0:1], -1.0, None, ALU.mult))
                            v.sem_inc(S("max"), 1)

                        maxima(0)
                        for hd in range(H):
                            e, q = j * H + hd, hd % 2
                            if hd + 1 < H:
                                maxima(hd + 1)
                            if more:
                                select(j + 1)
                            v.wait_ge(S("exp"), e + 1)
                            own(nc.vector.reciprocal(stat[0:n, q, 3:4], stat[0:n, q, 2:3]))
                            own(nc.vector.tensor_scalar(lg[0:n, q, 0:nk], lg[0:n, q, 0:nk], stat[0:n, q, 3:4], None,
                                                        ALU.mult))
                            v.sem_inc(S("probs"), 1)
                            if more:
                                select(j + 1)
                        if more:
                            nk1 = sum(QT[j + 1])
                            b1 = bias[:, (j + 1) % 2]
                            own(nc.vector.tensor_scalar(b1[:, 0:nk1], score[:, 0:nk1], TAKEN, NEG,
                                                        ALU.not_equal, ALU.mult))
                            own(nc.vector.memset(b1[0:64, nk1 - 64:nk1], NEG))
                        v.wait_ge(S("y_made"), j + 1)
                        nc.vector.tensor_copy(y_of[2][:, :, t0:t0 + n], PS[:, 7].rearrange(
                            "p (a n) -> p a n", n=P)[:, :, 0:n]).then_inc(S("y"), 1)

        def phase_mlstm(pj, tok, y_of, l, st):
            H = 4
            MQ, MK, MV, MO = 0, 4, 8, 12
            NS = len(ST_)
            cv = sb(st, "cv", [P, 8, T])
            vt = sb(st, "vt", [P, NS, BW])
            gi, gf, bsum, msum, tmp4, one4, zer4 = (sb(st, n, [4, T]) for n in (
                "gi", "gf", "bsum", "msum", "tmp4", "one4", "zer4"))
            ibf = sb(st, "ibf", [4, 2])
            at = sb(st, "at", [P, NS, 4])
            nmb = sb(st, "nmb", [P, H, T])
            dd = sb(st, "dd", [P, 2, T])
            ss = sb(st, "ss", [P, 2, T])
            den, floor = (sb(st, n, [P, 4 * len(ST_)]) for n in ("den", "floor"))
            hq = sb(st, "hq", [P, 4, T])
            rq = sb(st, "ml_rq", [P, 4 * len(ST_)])
            flat = lambda b: PS[:, b:b + 2].rearrange("p a n -> p (a n)")
            hy = y_of[1]

            def spans(j0):
                return ((j0, 512), (512, T)) if j0 < 512 else ((512, T),)

            with nc.Block() as block:
                @block.sync
                def _(sp):
                    for c, src in enumerate((ml_i_bias, ml_f_bias)):
                        sp.dma_start(ibf[:, c:c + 1], src[ds(l, 1)].rearrange("a h -> h a")).then_inc(loaded, 16)

                @block.tensor
                def _(pe):
                    for g in range(2):
                        for j, (t0, n) in enumerate(QT):
                            b, c = (1, 0) if j == 4 else (0, t0)
                            last = nc.tensor.transpose(PS[0:4, 2 * g + b, c:c + n], tok[0:n, j, 8 + 4 * g:12 + 4 * g],
                                                       ident[0:n, 0:n])
                    last.then_inc(S("gates_turned"), 1)
                    for j, (t0, n) in enumerate(ST_):
                        if j >= 2:
                            pe.wait_ge(S("v_out"), j - 1)
                        for m in range(4):
                            last = nc.tensor.transpose(PS[0:n, 4 + j % 2, m * P:(m + 1) * P],
                                                       pj[:, MV + m, t0:t0 + n], ident[:])
                        last.then_inc(S("v_turned"), 1)
                    pe.wait_ge(S("a"), 1)
                    for j, (t0, n) in enumerate(ST_):
                        last = nc.tensor.transpose(PS[0:n, 6, 4 * j:4 * j + 4], tmp4[:, t0:t0 + n], ident[0:4, 0:4])
                    last.then_inc(S("a_turned"), 1)

                @block.vector
                def _(v):
                    own = Chain(v, dve_own)
                    v.wait_ge(loaded, 32)
                    v.wait_ge(S("gates_turned"), 1)
                    for g, dst in ((0, gi), (1, gf)):
                        for c0, c1, b in ((0, 400, 0), (400, T, 1)):
                            last = nc.vector.tensor_scalar(dst[:, c0:c1], PS[0:4, 2 * g + b, 0:c1 - c0],
                                                           ibf[:, g:g + 1], None, ALU.add)
                    own(last)
                    v.sem_inc(S("gates_in"), 1)
                    nc.vector.memset(one4[:], 1.0)
                    nc.vector.memset(zer4[:], 0.0)
                    own(nc.vector.tensor_scalar(cv[:, 0], pj[:, 0], prm[:, G_CONVW + 24:G_CONVW + 25],
                                                prm[:, G_CONVB:G_CONVB + 1], ALU.mult, ALU.add))
                    for m in range(8):
                        if m:
                            own(nc.vector.tensor_scalar(cv[:, m], pj[:, m], prm[:, G_CONVW + 24 + m:G_CONVW + 25 + m],
                                                        prm[:, G_CONVB + m:G_CONVB + m + 1], ALU.mult, ALU.add))
                        for back in (1, 2, 3):
                            c = G_CONVW + 8 * (3 - back) + m
                            own(nc.vector.scalar_tensor_tensor(
                                out=cv[:, m, back:T], in0=pj[:, m, 0:T - back], scalar=prm[:, c:c + 1],
                                in1=cv[:, m, back:T], op0=ALU.mult, op1=ALU.add))
                        v.sem_inc(S("convolved"), 1)
                    v.wait_ge(S("softplus"), 1)
                    own(nc.vector.tensor_scalar(gf[:], gf[:], 0.0, None, ALU.min))
                    own(nc.vector.tensor_tensor(gf[:], gf[:], msum[:], ALU.subtract))
                    own(nc.vector.tensor_tensor_scan(bsum[:], one4[:], gf[:], 0.0, ALU.mult, ALU.add))
                    own(nc.vector.tensor_tensor(tmp4[:], gi[:], bsum[:], ALU.subtract))
                    v.sem_inc(S("a"), 1)
                    own(nc.vector.tensor_tensor_scan(msum[:], tmp4[:], tmp4[:], 0.0, ALU.max, ALU.max))
                    own(nc.vector.tensor_tensor(bsum[:], bsum[:], msum[:], ALU.add))
                    own(nc.vector.tensor_scalar(bsum[:], bsum[:], -1.0, 85.0, ALU.mult, ALU.min))
                    own(nc.vector.tensor_scalar(msum[:], msum[:], -1.0, None, ALU.mult))
                    v.sem_inc(S("m"), 1)
                    v.wait_ge(S("a_turned"), 1)
                    for j, (t0, n) in enumerate(ST_):
                        last = nc.vector.tensor_copy(at[0:n, j], PS[0:n, 6, 4 * j:4 * j + 4])
                    own(last)

                @block.scalar
                def _(act):
                    own = Chain(act, act_own)
                    act.wait_ge(S("gates_in"), 1)
                    own(nc.scalar.activation(msum[:], gf[:], ACT.Abs))
                    own(nc.scalar.activation(msum[:], msum[:], ACT.Exp, scale=-1.0))
                    own(nc.scalar.activation(msum[:], msum[:], ACT.Ln, bias=1.0))
                    act.sem_inc(S("softplus"), 1)
                    for j, (t0, n) in enumerate(ST_):
                        act.wait_ge(S("v_turned"), j + 1)
                        nc.scalar.activation(vt[0:n, j], PS[0:n, 4 + j % 2, :], ACT.Copy).then_inc(S("v_out"), 1)
                    for m in range(8):
                        act.wait_ge(S("convolved"), m + 1)
                        nc.scalar.activation(cv[:, m], cv[:, m], ACT.Silu)
                    nc.scalar.activation(pj[:, MO:MO + 4], pj[:, MO:MO + 4], ACT.Sigmoid)
                    act.wait_ge(S("m"), 1)
                    nc.scalar.activation(bsum[:], bsum[:], ACT.Exp).then_inc(act_own, 1)
            clear()

            with nc.Block() as block:
                steps = [(hd, i) for hd in range(H) for i in range(NS)]

                @block.tensor
                def _(pe):
                    for hd in range(H):
                        for a in range(2):
                            last = nc.tensor.matmul(PS[:, 2 * hd + a, 0:H2], sel[0:4, hd],
                                                    msum[:, a * H2:(a + 1) * H2], start=True, stop=True)
                        last.then_inc(S("spread"), 1)
                    pe.wait_ge(S("spread_out"), H)
                    for j, (t0, n) in enumerate(ST_):
                        last = nc.tensor.transpose(PS[0:n, 7, 4 * j:4 * j + 4], bsum[:, t0:t0 + n], ident[0:4, 0:4])
                    last.then_inc(S("floor"), 1)

                    def scores(e):
                        hd, i = steps[e]
                        s0, n = ST_[i]
                        if e >= 2:
                            pe.wait_ge(S("weighed"), e - 1)
                        for j0, j1 in spans(s0):
                            last = nc.tensor.matmul(flat(2 * (e % 2))[0:n, j0:j1], cv[:, MK + hd, s0:s0 + n],
                                                    cv[:, MQ + hd, j0:j1], start=True, stop=True)
                        last.then_inc(S("scores"), 1)

                    scores(0)
                    for e, (hd, i) in enumerate(steps):
                        if e + 1 < len(steps):
                            scores(e + 1)
                        s0, n = ST_[i]
                        pe.wait_ge(S("weighed"), e + 1)
                        for j in range(i, NS):
                            t0, m = ST_[j]
                            nc.tensor.matmul(PS[0:m, 6, 4 * j + hd:4 * j + hd + 1], ss[0:n, e % 2, t0:t0 + m],
                                             ones[0:n, 0:1], start=i == 0 and j == 0, stop=j == i,
                                             skip_group_check=True)
                        if i == 0 and hd:
                            pe.wait_ge(S("sums_out"), hd)
                        for j0, j1 in spans(s0):
                            last = nc.tensor.matmul(
                                flat(4)[:, j0:j1], vt[0:n, i, hd * P:(hd + 1) * P], ss[0:n, e % 2, j0:j1],
                                start=i == 0, stop=i == (NS - 1 if j0 == 512 else NS - 2), skip_group_check=True)
                        last.then_inc(S("summed"), 1)
                    pe.wait_ge(S("h_squares"), 1)
                    token_sums(lambda m: hq[:, m], ones[:, 0:1], 1).then_inc(S("h_sums"), 1)
                    pe.wait_ge(S("factor"), 1)
                    for m in range(4):
                        token_spread(lambda j: rq[:, 4 * j + m:4 * j + m + 1].broadcast_to([P, P]), m
                                     ).then_inc(S("h_spread"), 1)

                @block.vector
                def _(v):
                    own = Chain(v, dve_own)
                    tt = nc.vector.tensor_tensor
                    for t in (den, floor, rq):
                        own(nc.vector.memset(t[:], 1.0))
                    v.wait_ge(S("spread_out"), H)

                    def decay(e):
                        hd, i = steps[e]
                        s0, n = ST_[i]
                        if e >= 2:
                            v.wait_ge(S("weighed"), e - 1)
                        nc.vector.tensor_scalar(dd[0:n, e % 2, s0:T], nmb[0:n, hd, s0:T], at[0:n, i, hd:hd + 1], 0.0,
                                                ALU.add, ALU.min).then_inc(S("decay_log"), 1)
                    decay(0)
                    for e, (hd, i) in enumerate(steps):
                        if e + 1 < len(steps):
                            decay(e + 1)
                        s0, n = ST_[i]
                        v.wait_ge(S("decay"), e + 1)
                        v.wait_ge(S("scores"), e + 1)
                        if e >= 2:
                            v.wait_ge(S("summed"), e - 1)
                        nc.vector.scalar_tensor_tensor(
                            out=ss[0:n, e % 2, s0:T], in0=flat(2 * (e % 2))[0:n, s0:T], scalar=P ** -0.5,
                            in1=dd[0:n, e % 2, s0:T], op0=ALU.mult, op1=ALU.mult).then_inc(S("weighed"), 1)
                    v.wait_ge(S("floor"), 1)
                    v.wait_ge(S("summed"), len(steps))
                    for dst, bank in ((den, 6), (floor, 7)):
                        nc.vector.tensor_copy(dst[:, 0:16], PS[:, bank, 0:16])
                        own(nc.vector.tensor_copy(dst[0:ST_[-1][1], 16:20], PS[0:ST_[-1][1], bank, 16:20]))
                    own(tt(floor[:], floor[:], den[:], ALU.max))
                    own(nc.vector.tensor_scalar(den[:], den[:], -1.0, None, ALU.mult))
                    own(tt(den[:], floor[:], den[:], ALU.max))
                    own(nc.vector.reciprocal(den[:], den[:]))
                    v.wait_ge(S("h_sums"), 1)
                    own(token_sums_out(rq, 1, 1.0 / P, 0.0, ALU.mult, ALU.add))
                    own(tt(rq[:], rq[:], den[:], ALU.mult))
                    own(tt(rq[:], rq[:], den[:], ALU.mult))
                    own(nc.vector.tensor_scalar(rq[:], rq[:], EPS, None, ALU.add))
                    own(nc.vector.reciprocal(rq[:], rq[:]))
                    v.sem_inc(S("h_recip"), 1)
                    v.wait_ge(S("h_rsqrt"), 1)
                    tt(rq[:], rq[:], den[:], ALU.mult).then_inc(S("factor"), 1)
                    for m in range(4):
                        v.wait_ge(S("h_spread"), m + 1)
                        own(tt(hy[:, m], hy[:, m], spread(m), ALU.mult))
                        nc.vector.scalar_tensor_tensor(
                            out=hy[:, m], in0=hy[:, m], scalar=prm[:, G_MLN + m:G_MLN + m + 1], in1=pj[:, MO + m],
                            op0=ALU.mult, op1=ALU.mult)

                @block.scalar
                def _(act):
                    for hd in range(H):
                        act.wait_ge(S("spread"), hd + 1)
                        nc.scalar.activation(halves(nmb[:, hd]), PS[:, 2 * hd:2 * hd + 2, 0:H2], ACT.Copy
                                             ).then_inc(S("spread_out"), 1)

                    def sums_out(hd):
                        act.wait_ge(S("summed"), NS * (hd + 1))
                        nc.scalar.activation(hy[:, hd], flat(4)[:, 0:T], ACT.Copy).then_inc(S("sums_out"), 1)

                    for e, (hd, i) in enumerate(steps):
                        s0, n = ST_[i]
                        act.wait_ge(S("decay_log"), e + 1)
                        nc.scalar.activation(dd[0:n, e % 2, s0:T], dd[0:n, e % 2, s0:T], ACT.Exp
                                             ).then_inc(S("decay_exp"), 1)
                        if hd and i == 1:
                            sums_out(hd - 1)
                    sums_out(H - 1)
                    act.wait_ge(S("sums_out"), H)
                    nc.scalar.activation(hq[:], hy, ACT.Square).then_inc(S("h_squares"), 1)
                    act.wait_ge(S("h_recip"), 1)
                    nc.scalar.activation(rq[:], rq[:], ACT.Sqrt).then_inc(S("h_rsqrt"), 1)

                @block.gpsimd
                def _(g):
                    for e, (hd, i) in enumerate(steps):
                        s0, n = ST_[i]
                        g.wait_ge(S("decay_exp"), e + 1)
                        d = dd[0:n, e % 2, s0:s0 + n]
                        g.affine_select(out=d, in_=d, compare_op=ALU.is_ge, fill=0.0, base=0, pattern=[[1, n]],
                                        channel_multiplier=-1).then_inc(S("decay"), 1)

        def run(phase, *args):
            with ExitStack() as st:
                phase(st, *args)
            clear()

        run(phase_start)
        with nc.Fori(0, DEPTH) as l:
            run(phase_params, l)

            def ffn(which, post):
                with ExitStack() as st:
                    hh = sb(st, "hidden_high", [P, KF, T], F32R)
                    hl = sb(st, "hidden_low", [P, KF, T], F32R)
                    phase_ffn_in(hh, hl, l, which, post, G_NORM + KD * 4 * which)
                    phase_ffn_out(hh, hl, l, which)

            ffn(0, None)
            with ExitStack() as outer:
                y_dsa = sb(outer, "y_dsa", [P, 4, T])
                y_of = (fo[:, 0:4], fo[:, 4:8], y_dsa[:])
                with ExitStack() as st:
                    pj = sb(st, "pj", [P, 16, T])
                    tok = sb(st, "tok", [P, 5, 16])
                    for name, branch, c0, n, small_too in (
                            ("rw", phase_rwkv, 0, 14, False), ("dsa", phase_dsa, C_DSA, 9, True),
                            ("ml", phase_mlstm, RW_COLS, 16, False)):
                        if name == "rw":
                            phase_proj(pj, tok, w_in, uh, ul, l, c0, n, small_too, (G_NORM + KD, 0.5), G_NORM + 2 * KD)
                        else:
                            phase_proj(pj, tok, w_in, uh, ul, l, c0, n, small_too)
                        with ExitStack() as st2:
                            branch(pj, tok, y_of, l, st2)
                        clear()
                if debug is not None:
                    debug(nc, "fo", fo, l)
                    debug(nc, "y_dsa", y_dsa, l)
                mh = sb(outer, "mixed_high", [P, KD, T], F32R)
                ml = sb(outer, "mixed_low", [P, KD, T], F32R)
                with ExitStack() as st:
                    phase_merge(y_of, mh, ml, l, st)
                clear()
                phase_proj(fo, None, w_out, mh, ml, l, 0, KD, False)
            ffn(1, (G_NORM + 3 * KD, 1.0))
            run(phase_post_norm, (G_NORM + 5 * KD, 0.5))
        run(phase_end)


_INS = ["x", "meta_tokens", "norm_gain", "ffn_w_in", "ffn_w_out", "w_in", "rw_mu", "rw_w0", "rw_w_up", "rw_a0",
        "rw_a_up", "rw_g_up", "rw_k_k", "rw_k_a", "rw_r_k", "rw_gn_gain", "rw_gn_bias", "ml_conv_w", "ml_conv_b",
        "ml_i_bias", "ml_f_bias", "ml_norm_gain", "dsa_kv_norm", "dsa_w_uk", "dsa_w_uv", "w_branch", "w_out"]


def kernel(**inputs):
    import concourse.bacc as bacc
    from concourse.bass_utils import run_bass_kernel_spmd

    nc = bacc.Bacc("TRN2", target_bir_lowering=False, num_devices=1)
    arrays, args = {}, []
    for name in _INS:
        a = np.ascontiguousarray(inputs[name])
        arrays[f"in_{name}"] = a
        args.append(nc.dram_tensor(f"in_{name}", a.shape, mybir.dt.from_np(a.dtype), kind="ExternalInput").ap())
    args.append(nc.dram_tensor("out_0", (1, SEQ, D_MODEL), F32, kind="ExternalOutput").ap())
    build_program(nc, *args)
    r = run_bass_kernel_spmd(nc, [arrays], core_ids=[0])
    return r.results[0]["out_0"]
```
